# Optimizing a Trainium2 kernel written in Bass

```python
import jax, jax.numpy as jnp
from jax import lax
import numpy as np
import math
import jax
import jax.numpy as jnp

D_MODEL = 1024
BATCH = 1
SEQ = 1024
DEPTH = 1

MEM_LEN = 256
EPS = 1e-6
HEAD_DIM = 64
ATTN_WIDTH = D_MODEL // 2
ATTN_Q_HEADS = ATTN_WIDTH // HEAD_DIM
ATTN_KV_HEADS = 2
ATTN_REP = ATTN_Q_HEADS // ATTN_KV_HEADS
KV_WIDTH = ATTN_KV_HEADS * HEAD_DIM
WINDOW = 128
ATTN_BLOCK = 128
SGU_WIDTH = D_MODEL - ATTN_WIDTH
SGU_GROUP_DIM = 64
SGU_GROUPS = SGU_WIDTH // SGU_GROUP_DIM
SGU_CHUNK = 128
IN_WIDTH = ATTN_WIDTH + 2 * KV_WIDTH + 2 * SGU_WIDTH
X_HEADS = 4
X_HEAD_DIM = D_MODEL // X_HEADS
N_GROUPS = 4
EXPERTS_PER_GROUP = 8
N_EXPERTS = N_GROUPS * EXPERTS_PER_GROUP
TOP_K = 2
D_EXPERT = D_MODEL // 2
MOE_BLOCK = 256


def rms_norm(x, gain):
    xf = x.astype(jnp.float32)
    y = xf * lax.rsqrt(jnp.mean(xf * xf, axis=-1, keepdims=True) + EPS)
    return (y * gain.astype(jnp.float32)).astype(x.dtype)

def sliding_window_attention(q, k, v, sinks):
    B, S = q.shape[:2]
    nb = S // ATTN_BLOCK
    qb = q.reshape(B, nb, ATTN_BLOCK, ATTN_KV_HEADS, ATTN_REP, HEAD_DIM).astype(jnp.float32)
    kb = k.reshape(B, nb, ATTN_BLOCK, ATTN_KV_HEADS, HEAD_DIM)
    vb = v.reshape(B, nb, ATTN_BLOCK, ATTN_KV_HEADS, HEAD_DIM)
    pad = ((0, 0), (1, 0), (0, 0), (0, 0), (0, 0))
    kwin = jnp.concatenate([jnp.pad(kb, pad)[:, :-1], kb], axis=2).astype(jnp.float32)
    vwin = jnp.concatenate([jnp.pad(vb, pad)[:, :-1], vb], axis=2).astype(jnp.float32)
    scores = jnp.einsum('bnqhrd,bnkhd->bnhrqk', qb, kwin) * (HEAD_DIM ** -0.5)
    qi = jnp.arange(ATTN_BLOCK)[:, None]
    kj = jnp.arange(2 * ATTN_BLOCK)[None, :]
    dist = qi + ATTN_BLOCK - kj
    band = (dist >= 0) & (dist < WINDOW)
    key_pos = jnp.arange(nb)[:, None, None] * ATTN_BLOCK + kj[None] - ATTN_BLOCK
    mask = band[None] & (key_pos >= 0)
    scores = jnp.where(mask[None, :, None, None], scores, jnp.finfo(jnp.float32).min)
    sink = sinks.astype(jnp.float32).reshape(ATTN_KV_HEADS, ATTN_REP)[None, None, :, :, None, None]
    m = jnp.maximum(jnp.max(scores, axis=-1, keepdims=True), sink)
    p = jnp.exp(scores - m)
    denom = jnp.sum(p, axis=-1, keepdims=True) + jnp.exp(sink - m)
    out = jnp.einsum('bnhrqk,bnkhd->bnqhrd', p / denom, vwin)
    return out.reshape(B, S, ATTN_WIDTH).astype(q.dtype)

def spatial_gating(u, v, sgu_norm, sgu_w, sgu_b):
    B, S = u.shape[:2]
    nc = S // SGU_CHUNK
    vc = rms_norm(v, sgu_norm).reshape(B, nc, SGU_CHUNK, SGU_GROUPS, SGU_GROUP_DIM)
    causal = jnp.tril(jnp.ones((SGU_CHUNK, SGU_CHUNK), dtype=bool))
    w = jnp.where(causal[None], sgu_w, jnp.zeros((), sgu_w.dtype))
    s = jnp.einsum('gij,bcjgd->bcigd', w, vc) + sgu_b.T[None, None, :, :, None]
    return u * s.reshape(B, S, SGU_WIDTH)

def memory_cross_attention(h, mem_n, w_cq, w_ck, w_cv, cq_norm, ck_norm, w_co):
    B, S = h.shape[:2]
    M = mem_n.shape[1]
    q = rms_norm((h @ w_cq).reshape(B, S, X_HEADS, X_HEAD_DIM), cq_norm)
    k = rms_norm((mem_n @ w_ck).reshape(B, M, X_HEADS, X_HEAD_DIM), ck_norm)
    v = (mem_n @ w_cv).reshape(B, M, X_HEADS, X_HEAD_DIM)
    scores = jnp.einsum('bshd,bmhd->bhsm', q.astype(jnp.float32), k.astype(jnp.float32)) * (X_HEAD_DIM ** -0.5)
    p = jax.nn.softmax(scores, axis=-1)
    out = jnp.einsum('bhsm,bmhd->bshd', p, v.astype(jnp.float32)).astype(h.dtype)
    return out.reshape(B, S, D_MODEL) @ w_co

def hierarchical_moe(h, w_router_group, w_router_expert, w1, w3, w2):
    B, S, D = h.shape
    T = B * S
    xt = h.reshape(T, D)
    xf = xt.astype(jnp.float32)
    p_group = jax.nn.softmax(xf @ w_router_group.astype(jnp.float32), axis=-1)
    g_idx = jnp.argmax(p_group, axis=-1)
    g_w = jnp.take_along_axis(p_group, g_idx[:, None], axis=1)[:, 0]
    local = jnp.einsum('td,gde->tge', xf, w_router_expert.astype(jnp.float32))
    local = jnp.take_along_axis(local, g_idx[:, None, None], axis=1)[:, 0]
    top_logit, top_idx = lax.top_k(local, TOP_K)
    gate = jax.nn.softmax(top_logit, axis=-1) * g_w[:, None]
    flat_e = (g_idx[:, None] * EXPERTS_PER_GROUP + top_idx).reshape(-1).astype(jnp.int32)
    flat_w = gate.reshape(-1)
    A = T * TOP_K
    order = jnp.argsort(flat_e)
    sorted_e = flat_e[order]
    counts = jnp.zeros((N_EXPERTS,), jnp.int32).at[flat_e].add(1)
    starts = jnp.cumsum(counts) - counts
    padded = (counts + MOE_BLOCK - 1) // MOE_BLOCK * MOE_BLOCK
    pad_end = jnp.cumsum(padded)
    pad_start = pad_end - padded
    dest = pad_start[sorted_e] + jnp.arange(A, dtype=jnp.int32) - starts[sorted_e]
    nb = -(-A // MOE_BLOCK) + N_EXPERTS
    P = nb * MOE_BLOCK
    slot_tok = jnp.full((P,), T, jnp.int32).at[dest].set((order // TOP_K).astype(jnp.int32))
    slot_w = jnp.zeros((P,), jnp.float32).at[dest].set(flat_w[order])
    block_e = jnp.minimum(jnp.searchsorted(pad_end, jnp.arange(nb, dtype=jnp.int32) * MOE_BLOCK, side='right'), N_EXPERTS - 1)
    x_pad = jnp.concatenate([xt, jnp.zeros((1, D), xt.dtype)], axis=0)
    xb = x_pad[slot_tok].reshape(nb, MOE_BLOCK, D)

    def run_block(args):
        xblk, e = args
        hid = jax.nn.silu(xblk @ w1[e]) * (xblk @ w3[e])
        return hid @ w2[e]

    yb = lax.map(run_block, (xb, block_e)).reshape(P, D)
    y = jnp.zeros((T + 1, D), jnp.float32).at[slot_tok].add(yb.astype(jnp.float32) * slot_w[:, None])[:T]
    return y.astype(h.dtype).reshape(B, S, D)

def first_inputs(seed: int = 0) -> dict:
    key = jax.random.key(seed)
    ks = jax.random.split(key, 32)
    f32 = jnp.float32
    nrm = lambda k, shape, s: jax.random.normal(k, shape, f32) * s
    gain = lambda k, n: 1.0 + 0.02 * jax.random.normal(k, (n,), f32)
    return {
        "x": nrm(ks[0], (BATCH, SEQ, D_MODEL), 1.0),
        "mem": nrm(ks[1], (BATCH, MEM_LEN, D_MODEL), 1.0),
        "norm_mix": gain(ks[2], D_MODEL),
        "w_in": nrm(ks[3], (D_MODEL, IN_WIDTH), D_MODEL ** -0.5),
        "q_norm": gain(ks[4], HEAD_DIM),
        "k_norm": gain(ks[5], HEAD_DIM),
        "attn_sinks": nrm(ks[6], (ATTN_Q_HEADS,), 0.5),
        "sgu_norm": gain(ks[7], SGU_WIDTH),
        "sgu_w": nrm(ks[8], (SGU_GROUPS, SGU_CHUNK, SGU_CHUNK), SGU_CHUNK ** -0.5),
        "sgu_b": 1.0 + nrm(ks[9], (SGU_GROUPS, SGU_CHUNK), 0.1),
        "out_norm_attn": gain(ks[10], ATTN_WIDTH),
        "out_norm_sgu": gain(ks[11], SGU_WIDTH),
        "w_out": nrm(ks[12], (D_MODEL, D_MODEL), D_MODEL ** -0.5),
        "norm_cross": gain(ks[13], D_MODEL),
        "norm_mem": gain(ks[14], D_MODEL),
        "w_cq": nrm(ks[15], (D_MODEL, D_MODEL), D_MODEL ** -0.5),
        "w_ck": nrm(ks[16], (D_MODEL, D_MODEL), D_MODEL ** -0.5),
        "w_cv": nrm(ks[17], (D_MODEL, D_MODEL), D_MODEL ** -0.5),
        "cq_norm": gain(ks[18], X_HEAD_DIM),
        "ck_norm": gain(ks[19], X_HEAD_DIM),
        "w_co": nrm(ks[20], (D_MODEL, D_MODEL), D_MODEL ** -0.5),
        "norm_ffn": gain(ks[21], D_MODEL),
        "w_router_group": nrm(ks[22], (D_MODEL, N_GROUPS), D_MODEL ** -0.5),
        "w_router_expert": nrm(ks[23], (N_GROUPS, D_MODEL, EXPERTS_PER_GROUP), D_MODEL ** -0.5),
        "w1": nrm(ks[24], (N_EXPERTS, D_MODEL, D_EXPERT), D_MODEL ** -0.5),
        "w3": nrm(ks[25], (N_EXPERTS, D_MODEL, D_EXPERT), D_MODEL ** -0.5),
        "w2": nrm(ks[26], (N_EXPERTS, D_EXPERT, D_MODEL), D_EXPERT ** -0.5),
    }

def first_block(x, mem, norm_mix, w_in, q_norm, k_norm, attn_sinks, sgu_norm, sgu_w, sgu_b,
              out_norm_attn, out_norm_sgu, w_out, norm_cross, norm_mem, w_cq, w_ck, w_cv,
              cq_norm, ck_norm, w_co, norm_ffn, w_router_group, w_router_expert, w1, w3, w2):
    B, S = x.shape[:2]
    mem_n = rms_norm(mem, norm_mem)
    for _ in range(DEPTH):
        h = rms_norm(x, norm_mix)
        proj = h @ w_in
        c0 = ATTN_WIDTH
        c1 = c0 + KV_WIDTH
        c2 = c1 + KV_WIDTH
        c3 = c2 + SGU_WIDTH
        q = rms_norm(proj[..., :c0].reshape(B, S, ATTN_Q_HEADS, HEAD_DIM), q_norm)
        k = rms_norm(proj[..., c0:c1].reshape(B, S, ATTN_KV_HEADS, HEAD_DIM), k_norm)
        v = proj[..., c1:c2].reshape(B, S, ATTN_KV_HEADS, HEAD_DIM)
        u = jax.nn.gelu(proj[..., c2:c3])
        g = jax.nn.gelu(proj[..., c3:])
        attn = sliding_window_attention(q, k, v, attn_sinks)
        sg = spatial_gating(u, g, sgu_norm, sgu_w, sgu_b)
        mixed = jnp.concatenate([rms_norm(attn, out_norm_attn), rms_norm(sg, out_norm_sgu)], axis=-1)
        x = x + mixed @ w_out
        x = x + memory_cross_attention(rms_norm(x, norm_cross), mem_n, w_cq, w_ck, w_cv, cq_norm, ck_norm, w_co)
        x = x + hierarchical_moe(rms_norm(x, norm_ffn), w_router_group, w_router_expert, w1, w3, w2)
    return x


D_MIX = D_MODEL
D_LRU = D_MIX // 2
LRU_BLOCKS = 8
LRU_BLOCK = D_LRU // LRU_BLOCKS
LRU_C = 8.0
CONV_W = 4
CONV_LEFT = 2
N_ATT_HEADS = 4
D_ATT = D_MIX - D_LRU
HEAD_DV = D_ATT // N_ATT_HEADS
HEAD_DK = HEAD_DV // 2
QK_W = N_ATT_HEADS * 2 * HEAD_DK
D_IN_PROJ = 2 * D_LRU + 2 * QK_W + D_ATT
SPLITS = [D_LRU, 2 * D_LRU, 2 * D_LRU + QK_W, 2 * D_LRU + 2 * QK_W]
N_BUCKETS = 32
MAX_DISTANCE = 128
Q_BLOCK = 128
N_EXPERTS_2 = 16
EC_FACTOR = 2
D_FF_EXPERT = D_MODEL


def rms_norm_2(x, g):
    xf = x.astype(jnp.float32)
    y = xf * lax.rsqrt(jnp.mean(xf * xf, axis=-1, keepdims=True) + EPS)
    return (y * g.astype(jnp.float32)).astype(x.dtype)

def t5_buckets(rel):
    half = N_BUCKETS // 2
    max_exact = half // 2
    ret = jnp.where(rel > 0, half, 0)
    n = jnp.abs(rel)
    nf = jnp.maximum(n, 1).astype(jnp.float32)
    large = max_exact + (jnp.log(nf / max_exact) / math.log(MAX_DISTANCE / max_exact)
                         * (half - max_exact)).astype(jnp.int32)
    large = jnp.minimum(large, half - 1)
    return ret + jnp.where(n < max_exact, n, large)

def rg_lru(xc, w_a, b_a, w_x, b_x, lam, reverse):
    B, S, _ = xc.shape
    xb = xc.reshape(B, S, LRU_BLOCKS, LRU_BLOCK)
    r = jax.nn.sigmoid((jnp.einsum('bsnc,ncd->bsnd', xb, w_a).reshape(B, S, D_LRU) + b_a).astype(jnp.float32))
    i = jax.nn.sigmoid((jnp.einsum('bsnc,ncd->bsnd', xb, w_x).reshape(B, S, D_LRU) + b_x).astype(jnp.float32))
    log_a = LRU_C * r * jax.nn.log_sigmoid(lam.astype(jnp.float32))
    a = jnp.exp(log_a)
    u = jnp.sqrt(-jnp.expm1(2.0 * log_a)) * (i * xc.astype(jnp.float32))

    def combine(left, right):
        a1, b1 = left
        a2, b2 = right
        return a1 * a2, a2 * b1 + b2

    _, h = lax.associative_scan(combine, (a, u), axis=1, reverse=reverse)
    return h.astype(xc.dtype)

def diff_attention(q, k, v, g_q, g_k, lam, g_o, bias_table, lam_init):
    B, S = q.shape[0], q.shape[1]
    q = rms_norm_2(q, g_q) * (HEAD_DK ** -0.5)
    k = rms_norm_2(k, g_k)
    nb = S // Q_BLOCK
    qb = q.reshape(B, nb, Q_BLOCK, N_ATT_HEADS, 2, HEAD_DK).transpose(1, 0, 2, 3, 4, 5)
    kpos = jnp.arange(S, dtype=jnp.int32)

    def block(args):
        qi, start = args
        qpos = start + jnp.arange(Q_BLOCK, dtype=jnp.int32)
        bias = bias_table[t5_buckets(kpos[None, :] - qpos[:, None])].astype(jnp.float32)
        bias = bias.transpose(2, 0, 1)
        s = jnp.einsum('bqhjd,bkhjd->bhjqk', qi, k).astype(jnp.float32) + bias[None, :, None]
        p = jax.nn.softmax(s, axis=-1)
        w = (p[:, :, 0] - lam * p[:, :, 1]).astype(v.dtype)
        return jnp.einsum('bhqk,bkhd->bqhd', w, v)

    o = lax.map(block, (qb, jnp.arange(nb, dtype=jnp.int32) * Q_BLOCK))
    o = o.transpose(1, 0, 2, 3, 4).reshape(B, S, N_ATT_HEADS, HEAD_DV)
    o = rms_norm_2(o, g_o) * (1.0 - lam_init)
    return o.reshape(B, S, D_ATT)

def expert_choice_ffn(h, w_router, w1, w3, w2):
    B, S, D = h.shape
    cap = max(1, EC_FACTOR * S // N_EXPERTS_2)
    aff = jax.nn.softmax(jnp.dot(h, w_router).astype(jnp.float32), axis=-1)
    g, idx = lax.top_k(aff.transpose(0, 2, 1), cap)
    xe = jax.vmap(lambda hb, ib: hb[ib])(h, idx)
    a = jnp.einsum('becd,edf->becf', xe, w1)
    b = jnp.einsum('becd,edf->becf', xe, w3)
    y = jnp.einsum('becf,efd->becd', jax.nn.silu(a) * b, w2)
    y = y * g[..., None].astype(y.dtype)
    return jax.vmap(lambda ib, yb: jnp.zeros((S, D), yb.dtype).at[ib.reshape(-1)].add(yb.reshape(-1, D)))(idx, y)

def second_inputs(seed: int = 0) -> dict:
    key = jax.random.key(seed)
    ks = jax.random.split(key, 26)
    f32 = jnp.float32

    def nrm(k, shape, fan_in):
        return jax.random.normal(k, shape, f32) * (fan_in ** -0.5)

    def gain(k, shape):
        return 1.0 + 0.02 * jax.random.normal(k, shape, f32)

    a0 = jax.random.uniform(ks[12], (DEPTH, 2, D_LRU), f32, minval=0.9, maxval=0.999)
    return {
        'x': jax.random.normal(ks[0], (BATCH, SEQ, D_MODEL), f32),
        'c': jax.random.normal(ks[1], (BATCH, D_MODEL), f32),
        'w_mod': nrm(ks[2], (DEPTH, D_MODEL, 6 * D_MODEL), D_MODEL),
        'b_mod': 0.02 * jax.random.normal(ks[3], (DEPTH, 6 * D_MODEL), f32),
        'g_norm1': gain(ks[4], (DEPTH, D_MODEL)),
        'w_in': nrm(ks[5], (DEPTH, D_MODEL, D_IN_PROJ), D_MODEL),
        'conv_w': nrm(ks[6], (DEPTH, CONV_W, 1, D_LRU), CONV_W),
        'conv_b': 0.02 * jax.random.normal(ks[7], (DEPTH, D_LRU), f32),
        'lru_w_a': nrm(ks[8], (DEPTH, 2, LRU_BLOCKS, LRU_BLOCK, LRU_BLOCK), LRU_BLOCK),
        'lru_b_a': 0.1 * jax.random.normal(ks[9], (DEPTH, 2, D_LRU), f32),
        'lru_w_x': nrm(ks[10], (DEPTH, 2, LRU_BLOCKS, LRU_BLOCK, LRU_BLOCK), LRU_BLOCK),
        'lru_b_x': 0.1 * jax.random.normal(ks[11], (DEPTH, 2, D_LRU), f32),
        'lru_lambda': jnp.log(a0) - jnp.log1p(-a0),
        'g_q': gain(ks[13], (DEPTH, HEAD_DK)),
        'g_k': gain(ks[14], (DEPTH, HEAD_DK)),
        'lambda_qk': 0.1 * jax.random.normal(ks[15], (DEPTH, 4, HEAD_DK), f32),
        'g_attn_out': gain(ks[16], (DEPTH, HEAD_DV)),
        'rel_bias': 0.5 * jax.random.normal(ks[17], (N_BUCKETS, N_ATT_HEADS), f32),
        'w_out': nrm(ks[18], (DEPTH, D_MIX, D_MODEL), D_MIX),
        'g_norm2': gain(ks[19], (DEPTH, D_MODEL)),
        'w_router': nrm(ks[20], (DEPTH, D_MODEL, N_EXPERTS_2), D_MODEL),
        'w1': nrm(ks[21], (DEPTH, N_EXPERTS_2, D_MODEL, D_FF_EXPERT), D_MODEL),
        'w3': nrm(ks[22], (DEPTH, N_EXPERTS_2, D_MODEL, D_FF_EXPERT), D_MODEL),
        'w2': nrm(ks[23], (DEPTH, N_EXPERTS_2, D_FF_EXPERT, D_MODEL), D_FF_EXPERT),
    }

def second_block(x, c, w_mod, b_mod, g_norm1, w_in, conv_w, conv_b, lru_w_a, lru_b_a, lru_w_x, lru_b_x,
              lru_lambda, g_q, g_k, lambda_qk, g_attn_out, rel_bias, w_out, g_norm2, w_router, w1, w3, w2):
    B, S, _ = x.shape
    for l in range(DEPTH):
        mod = jnp.dot(jax.nn.silu(c), w_mod[l]) + b_mod[l]
        shift1, scale1, gate1, shift2, scale2, gate2 = jnp.split(mod[:, None, :], 6, axis=-1)

        h = rms_norm_2(x, g_norm1[l]) * (1.0 + scale1) + shift1
        proj = jnp.dot(h, w_in[l])
        x_lru, z_lru, q, k, v = jnp.split(proj, SPLITS, axis=-1)

        xc = lax.conv_general_dilated(x_lru, conv_w[l], (1,), [(CONV_LEFT, CONV_W - 1 - CONV_LEFT)],
                                      dimension_numbers=('NWC', 'WIO', 'NWC'),
                                      feature_group_count=D_LRU) + conv_b[l]
        h_fwd = rg_lru(xc, lru_w_a[l, 0], lru_b_a[l, 0], lru_w_x[l, 0], lru_b_x[l, 0], lru_lambda[l, 0], False)
        h_bwd = rg_lru(xc, lru_w_a[l, 1], lru_b_a[l, 1], lru_w_x[l, 1], lru_b_x[l, 1], lru_lambda[l, 1], True)
        y_lru = (h_fwd + h_bwd) * jax.nn.gelu(z_lru)

        lam_init = 0.8 - 0.6 * math.exp(-0.3 * l)
        lq = lambda_qk[l].astype(jnp.float32)
        lam = jnp.exp(jnp.sum(lq[0] * lq[1])) - jnp.exp(jnp.sum(lq[2] * lq[3])) + lam_init
        y_att = diff_attention(q.reshape(B, S, N_ATT_HEADS, 2, HEAD_DK),
                               k.reshape(B, S, N_ATT_HEADS, 2, HEAD_DK),
                               v.reshape(B, S, N_ATT_HEADS, HEAD_DV),
                               g_q[l], g_k[l], lam, g_attn_out[l], rel_bias, lam_init)

        mix = jnp.dot(jnp.concatenate([y_lru, y_att], axis=-1), w_out[l])
        x = x + gate1 * mix

        h2 = rms_norm_2(x, g_norm2[l]) * (1.0 + scale2) + shift2
        x = x + gate2 * expert_choice_ffn(h2, w_router[l], w1[l], w3[l], w2[l])
    return x


def setup_inputs(seed=0):
    out = dict(first_inputs(seed))
    for name, value in second_inputs(seed + 1).items():
        if name != "x":
            out[name + "_2"] = value
    return out


def reference(
    x, mem, norm_mix, w_in, q_norm, k_norm, attn_sinks, sgu_norm, sgu_w, sgu_b, out_norm_attn,
    out_norm_sgu, w_out, norm_cross, norm_mem, w_cq, w_ck, w_cv, cq_norm, ck_norm, w_co,
    norm_ffn, w_router_group, w_router_expert, w1, w3, w2, c_2, w_mod_2, b_mod_2, g_norm1_2,
    w_in_2, conv_w_2, conv_b_2, lru_w_a_2, lru_b_a_2, lru_w_x_2, lru_b_x_2, lru_lambda_2, g_q_2,
    g_k_2, lambda_qk_2, g_attn_out_2, rel_bias_2, w_out_2, g_norm2_2, w_router_2, w1_2, w3_2,
    w2_2,
):
    x = first_block(
        x, mem, norm_mix, w_in, q_norm, k_norm, attn_sinks, sgu_norm, sgu_w, sgu_b,
        out_norm_attn, out_norm_sgu, w_out, norm_cross, norm_mem, w_cq, w_ck, w_cv, cq_norm,
        ck_norm, w_co, norm_ffn, w_router_group, w_router_expert, w1, w3, w2,
    )
    return second_block(
        x, c_2, w_mod_2, b_mod_2, g_norm1_2, w_in_2, conv_w_2, conv_b_2, lru_w_a_2, lru_b_a_2,
        lru_w_x_2, lru_b_x_2, lru_lambda_2, g_q_2, g_k_2, lambda_qk_2, g_attn_out_2, rel_bias_2,
        w_out_2, g_norm2_2, w_router_2, w1_2, w3_2, w2_2,
    )


_drawn_inputs = setup_inputs


def setup_inputs(seed=0):
    import zlib

    import numpy as np

    out = dict(_drawn_inputs(seed))
    spreads = {}
    factors = {'q_norm': 2.886,
     'attn_sinks': 5.517,
     'sgu_norm': 4.266,
     'out_norm_sgu': 2.729,
     'norm_cross': 6.698,
     'norm_mem': 5.568,
     'cq_norm': 8.0,
     'ck_norm': 8.0,
     'g_norm1_2': 3.28,
     'lru_b_a_2': 4.283,
     'g_q_2': 8.0,
     'g_k_2': 8.0,
     'lambda_qk_2': 7.009,
     'g_attn_out_2': 8.0,
     'rel_bias_2': 4.664,
     'g_norm2_2': 4.517}
    for name, (base, spread) in spreads.items():
        noise = np.random.default_rng([zlib.crc32(name.encode()), seed]).standard_normal(out[name].shape)
        drawn = base * np.exp(spread * noise) if base else spread * noise
        out[name] = jnp.asarray(drawn.astype(out[name].dtype))
    for name, factor in factors.items():
        out[name] = (out[name] * factor).astype(out[name].dtype)
    return out
```

```python
from collections import namedtuple
from contextlib import ExitStack

import numpy as np

import concourse.bass as bass
from concourse import mybir

F32 = mybir.dt.float32
I32 = mybir.dt.int32
ALU = mybir.AluOpType
ACT = mybir.ActivationFunctionType
AX = mybir.AxisListType.X

P = 128
T = 1024
NT = T // P
D = 1024
NC = D // P
EPS = 1e-6
MASKED = -1e30

HD = 64
QH = 8
KVH = 2
REP = QH // KVH
ATT = QH * HD
SG = 512
GRP = 8
MEM = 256
XH = 4
XD = D // XH
G1 = 4
E1 = 32
PER_G = E1 // G1
F1 = 512
MAX_OVER = 2 * T // P - 1

LRU = 512
LC = LRU // P
AH = 4
DK = 64
DV = 128
E2 = 16
F2 = 1024
CAP = 2 * T // E2
LAM_INIT = 0.8 - 0.6
BUCKETS = 32
BUCKET_FROM = [0, 1, 2, 3, 4, 5, 6, 7, 8, 12, 16, 23, 32, 46, 64, 91]

K_IDENT = 0
K_BEFORE = 128
K_IOTA = 256
K_UPTO = 384
K_ODD = 512
K_EVEN = 768
K_TOKEN = K_EVEN + 4 * 256
K_SPARE = K_TOKEN + 8
K_REV32 = K_SPARE + 2
K_BUCKET = K_REV32 + 32
K_ALL = K_BUCKET + 512


def constants():
    k = np.zeros((P, K_ALL), np.float32)
    p = np.arange(P)[:, None]
    c = np.arange(P)[None, :]
    k[:, K_IDENT:K_IDENT + P] = p == c
    k[:, K_BEFORE:K_BEFORE + P] = p < c
    k[:, K_IOTA:K_IOTA + P] = c
    k[:, K_UPTO:K_UPTO + P] = p <= c
    own = np.where(c <= p, 0.0, MASKED)
    previous = np.where(c > p, 0.0, MASKED)
    k[:, K_ODD:K_ODD + 256] = np.concatenate([previous, own], 1)
    for n in range(4):
        k[:, K_EVEN + 256 * n:K_EVEN + 256 * n + 256] = np.concatenate(
            [own, previous if n else np.full((P, P), MASKED)], 1)
    k[:, K_TOKEN:K_TOKEN + NT] = p + P * np.arange(NT)[None, :]
    k[:, K_SPARE] = T + np.arange(P)
    k[:, K_SPARE + 1] = -(T + np.arange(P))
    k[:, K_REV32:K_REV32 + 32] = 32 - np.arange(32)[None, :]
    for m in range(511):
        away = m - 255
        n = max(b for b in range(16) if BUCKET_FROM[b] <= abs(away))
        k[n + (16 if away > 0 else 0), K_BUCKET + m] = 1.0
    return k


class Steps:

    def __init__(self, eng, sem):
        self.eng, self.sem, self.base, self.n, self.round = eng, sem, 0, 0, None

    def did(self, instruction):
        instruction.then_inc(self.sem, 1)
        self.n += 1

    def wait(self, n=None):
        n = self.n if n is None else n
        value = self.base + n if self.round is None else self.round + (self.base + n)
        self.eng.wait_ge(self.sem, value)

    def enter(self, i, per):
        self.base, self.n, self.per, self.round = self.base + self.n, 0, per, i * per

    def leave(self, rounds):
        assert self.n == self.per, ("steps in a round", self.n)
        self.base, self.n, self.round = self.base + self.per * rounds, 0, None


class Phase:

    def __init__(self, nc, name):
        self.nc, self.name, self.ctx, self.used = nc, name, ExitStack(), []

    def __enter__(self):
        self.ctx.__enter__()
        return self

    def __exit__(self, *failed):
        self.ctx.__exit__(*failed)
        if failed[0] is None:
            self.nc.clear_and_free_semaphores(self.used)
            self.nc.all_engine_barrier()

    def sb(self, name, shape, dt=F32):
        return self.ctx.enter_context(self.nc.sbuf_tensor(f"{self.name}_{name}", shape, dt))

    def ps(self, name, shape):
        return self.ctx.enter_context(self.nc.psum_tensor(f"{self.name}_{name}", shape, F32))

    def sems(self, names, ns=False, prefix=""):
        names = names.split()
        found = [self.nc.alloc_semaphore(f"{self.name}_{prefix}{n}") for n in names]
        self.used += found
        return namedtuple("Semaphores", names)(*found) if ns else found

    def block(self):
        return self.ctx.enter_context(self.nc.Block())


def rows_by_partition(w, rows_each=NC):
    return w.rearrange("(p c) n -> p c n", c=rows_each)


def spread(ap, n):
    return ap.unsqueeze(2).broadcast_to([ap.shape[0], ap.shape[1], n])


def tiled(ap, n):
    return ap.unsqueeze(1).broadcast_to([ap.shape[0], n, ap.shape[1]])


def tile_of(x, t):
    return x[:, bass.ds(t, 1), :].rearrange("p a d -> p (a d)")


def strided(x):
    return x.rearrange("p (d c) -> p c d", c=NC)


def transpose_tile(pe, out, src, ident):
    for c in range(NC):
        last = pe.transpose(out[:, c, :], strided(src)[:, c, :], ident)
    return last


def product(pe, out, left, right, chunks=NC):
    for c in range(chunks):
        last = pe.matmul(out, left[:, c, :], right[:, c, :], start=(c == 0), stop=(c == chunks - 1))
    return last


def hold(eng, sem, value, passed):
    eng.wait_ge(sem, value)
    eng.sem_inc(passed, 1)


def inverse_root(pool, step, out, mean, minus_half):
    step.did(pool.tensor_scalar(mean, mean, EPS, None, ALU.add))
    step.wait()
    return pool.tensor_tensor(out, mean, minus_half.broadcast_to([P, mean.shape[1]]), ALU.pow)


def phase_memory(nc, io, keep):
    kmT, vm, ks = keep["kmT"], keep["vm"], keep["consts"]
    ident = ks[:, K_IDENT:K_IDENT + P]
    MT = MEM // P
    with Phase(nc, "mem") as ph:
        mem = ph.sb("mem", [P, MT, D])
        gain = ph.sb("gain", [P, D])
        xgain = ph.sb("xgain", [P, 2, XD])
        gg = ph.sb("gg", [P, XD])
        wk = ph.sb("wk", [P, NC, D])
        wv = ph.sb("wv", [P, NC, D])
        junk = ph.sb("junk", [P, D])
        normed = ph.sb("normed", [P, MT, D])
        mT = ph.sb("mT", [P, NC, MEM])
        kn = ph.sb("kn", [P, MT, D])
        stat = ph.sb("stat", [P, 4 * MT + 2 * XH * MT])
        tp = ph.ps("tp", [P, NC, P])
        kv = ph.ps("kv", [P, 2, 2, 512])
        (loaded, wk_loaded, wv_loaded, squared, rms, mem_normed, turned, mT_ready, k_done, v_done,
         k_squared, k_rms, k_normed, k_turned, vec, kept, pool_steps, x_loaded) = ph.sems(
            "loaded wk_loaded wv_loaded squared rms mem_normed turned mT_ready k_done v_done "
            "k_squared k_rms k_normed k_turned vec kept pool_steps x_loaded")
        ms = stat[:, 0:MT]
        rstd = stat[:, MT:2 * MT]
        kms = stat[:, 8:8 + XH * MT]
        krstd = stat[:, 8 + XH * MT:8 + 2 * XH * MT]
        block = ph.block()

        @block.sync
        def _(sp):
            sp.dma_start(mem[:], io["mem"].rearrange("a (t p) d -> p (a t) d", p=P)).then_inc(loaded, 16)
            sp.dma_start(ks[:], io["consts"]).then_inc(loaded, 16)
            sp.dma_start(gain[:], io["norm_mem"].partition_broadcast(P)).then_inc(loaded, 16)
            sp.dma_start(xgain[:, 0, :], io["cq_norm"].partition_broadcast(P)).then_inc(loaded, 16)
            sp.dma_start(xgain[:, 1, :], io["ck_norm"].partition_broadcast(P)).then_inc(loaded, 16)
            sp.dma_start(wk[:], rows_by_partition(io["w_ck"])).then_inc(wk_loaded, 16)
            sp.dma_start(wv[:], rows_by_partition(io["w_cv"])).then_inc(wv_loaded, 16)
            sp.dma_start(keep["x"][:], io["x"].rearrange("a (t p) d -> p (a t) d", p=P)).then_inc(x_loaded, 16)
            sp.wait_ge(x_loaded, 16)

        @block.scalar
        def _(act):
            act.wait_ge(loaded, 16 * 5)
            for t in range(MT):
                act.activation(junk[:], mem[:, t, :], ACT.Square, scale=D ** -0.5,
                               accum_out=ms[:, t:t + 1]).then_inc(squared, 1)
                act.wait_ge(squared, t + 1)
            for t in range(MT):
                act.wait_ge(turned, t + 1)
                act.copy(mT[:, :, t * P:(t + 1) * P], tp[:]).then_inc(mT_ready, 1)
            for t in range(MT):
                act.wait_ge(k_done, t + 1)
                for h in range(XH):
                    act.activation(junk[:, h * XD:(h + 1) * XD], kv[:, t, h // 2, (h % 2) * XD:(h % 2 + 1) * XD],
                                   ACT.Square, scale=XD ** -0.5,
                                   accum_out=kms[:, t * XH + h:t * XH + h + 1]).then_inc(k_squared, 1)
                    act.wait_ge(k_squared, XH * t + h + 1)
            for t in range(MT):
                act.wait_ge(k_turned, t + 1)
                act.copy(kmT[:, :, t * P:(t + 1) * P], tp[:]).then_inc(kept, 1)
            for t in range(MT):
                act.wait_ge(v_done, t + 1)
                act.copy(vm[:, t, :], kv[:, t, :, :].rearrange("p a n -> p (a n)")).then_inc(kept, 1)
            act.wait_ge(kept, 2 * MT)

        @block.gpsimd
        def _(pool):
            step = Steps(pool, pool_steps)
            half = keep["minus_half"]
            step.did(pool.memset(half, -0.5))
            step.did(pool.memset(keep["zero"], 0.0))
            for t in range(MT):
                pool.wait_ge(squared, t + 1)
                inverse_root(pool, step, rstd[:, t:t + 1], ms[:, t:t + 1], half).then_inc(rms, 1)
            for t in range(MT):
                pool.wait_ge(k_squared, XH * (t + 1))
                inverse_root(pool, step, krstd[:, XH * t:XH * t + XH],
                             kms[:, XH * t:XH * t + XH], half).then_inc(k_rms, 1)

        @block.vector
        def _(dve):
            step = Steps(dve, vec)
            dve.wait_ge(loaded, 16 * 5)
            dve.scalar_tensor_tensor(gg[:], xgain[:, 0, :], XD ** -0.5, xgain[:, 1, :], ALU.mult, ALU.mult) \
                .then_inc(vec, 1)
            step.n = 1
            for t in range(MT):
                dve.wait_ge(rms, t + 1)
                dve.scalar_tensor_tensor(normed[:, t, :], mem[:, t, :], rstd[:, t:t + 1], gain[:], ALU.mult,
                                         ALU.mult).then_inc(mem_normed, 1)
            for t in range(MT):
                dve.wait_ge(k_rms, t + 1)
                step.did(dve.tensor_tensor(kn[:, t, :].rearrange("p (h d) -> p h d", h=XH),
                                           kv[:, t, :, :].rearrange("p a (h d) -> p (a h) d", d=XD),
                                           spread(krstd[:, XH * t:XH * t + XH], XD), ALU.mult))
                step.wait()
                dve.tensor_tensor(kn[:, t, :].rearrange("p (h d) -> p h d", h=XH),
                                  kn[:, t, :].rearrange("p (h d) -> p h d", h=XH), tiled(gg[:], XH),
                                  ALU.mult).then_inc(k_normed, 1)

        @block.tensor
        def _(pe):
            pe.wait_ge(loaded, 16 * 5)
            for t in range(MT):
                pe.wait_ge(mem_normed, t + 1)
                if t:
                    pe.wait_ge(mT_ready, t)
                transpose_tile(pe, tp, normed[:, t, :], ident).then_inc(turned, 1)
            pe.wait_ge(mT_ready, MT)
            pe.wait_ge(wk_loaded, 16)
            for t in range(MT):
                for n in range(2):
                    last = product(pe, kv[:, t, n, :], mT[:, :, t * P:(t + 1) * P], wk[:, :, n * 512:(n + 1) * 512])
                last.then_inc(k_done, 1)
            for t in range(MT):
                pe.wait_ge(k_normed, t + 1)
                if t:
                    pe.wait_ge(kept, t)
                for c in range(NC):
                    last = pe.transpose(tp[:, c, :], kn[:, t, c * P:(c + 1) * P], ident)
                last.then_inc(k_turned, 1)
            pe.wait_ge(wv_loaded, 16)
            for t in range(MT):
                for n in range(2):
                    last = product(pe, kv[:, t, n, :], mT[:, :, t * P:(t + 1) * P], wv[:, :, n * 512:(n + 1) * 512])
                last.then_inc(v_done, 1)


IN_W = ATT + 2 * KVH * HD + 2 * SG


def phase_mix(nc, io, keep):
    x, ks = keep["x"], keep["consts"]
    ident = ks[:, K_IDENT:K_IDENT + P]
    NQK = QH + KVH
    KV = KVH * HD
    with Phase(nc, "mix") as ph:
        w_in = ph.sb("w_in", [P, NC, IN_W])
        w_out = ph.sb("w_out", [P, NC, D])
        gain = ph.sb("gain", [P, D])
        out_gain = ph.sb("out_gain", [P, D])
        sgu_gain = ph.sb("sgu_gain", [P, SG])
        qk_gain = ph.sb("qk_gain", [P, 2])
        qk = ph.sb("qk", [P, 1])
        sinks = ph.sb("sinks", [P, QH])
        brow = ph.sb("brow", [GRP, P])
        bcol = ph.sb("bcol", [P, GRP])
        wT = ph.sb("wT", [P, GRP, P])
        junk = ph.sb("junk", [P, D])
        hn = ph.sb("hn", [P, D])
        hT = ph.sb("hT", [P, NC, P])
        qn = ph.sb("qn", [P, ATT])
        kn = ph.sb("kn", [P, KV])
        v = ph.sb("v", [P, 2, KV])
        u = ph.sb("u", [P, SG])
        g = ph.sb("g", [P, SG])
        qT = ph.sb("qT", [P, REP, P])
        kT = ph.sb("kT", [P, 2, P])
        pr = ph.sb("pr", [P, QH, 2 * P])
        pT = ph.sb("pT", [P, QH * 2, P])
        wraw = pT[:, 0:GRP, :]
        ss = ph.sb("ss", [P, NQK])
        rqk = ph.sb("rqk", [P, NQK])
        st = ph.sb("st", [P, 64])
        ms, rstd, gms, grstd, ams, arstd, sms, srstd = (st[:, n:n + 1] for n in range(8))
        top, ntop, total, esink, den, rden = (st[:, 8 + 8 * n:16 + 8 * n] for n in range(6))
        big = ph.ps("big", [P, 4, 512])
        two = ph.ps("two", [P, 2, 512])
        low = ph.ps("low", [P, 2, 512])
        tp = two[:].rearrange("p a (c n) -> p (a c) n", n=P)
        PQ, PKV, PU, PG = big[:, 0, :], big[:, 1, 0:2 * KV], big[:, 2, :], big[:, 3, :]
        scores = big[:].rearrange("p a (h k) -> p (a h) k", k=2 * P)
        pTp = big[:].rearrange("p a (h k) -> p (a h) k", k=P)
        (loaded, w_in_loaded, w_out_loaded, spatial_turned, spatial_ready, squared, normed, turned,
         hT_ready, projected, qk_squared, gelus, g_squared, qk_normed, v_ready, qk_turned, q_ready, k_ready,
         scored, top_ready, exps, p_turned, p_ready, attended, att_ready, att_squared, gated, gated_ready,
         sg_squared, mixed, mix_turned, mT_ready, out_done, x_done, vec, gate_in, rms, qk_summed, qk_rms,
         g_rms, mix_rms, pool_steps, passed) = ph.sems(
            "loaded w_in_loaded w_out_loaded spatial_turned spatial_ready squared normed turned "
            "hT_ready projected qk_squared gelus g_squared qk_normed v_ready qk_turned q_ready k_ready "
            "scored top_ready exps p_turned p_ready attended att_ready att_squared gated gated_ready "
            "sg_squared mixed mix_turned mT_ready out_done x_done vec gate_in rms qk_summed qk_rms g_rms mix_rms pool_steps passed")
        block = ph.block()

        @block.sync
        def _(sp):
            def one(dst, src):
                sp.dma_start(dst, src).then_inc(loaded, 16)
            one(gain[:], io["norm_mix"].partition_broadcast(P))
            one(out_gain[:, 0:ATT], io["out_norm_attn"].partition_broadcast(P))
            one(out_gain[:, ATT:D], io["out_norm_sgu"].partition_broadcast(P))
            one(sgu_gain[:], io["sgu_norm"].partition_broadcast(P))
            one(sinks[:], io["attn_sinks"].partition_broadcast(P))
            for r in range(2):
                one(qk_gain[r * HD:(r + 1) * HD, 0:1], io["q_norm"].rearrange("(p o) -> p o", o=1))
                one(qk_gain[r * HD:(r + 1) * HD, 1:2], io["k_norm"].rearrange("(p o) -> p o", o=1))
            one(brow[:], io["sgu_b"])
            one(wraw, io["sgu_w"].rearrange("g i j -> i g j"))
            sp.dma_start(w_in[:], rows_by_partition(io["w_in"])).then_inc(w_in_loaded, 16)
            sp.dma_start(w_out[:], rows_by_partition(io["w_out"])).then_inc(w_out_loaded, 16)

        @block.scalar
        def _(act):
            act.wait_ge(loaded, 16 * 11)
            with act.Fori(0, NT // 2) as r:
                for half in range(2):
                    t = r * 2 + half
                    hold(act, x_done, t + 1, passed)
                    act.activation(junk[:], tile_of(x, t), ACT.Square, scale=D ** -0.5,
                                   accum_out=ms).then_inc(squared, 1)
                    act.wait_ge(turned, t + 1)
                    act.copy(hT[:], tp).then_inc(hT_ready, 1)
                    act.wait_ge(projected, t + 1)
                    act.activation(junk[:, 0:ATT], PQ, ACT.Square, scale=HD ** -0.5)
                    act.activation(junk[:, ATT:ATT + KV], PKV[:, 0:KV], ACT.Square,
                                   scale=HD ** -0.5).then_inc(qk_squared, 1)
                    act.activation(g[:], PG, ACT.Gelu_apprx_tanh).then_inc(gelus, 1)
                    act.activation(u[:], PU, ACT.Gelu_apprx_tanh).then_inc(gelus, 1)
                    act.wait_ge(gelus, 2 * t + 1)
                    act.wait_ge(qk_normed, t + 1)
                    act.activation(junk[:, 0:SG], g[:], ACT.Square, scale=SG ** -0.5,
                                   accum_out=gms).then_inc(g_squared, 1)
                    act.wait_ge(qk_turned, t + 1)
                    act.copy(qT[:], low[:, 0, :].rearrange("p (a n) -> p a n", n=P)).then_inc(q_ready, 1)
                    act.wait_ge(top_ready, t + 1)
                    for h in range(QH):
                        ex = act.activation(pr[:, h, :], pr[:, h, :], ACT.Exp, bias=ntop[:, h:h + 1],
                                            accum_out=total[:, h:h + 1])
                    ex = act.activation(esink, esink, ACT.Exp)
                    ex.then_inc(exps, 1)
                    act.wait_ge(p_turned, t + 1)
                    act.copy(pT[:, 0:QH, :], pTp[:, 0:QH, :]).then_inc(p_ready, 1)
                    act.wait_ge(att_ready, t + 1)
                    act.activation(junk[:, 0:ATT], hn[:, 0:ATT], ACT.Square, scale=ATT ** -0.5,
                                   accum_out=ams).then_inc(att_squared, 1)
                    act.wait_ge(gated_ready, t + 1)
                    act.activation(junk[:, ATT:D], hn[:, ATT:D], ACT.Square, scale=SG ** -0.5,
                                   accum_out=sms).then_inc(sg_squared, 1)
                    act.wait_ge(mix_turned, t + 1)
                    act.copy(hT[:], tp).then_inc(mT_ready, 1)

        @block.gpsimd
        def _(pool):
            step = Steps(pool, pool_steps)
            mh = keep["minus_half"]
            with pool.Fori(0, NT // 2) as r:
                step.enter(r, 2 * 5)
                for half in range(2):
                    t = r * 2 + half
                    hold(pool, squared, t + 1, passed)
                    inverse_root(pool, step, rstd, ms, mh).then_inc(rms, 1)
                    hold(pool, qk_summed, t + 1, passed)
                    inverse_root(pool, step, rqk[:], ss[:], mh).then_inc(qk_rms, 1)
                    hold(pool, g_squared, t + 1, passed)
                    inverse_root(pool, step, grstd, gms, mh).then_inc(g_rms, 1)
                    hold(pool, att_squared, t + 1, passed)
                    inverse_root(pool, step, arstd, ams, mh).then_inc(mix_rms, 1)
                    hold(pool, sg_squared, t + 1, passed)
                    inverse_root(pool, step, srstd, sms, mh).then_inc(mix_rms, 1)
                step.leave(NT // 2)

        @block.vector
        def _(dve):
            step = Steps(dve, vec)
            dve.sem_inc(x_done, 1)
            dve.wait_ge(loaded, 16 * 11)
            step.did(dve.memset(kT[:], 0.0))
            step.did(dve.memset(v[:], 0.0))
            step.did(dve.scalar_tensor_tensor(qk[:], qk_gain[:, 0:1], HD ** -0.5, qk_gain[:, 1:2], ALU.mult,
                                              ALU.mult))
            dve.wait_ge(spatial_turned, 1)
            step.did(dve.tensor_tensor(wT[:], tp, tiled(ks[:, K_UPTO:K_UPTO + P], GRP), ALU.mult))
            step.did(dve.tensor_copy(bcol[:], low[:, 0, 0:GRP]))
            step.wait()
            dve.sem_inc(spatial_ready, 1)
            with dve.Fori(0, NT // 2) as r:
                step.enter(r, 2 * 7)
                for half in range(2):
                    t = r * 2 + half
                    dve.wait_ge(rms, t + 1)
                    dve.scalar_tensor_tensor(hn[:], tile_of(x, t), rstd, gain[:], ALU.mult,
                                             ALU.mult).then_inc(normed, 1)
                    dve.wait_ge(qk_squared, t + 1)
                    dve.tensor_reduce(ss[:], junk[:, 0:ATT + KV].rearrange("p (h d) -> p h d", d=HD), AX,
                                      ALU.add).then_inc(qk_summed, 1)
                    dve.wait_ge(qk_rms, t + 1)
                    dve.tensor_tensor(qn[:].rearrange("p (a k d) -> p k a d", k=KVH, d=HD),
                                      PQ.rearrange("p (k a d) -> p k a d", k=KVH, d=HD),
                                      rqk[:, 0:QH].rearrange("p (k a) -> p k a", k=KVH).unsqueeze(3)
                                      .broadcast_to([P, KVH, REP, HD]), ALU.mult)
                    dve.tensor_tensor(kn[:].rearrange("p (h d) -> p h d", d=HD),
                                      PKV[:, 0:KV].rearrange("p (h d) -> p h d", d=HD),
                                      spread(rqk[:, QH:NQK], HD), ALU.mult).then_inc(qk_normed, 1)
                    dve.tensor_copy(v[:, half, :], PKV[:, KV:2 * KV]).then_inc(v_ready, 1)
                    dve.wait_ge(g_rms, t + 1)
                    dve.scalar_tensor_tensor(g[:], g[:], grstd, sgu_gain[:], ALU.mult, ALU.mult) \
                        .then_inc(gate_in, 1)
                    dve.wait_ge(qk_turned, t + 1)
                    dve.tensor_scalar(kT[:, half, :], low[:, 1, 0:P], qk[:], None, ALU.mult).then_inc(k_ready, 1)
                    dve.wait_ge(scored, t + 1)
                    mask = (ks[:, K_ODD:K_ODD + 2 * P] if half else
                            ks[:, K_EVEN:K_EVEN + 1024].rearrange("p (a n) -> p a n", n=2 * P)[:, bass.ds(r, 1), :]
                            .rearrange("p a n -> p (a n)"))
                    step.did(dve.tensor_tensor(pr[:], scores, tiled(mask, QH), ALU.add))
                    step.wait()
                    step.did(dve.tensor_reduce(top, pr[:], AX, ALU.max))
                    step.wait()
                    step.did(dve.tensor_tensor(top, top, sinks[:], ALU.max))
                    step.wait()
                    step.did(dve.tensor_tensor(esink, sinks[:], top, ALU.subtract))
                    dve.tensor_scalar(ntop, top, -1.0, None, ALU.mult).then_inc(top_ready, 1)
                    dve.wait_ge(exps, t + 1)
                    step.did(dve.tensor_tensor(den, total, esink, ALU.add))
                    step.wait()
                    step.did(dve.reciprocal(rden, den))
                    dve.wait_ge(p_turned, t + 1)
                    dve.tensor_copy(pT[:, QH:2 * QH, :], pTp[:, QH:2 * QH, :]).then_inc(p_ready, 1)
                    step.wait()
                    dve.wait_ge(attended, t + 1)
                    dve.tensor_tensor(hn[:, 0:ATT].rearrange("p (h d) -> p h d", d=HD),
                                      low[:, 0, :].rearrange("p (h d) -> p h d", d=HD), spread(rden, HD),
                                      ALU.mult).then_inc(att_ready, 1)
                    dve.wait_ge(gated, t + 1)
                    step.did(dve.tensor_tensor(hn[:, ATT:D].rearrange("p (h d) -> p h d", h=GRP),
                                               low[:, 1, :].rearrange("p (h d) -> p h d", h=GRP),
                                               spread(bcol[:], SG // GRP), ALU.add))
                    step.wait()
                    dve.tensor_tensor(hn[:, ATT:D], hn[:, ATT:D], u[:], ALU.mult).then_inc(gated_ready, 1)
                    dve.wait_ge(mix_rms, 2 * t + 2)
                    dve.scalar_tensor_tensor(hn[:, 0:ATT], hn[:, 0:ATT], arstd, out_gain[:, 0:ATT], ALU.mult,
                                             ALU.mult)
                    dve.scalar_tensor_tensor(hn[:, ATT:D], hn[:, ATT:D], srstd, out_gain[:, ATT:D], ALU.mult,
                                             ALU.mult).then_inc(mixed, 1)
                    dve.wait_ge(out_done, t + 1)
                    dve.tensor_tensor(tile_of(x, t), low[:].rearrange("p a n -> p (a n)"), tile_of(x, t),
                                      ALU.add).then_inc(x_done, 1)
                step.leave(NT // 2)

        @block.tensor
        def _(pe):
            pe.wait_ge(loaded, 16 * 11)
            for n in range(GRP):
                pe.transpose(tp[:, n, :], wraw[:, n, :], ident)
            pe.transpose(low[:, 0, 0:GRP], brow[:], ident[0:GRP, 0:GRP]).then_inc(spatial_turned, 1)
            pe.wait_ge(spatial_ready, 1)
            pe.wait_ge(w_in_loaded, 16)
            pe.wait_ge(w_out_loaded, 16)
            with pe.Fori(0, NT // 2) as r:
                for half in range(2):
                    t = r * 2 + half
                    pe.wait_ge(normed, t + 1)
                    transpose_tile(pe, tp, hn[:], ident).then_inc(turned, 1)
                    pe.wait_ge(hT_ready, t + 1)
                    for out, col, n in ((PQ, 0, ATT), (PKV, ATT, 2 * KV), (PG, ATT + 2 * KV + SG, SG),
                                        (PU, ATT + 2 * KV, SG)):
                        last = product(pe, out, hT, w_in[:, :, col:col + n])
                    last.then_inc(projected, 1)
                    pe.wait_ge(qk_normed, t + 1)
                    for a in range(REP):
                        pe.transpose(low[:, 0, a * P:(a + 1) * P], qn[:, a * P:(a + 1) * P], ident)
                    pe.transpose(low[:, 1, 0:P], kn[:], ident).then_inc(qk_turned, 1)
                    pe.wait_ge(q_ready, t + 1)
                    pe.wait_ge(k_ready, t + 1)
                    pe.wait_ge(gelus, 2 * t + 2)
                    pe.wait_ge(v_ready, t + 1)
                    for h in range(QH):
                        a = h // REP * HD
                        last = pe.matmul(scores[:, h, :], qT[a:a + HD, h % REP, :],
                                         kT[a:a + HD, :, :].rearrange("p a n -> p (a n)"), start=True, stop=True)
                    last.then_inc(scored, 1)
                    pe.wait_ge(gate_in, t + 1)
                    for n in range(GRP):
                        w = SG // GRP
                        last = pe.matmul(low[:, 1, n * w:(n + 1) * w], wT[:, n, :], g[:, n * w:(n + 1) * w],
                                         start=True, stop=True)
                    last.then_inc(gated, 1)
                    pe.wait_ge(exps, t + 1)
                    for h in range(QH):
                        for b in range(2):
                            last = pe.transpose(pTp[:, 2 * h + b, :], pr[:, h, b * P:(b + 1) * P], ident)
                    last.then_inc(p_turned, 1)
                    pe.wait_ge(p_ready, 2 * t + 2)
                    for h in range(QH):
                        for b in range(2):
                            last = pe.matmul(low[:, 0, h * HD:(h + 1) * HD], pT[:, 2 * h + b, :],
                                             v[:, b, h // REP * HD:(h // REP + 1) * HD], start=(b == 0),
                                             stop=(b == 1))
                    last.then_inc(attended, 1)
                    pe.wait_ge(mixed, t + 1)
                    transpose_tile(pe, tp, hn[:], ident).then_inc(mix_turned, 1)
                    pe.wait_ge(mT_ready, t + 1)
                    for n in range(2):
                        last = product(pe, low[:, n, :], hT, w_out[:, :, n * 512:(n + 1) * 512])
                    last.then_inc(out_done, 1)


MOD = 6 * D
PIECE = 768
LOGITS = G1 + E1


def phase_cross(nc, io, keep):
    x, ks, kmT, vm, logits = keep["x"], keep["consts"], keep["kmT"], keep["vm"], keep["logits"]
    ident = ks[:, K_IDENT:K_IDENT + P]
    with Phase(nc, "cross") as ph:
        wq = ph.sb("wq", [P, NC, D])
        wo = ph.sb("wo", [P, NC, D])
        wr = ph.sb("wr", [P, NC, LOGITS])
        gain = ph.sb("gain", [P, D])
        ffn_gain = ph.sb("ffn_gain", [P, D])
        junk2 = ph.sb("junk", [P, 2, D])
        hn2 = ph.sb("hn", [P, 2, D])
        hT2 = ph.sb("hT", [P, 2, NC, P])
        pr2 = ph.sb("pr", [P, 2, D])
        st = ph.sb("st", [P, 2, 32])
        csilu = ph.sb("csilu", [P, NC])
        pieces = ph.sb("pieces", [P, 4, PIECE])
        sums = ph.sb("sums", [P, 2, PIECE])
        tp2 = [ph.ps(f"tp{n}", [P, NC, P]) for n in range(2)]
        acc2 = [ph.ps(f"acc{n}", [P, 2, 512]) for n in range(2)]
        s = ph.sems("loaded wq_loaded wo_loaded wr_loaded x_free hn_free squared rms normed turned hT_ready q_done "
                    "q_squared q_rms q_normed q_turned qT_ready scored top_ready exps p_turned pT_ready attended "
                    "o_read o_ready o_turned oT_ready out_done x_done squared_b rms_b routed_rows b_turned bT_ready "
                    "logits_done logits_ready stored vec pool_steps passed piece_loaded0 piece_loaded1 "
                    "piece_loaded2 piece_loaded3 piece_free sums_ready sums_stored0 sums_stored1 silu_ready", ns=True)
        piece_loaded = [s.piece_loaded0, s.piece_loaded1, s.piece_loaded2, s.piece_loaded3]
        sums_stored = [s.sums_stored0, s.sums_stored1]

        def stat(half, at, n=1):
            return st[:, half, at:at + n]

        block = ph.block()

        @block.sync
        def _(sp):
            def one(dst, src):
                sp.dma_start(dst, src).then_inc(s.loaded, 16)
            one(gain[:], io["norm_cross"].partition_broadcast(P))
            one(ffn_gain[:], io["norm_ffn"].partition_broadcast(P))
            one(csilu[:], io["c_2"].rearrange("a (p c) -> p (a c)", c=NC))
            sp.dma_start(wq[:], rows_by_partition(io["w_cq"])).then_inc(s.wq_loaded, 16)
            sp.dma_start(wo[:], rows_by_partition(io["w_co"])).then_inc(s.wo_loaded, 16)
            sp.dma_start(wr[:, :, 0:G1], rows_by_partition(io["w_router_group"])).then_inc(s.wr_loaded, 16)
            for g in range(G1):
                sp.dma_start(wr[:, :, G1 + g * PER_G:G1 + (g + 1) * PER_G],
                             rows_by_partition(io["w_router_expert"][g])).then_inc(s.wr_loaded, 16)
            w_mod = io["w_mod_2"][0].rearrange("(p c) n -> p c n", c=NC)
            with sp.Fori(0, NT // 2) as r:
                for n in range(2 * NC):
                    b, c = n // NC, n % NC
                    sp.wait_ge(s.piece_free, 2 * NC * r + n + 1)
                    sp.dma_start(pieces[:, n % 4, :], w_mod[:, c, bass.ds(r * (2 * PIECE) + b * PIECE, PIECE)]) \
                        .then_inc(piece_loaded[n % 4], 16)
                    if c == NC - 1:
                        sp.wait_ge(s.sums_ready, 2 * r + b + 1)
                        sp.dma_start(keep["mod_part"][:, bass.ds(r * (2 * PIECE) + b * PIECE, PIECE)],
                                     sums[:, b, :]).then_inc(sums_stored[b], 16)
                for half in range(2):
                    t = 2 * r + half
                    sp.wait_ge(s.routed_rows, t + 1)
                    sp.dma_start(keep["rows"][bass.ts(t, P), :], hn2[:, half, :]).then_inc(s.stored, 16)
                    sp.dma_start(keep["acc"][bass.ts(t, P), :], tile_of(x, t)).then_inc(s.stored, 16)
            sp.dma_start(keep["acc"][T:T + P, :], tile_of(x, 0)).then_inc(s.stored, 16)
            sp.wait_ge(s.stored, 64 + 16 * (2 * NT + 1))
            for b in range(2):
                sp.wait_ge(sums_stored[b], 16 * (NT // 2) + 16)

        @block.gpsimd
        def _(pool):
            step = Steps(pool, s.pool_steps)
            mh = keep["minus_half"]

            def add(r, n):
                c, b = n % NC, n // NC
                hold(pool, piece_loaded[n % 4], 64 * r + 16 * (n // 4 + 1), s.passed)
                if c == 0:
                    hold(pool, sums_stored[b], 16 * r + 16, s.passed)
                    step.did(pool.tensor_scalar(sums[:, b, :], pieces[:, n % 4, :], csilu[:, c:c + 1], None,
                                                ALU.mult))
                else:
                    step.did(pool.tensor_scalar(pieces[:, n % 4, :], pieces[:, n % 4, :], csilu[:, c:c + 1], None,
                                                ALU.mult))
                    step.wait()
                    step.did(pool.tensor_tensor(sums[:, b, :], sums[:, b, :], pieces[:, n % 4, :], ALU.add))
                step.wait()
                pool.sem_inc(s.piece_free, 1)
                if c == NC - 1:
                    pool.sem_inc(s.sums_ready, 1)

            pool.sem_inc(s.piece_free, 4)
            pool.sem_inc(sums_stored[0], 16)
            pool.sem_inc(sums_stored[1], 16)
            pool.wait_ge(s.silu_ready, 1)
            with pool.Fori(0, NT // 2) as r:
                step.enter(r, 6 + 2 * (2 * NC - 1))
                roots = [(s.squared, s.rms, 0, 1), (s.q_squared, s.q_rms, 2, XH), (s.squared_b, s.rms_b, 0, 1)]
                n = 0
                for squared, rms, at, width in roots:
                    for half in range(2):
                        hold(pool, squared, (2 * r + half) * (XH if at else 1) + (XH if at else 1), s.passed)
                        inverse_root(pool, step, stat(half, at + 8, width), stat(half, at, width), mh) \
                            .then_inc(rms, 1)
                        for _ in range(3 if n < 12 else 2):
                            if n < 2 * NC:
                                add(r, n)
                                n += 1
                assert n == 2 * NC
                step.leave(NT // 2)

        @block.scalar
        def _(act):
            act.wait_ge(s.loaded, 48)
            act.activation(csilu[:], csilu[:], ACT.Silu).then_inc(s.silu_ready, 1)
            with act.Fori(0, NT // 2) as r:
                ts = [(h, 2 * r + h) for h in range(2)]
                for h, t in ts:
                    hold(act, s.x_free, t + 1, s.passed)
                    act.activation(junk2[:, h, :], tile_of(x, t), ACT.Square, scale=D ** -0.5,
                                   accum_out=stat(h, 0)).then_inc(s.squared, 1)
                for h, t in ts:
                    act.wait_ge(s.turned, t + 1)
                    act.copy(hT2[:, h, :, :], tp2[h][:]).then_inc(s.hT_ready, 1)
                for h, t in ts:
                    act.wait_ge(s.q_done, t + 1)
                    for n in range(XH):
                        act.activation(junk2[:, h, n * XD:(n + 1) * XD], acc2[h][:, n // 2, n % 2 * XD:(n % 2 + 1) * XD],
                                       ACT.Square, scale=XD ** -0.5,
                                       accum_out=stat(h, 2 + n)).then_inc(s.q_squared, 1)
                for h, t in ts:
                    act.wait_ge(s.q_turned, t + 1)
                    act.copy(hT2[:, h, :, :], tp2[h][:]).then_inc(s.qT_ready, 1)
                for h, t in ts:
                    act.wait_ge(s.top_ready, t + 1)
                    for n in range(XH):
                        last = act.activation(pr2[:, h, n * MEM:(n + 1) * MEM],
                                              acc2[h][:, n // 2, n % 2 * MEM:(n % 2 + 1) * MEM], ACT.Exp,
                                              bias=stat(h, 20 + n), accum_out=stat(h, 24 + n))
                    last.then_inc(s.exps, 1)
                for h, t in ts:
                    act.wait_ge(s.p_turned, t + 1)
                    act.copy(hT2[:, h, :, :], tp2[h][:]).then_inc(s.pT_ready, 1)
                for h, t in ts:
                    act.wait_ge(s.o_turned, t + 1)
                    act.copy(hT2[:, h, :, :], tp2[h][:]).then_inc(s.oT_ready, 1)
                for h, t in ts:
                    hold(act, s.x_done, t + 1, s.passed)
                    act.activation(junk2[:, h, :], tile_of(x, t), ACT.Square, scale=D ** -0.5,
                                   accum_out=stat(h, 0)).then_inc(s.squared_b, 1)
                for h, t in ts:
                    act.wait_ge(s.b_turned, t + 1)
                    act.copy(hT2[:, h, :, :], tp2[h][:]).then_inc(s.bT_ready, 1)

        @block.vector
        def _(dve):
            step = Steps(dve, s.vec)
            dve.sem_inc(s.x_free, NT)
            dve.sem_inc(s.stored, 64)
            dve.wait_ge(s.loaded, 48)
            with dve.Fori(0, NT // 2) as r:
                step.enter(r, 2 * 2)
                ts = [(h, 2 * r + h) for h in range(2)]
                for h, t in ts:
                    dve.wait_ge(s.stored, 64 * r + 64)
                    dve.wait_ge(s.rms, t + 1)
                    dve.scalar_tensor_tensor(hn2[:, h, :], tile_of(x, t), stat(h, 8), gain[:], ALU.mult,
                                             ALU.mult).then_inc(s.normed, 1)
                for h, t in ts:
                    dve.wait_ge(s.q_rms, t + 1)
                    dve.tensor_tensor(hn2[:, h, :].rearrange("p (h d) -> p h d", h=XH),
                                      acc2[h][:].rearrange("p a (h d) -> p (a h) d", d=XD),
                                      spread(stat(h, 10, XH), XD), ALU.mult).then_inc(s.q_normed, 1)
                for h, t in ts:
                    dve.wait_ge(s.scored, t + 1)
                    step.did(dve.tensor_reduce(stat(h, 16, XH), acc2[h][:].rearrange("p a (h m) -> p (a h) m", m=MEM),
                                               AX, ALU.max))
                    step.wait()
                    dve.tensor_scalar(stat(h, 20, XH), stat(h, 16, XH), -1.0, None, ALU.mult).then_inc(s.top_ready, 1)
                for h, t in ts:
                    dve.wait_ge(s.exps, t + 1)
                    step.did(dve.reciprocal(stat(h, 28, XH), stat(h, 24, XH)))
                    step.wait()
                    dve.wait_ge(s.attended, t + 1)
                    dve.tensor_tensor(hn2[:, h, :].rearrange("p (h d) -> p h d", h=XH),
                                      acc2[h][:].rearrange("p a (h d) -> p (a h) d", d=XD),
                                      spread(stat(h, 28, XH), XD), ALU.mult).then_inc(s.o_ready, 1)
                for h, t in ts:
                    dve.wait_ge(s.out_done, t + 1)
                    dve.tensor_tensor(tile_of(x, t), acc2[h][:].rearrange("p a n -> p (a n)"), tile_of(x, t),
                                      ALU.add).then_inc(s.x_done, 1)
                for h, t in ts:
                    dve.wait_ge(s.rms_b, t + 1)
                    dve.scalar_tensor_tensor(hn2[:, h, :], tile_of(x, t), stat(h, 8), ffn_gain[:], ALU.mult,
                                             ALU.mult).then_inc(s.routed_rows, 1)
                for h, t in ts:
                    dve.wait_ge(s.logits_done, t + 1)
                    dve.tensor_tensor(tile_of(logits, t), acc2[h][:, 0, 0:LOGITS], keep["zero"].broadcast_to([P, LOGITS]),
                                      ALU.add).then_inc(s.logits_ready, 1)
                step.leave(NT // 2)

        @block.tensor
        def _(pe):
            pe.wait_ge(s.wq_loaded, 16)
            pe.wait_ge(s.wo_loaded, 16)
            pe.wait_ge(s.wr_loaded, 16 * (1 + G1))
            with pe.Fori(0, NT // 2) as r:
                ts = [(h, 2 * r + h) for h in range(2)]
                for h, t in ts:
                    pe.wait_ge(s.normed, t + 1)
                    transpose_tile(pe, tp2[h], hn2[:, h, :], ident).then_inc(s.turned, 1)
                pe.sem_inc(s.passed, 1)
                for h, t in ts:
                    pe.wait_ge(s.hT_ready, t + 1)
                    for n in range(2):
                        last = product(pe, acc2[h][:, n, :], hT2[:, h, :, :], wq[:, :, n * 512:(n + 1) * 512])
                    last.then_inc(s.q_done, 1)

                def turn(h, src):
                    for c in range(NC):
                        last = pe.transpose(tp2[h][:, c, :], src[:, c * P:(c + 1) * P], ident)
                    return last

                for h, t in ts:
                    pe.wait_ge(s.q_normed, t + 1)
                    turn(h, hn2[:, h, :]).then_inc(s.q_turned, 1)
                for h, t in ts:
                    pe.wait_ge(s.qT_ready, t + 1)
                    for n in range(XH):
                        for c in range(2):
                            last = pe.matmul(acc2[h][:, n // 2, n % 2 * MEM:(n % 2 + 1) * MEM],
                                             hT2[:, h, 2 * n + c, :], kmT[:, 2 * n + c, :], start=(c == 0),
                                             stop=(c == 1))
                    last.then_inc(s.scored, 1)
                for h, t in ts:
                    pe.wait_ge(s.exps, t + 1)
                    turn(h, pr2[:, h, :]).then_inc(s.p_turned, 1)
                for h, t in ts:
                    pe.wait_ge(s.pT_ready, t + 1)
                    for n in range(XH):
                        for c in range(2):
                            last = pe.matmul(acc2[h][:, n // 2, n % 2 * XD:(n % 2 + 1) * XD],
                                             hT2[:, h, 2 * n + c, :], vm[:, c, n * XD:(n + 1) * XD],
                                             start=(c == 0), stop=(c == 1))
                    last.then_inc(s.attended, 1)
                for h, t in ts:
                    pe.wait_ge(s.o_ready, t + 1)
                    transpose_tile(pe, tp2[h], hn2[:, h, :], ident).then_inc(s.o_turned, 1)
                for h, t in ts:
                    pe.wait_ge(s.oT_ready, t + 1)
                    for n in range(2):
                        last = product(pe, acc2[h][:, n, :], hT2[:, h, :, :], wo[:, :, n * 512:(n + 1) * 512])
                    last.then_inc(s.out_done, 1)
                for h, t in ts:
                    pe.wait_ge(s.routed_rows, t + 1)
                    transpose_tile(pe, tp2[h], hn2[:, h, :], ident).then_inc(s.b_turned, 1)
                for h, t in ts:
                    pe.wait_ge(s.bT_ready, t + 1)
                    product(pe, acc2[h][:, 0, 0:LOGITS], hT2[:, h, :, :], wr).then_inc(s.logits_done, 1)
                pe.wait_ge(s.logits_ready, 2 * r + 2)


UNIT = 4096
RING = 6
FAR = 1e6
Shared = namedtuple("Shared", "slot_of gate over over_from pa pb")


def phase_experts(nc, io, keep, cfg, route):
    NE, F = cfg["experts"], cfg["width"]
    FC = F // P
    HALVES = F // 512
    PER_UNIT = UNIT // F
    U1 = NC // PER_UNIT
    U2 = FC * D // UNIT
    UNITS = 2 * U1 + U2
    TOGETHER = RING // UNITS
    ks = keep["consts"]
    ident = ks[:, K_IDENT:K_IDENT + P]
    rows, sums = cfg["rows"], cfg["sums"]
    with Phase(nc, cfg["name"]) as ph:
        ring = ph.sb("ring", [P, RING, UNIT])
        xg = ph.sb("xg", [P, 2, D])
        xT = ph.sb("xT", [P, NC, P])
        hit = ph.sb("hit", [P, NT, P])
        act_out = ph.sb("act_out", [P, F])
        hid = ph.sb("hid", [P, F])
        hidT = ph.sb("hidT", [P, FC, P])
        y = ph.sb("y", [P, D])
        what = ph.sb("what", [P, NT, 4])
        slots = ph.sb("slots", [P, 2, 4])
        gidx = ph.sb("gidx", [P, 2], I32)
        sidx = ph.sb("sidx", [P, 2], I32)
        local = ph.sb("local", [P, NT])
        over = ph.sb("over", [P, 16], I32)
        over_from = ph.sb("over_from", [P, 16])
        slot_of = ph.sb("slot_of", [P, NT, NE + 1])
        gate = ph.sb("gate", [P, NT, NE + 1])
        tp = ph.ps("tp", [P, NC, P])
        pa = ph.ps("pa", [P, 2, 512])
        pb = ph.ps("pb", [P, 2, 512])
        py = ph.ps("py", [P, 2, 512])
        names = ("hits_ready ids_done ids_ready gathered0 gathered1 x_turned xT_ready ab_done silu_done hid_ready "
                 "hid_turned hidT_ready y_done y_ready y_free added vec passed units_used")
        main = ph.sems(names, ns=True)
        more = ph.sems(names, ns=True, prefix="o_")
        more_loaded, = ph.sems("o_loaded")
        unit_loaded = ph.sems(" ".join(f"unit{n}_loaded" for n in range(RING)))
        routed, = ph.sems("routed")
        route.buffers(ph, Shared(slot_of=slot_of, gate=gate, over=over, over_from=over_from, pa=pa, pb=pb))
        block = ph.block()


        def hits(dve, S, step, e, start, k):
            slot = slot_of[:, :, bass.ds(e, 1)].rearrange("p t a -> p (t a)")
            if start is not None:
                step.did(dve.tensor_scalar(local[:], slot, start, None, ALU.subtract))
                step.wait()
                slot = local[:]
            dve.tensor_tensor(hit[:], tiled(ks[:, K_IOTA:K_IOTA + P], NT), spread(slot, P), ALU.is_equal)
            dve.tensor_scalar(what[:, :, 1:2], gate[:, :, bass.ds(e, 1)], 1.0, None, ALU.mult) \
                .then_inc(S.hits_ready, 1)

        def indices(dve, S, step, par, k, added):
            dve.wait_ge(S.ids_done, k + 1)
            dve.wait_ge(S.y_free, added)
            step.did(dve.tensor_copy(slots[:, par, 0:3], tp[:, 0, 0:3]))
            step.wait()
            step.did(dve.tensor_copy(gidx[:, par:par + 1], slots[:, par, 0:1]))
            step.did(dve.scalar_tensor_tensor(slots[:, par, 3:4], slots[:, par, 2:3],
                                              ks[:, K_SPARE + 1:K_SPARE + 2], slots[:, par, 0:1], ALU.mult,
                                              ALU.add))
            step.wait()
            dve.tensor_tensor(sidx[:, par:par + 1], slots[:, par, 3:4], ks[:, K_SPARE:K_SPARE + 1], ALU.add) \
                .then_inc(S.ids_ready, 1)

        def hidden(dve, S, k):
            dve.wait_ge(S.silu_done, k + 1)
            dve.tensor_tensor(hid[:].rearrange("p (a n) -> p a n", n=512), pb[:, 0:HALVES, :],
                              act_out[:].rearrange("p (a n) -> p a n", n=512), ALU.mult).then_inc(S.hid_ready, 1)

        def weighted(dve, S, par, k):
            dve.wait_ge(S.y_done, k + 1)
            dve.wait_ge(S.y_free, k + 1)
            if cfg["out_scale"] is None:
                last = dve.tensor_scalar(y[:], py[:].rearrange("p a n -> p (a n)"), slots[:, par, 1:2], None, ALU.mult)
            else:
                last = dve.scalar_tensor_tensor(y[:], py[:].rearrange("p a n -> p (a n)"), slots[:, par, 1:2],
                                                cfg["out_scale"], ALU.mult, ALU.mult)
            last.then_inc(S.y_ready, 1)

        def identify(pe, S, k):
            pe.wait_ge(S.hits_ready, k + 1)
            for t in range(NT):
                last = pe.matmul(tp[:, 0, 0:4], hit[:, t, :], what[:, t, :], start=(t == 0), stop=(t == NT - 1))
            last.then_inc(S.ids_done, 1)

        def turn_rows(pe, S, par, loads, k):
            pe.wait_ge(S.ids_ready, k + 1)
            pe.wait_ge((S.gathered0, S.gathered1)[par], loads)
            transpose_tile(pe, tp, xg[:, par, :], ident).then_inc(S.x_turned, 1)

        def up(pe, S, k, slot_at, arrived):
            pe.wait_ge(S.xT_ready, k + 1)
            for u in range(2 * U1):
                out = pb if u % 2 else pa
                w = ring[:, slot_at + u, :].rearrange("p (c n) -> p c n", n=F)
                arrived(pe, slot_at + u)
                for n in range(HALVES):
                    for c in range(PER_UNIT):
                        at = u // 2 * PER_UNIT + c
                        last = pe.matmul(out[:, n, :], xT[:, at, :], w[:, c, n * 512:(n + 1) * 512],
                                         start=(at == 0), stop=(at == NC - 1))
                last.then_inc(S.units_used, 1)
            pe.sem_inc(S.passed, 1)

        def turn_hidden(pe, S, k, xT_done):
            pe.wait_ge(S.hid_ready, k + 1)
            if xT_done is not None:
                pe.wait_ge(S.xT_ready, xT_done)
            for c in range(FC):
                last = pe.transpose(tp[:, c, :], hid[:].rearrange("p (d c) -> p c d", c=FC)[:, c, :], ident)
            last.then_inc(S.hid_turned, 1)

        def down(pe, S, k, slot_at, arrived):
            pe.wait_ge(S.hidT_ready, k + 1)
            pe.wait_ge(S.y_ready, k + 1)
            for u in range(U2):
                w = ring[:, slot_at + 2 * U1 + u, :].rearrange("p (c n) -> p c n", n=D)
                arrived(pe, slot_at + 2 * U1 + u)
                for n in range(2):
                    for c in range(4):
                        at = 4 * u + c
                        last = pe.matmul(py[:, n, :], hidT[:, at, :], w[:, c, n * 512:(n + 1) * 512],
                                         start=(at == 0), stop=(at == FC - 1))
                if u < U2 - 1:
                    last.then_inc(S.units_used, 1)
            last.then_inc(S.y_done, 1)

        def silu(act, S, used, k):
            act.wait_ge(S.units_used, used)
            act.activation(act_out[:].rearrange("p (a n) -> p a n", n=512), pa[:, 0:HALVES, :],
                           ACT.Silu).then_inc(S.silu_done, 1)

        def keep_rows(act, S, k):
            act.wait_ge(S.x_turned, k + 1)
            act.copy(xT[:], tp[:]).then_inc(S.xT_ready, 1)

        def keep_hidden(act, S, k):
            act.wait_ge(S.hid_turned, k + 1)
            act.copy(hidT[:], tp[:, 0:FC, :]).then_inc(S.hidT_ready, 1)

        def gather(pool, S, par, k):
            hold(pool, S.ids_ready, k + 1, S.passed)
            pool.indirect_dma_start(xg[:, par, :], None, rows,
                                    bass.IndirectOffsetOnAxis(ap=gidx[:, par:par + 1], axis=0)) \
                .then_inc((S.gathered0, S.gathered1)[par], 16)

        def add_rows(pool, S, par, k):
            hold(pool, S.y_ready, k + 2, S.passed)
            pool.indirect_dma_start(sums, bass.IndirectOffsetOnAxis(ap=sidx[:, par:par + 1], axis=0), y[:], None,
                                    compute_op=ALU.add).then_inc(S.added, 16)
            hold(pool, S.added, 16 * k + 16, S.passed)
            pool.sem_inc(S.y_free, 1)

        def main_arrived(r):
            return lambda pe, slot: pe.wait_ge(unit_loaded[slot], 16 * r + 16)

        ROUNDS = NE // TOGETHER

        def weights(e):
            found = []
            for u in range(U1):
                for w in (io[cfg["w1"]], io[cfg["w3"]]):
                    found.append(cfg["pick"](w, e).rearrange("(p c) n -> p c n", c=NC)
                                 [:, u * PER_UNIT:(u + 1) * PER_UNIT, :])
            for u in range(U2):
                found.append(cfg["pick"](io[cfg["w2"]], e).rearrange("(p c) n -> p c n", c=FC)[:, 4 * u:4 * u + 4, :])
            return found

        @block.sync
        def _(sp):
            route.sync(sp)
            with sp.Fori(0, ROUNDS) as r:
                for b in range(TOGETHER):
                    for n, src in enumerate(weights(r * TOGETHER + b)):
                        slot = b * UNITS + n
                        sp.wait_ge(main.units_used, RING * r + slot + 1)
                        sp.dma_start(ring[:, slot, :].rearrange("p (c n) -> p c n", n=src.shape[2]), src) \
                            .then_inc(unit_loaded[slot], 16)
            if cfg["overflow"]:
                sp.wait_ge(routed, 1)
                n_over = sp.value_load(over[0:1, 15:16], min_val=0, max_val=MAX_OVER)
                sp.wait_ge(main.units_used, RING * (ROUNDS + 1))
                with sp.Fori(0, MAX_OVER) as j:
                    with sp.If(n_over > j):
                        e = sp.value_load(over[0:1, bass.ds(j, 1)], min_val=0, max_val=NE - 1)
                        sp.wait_ge(more.units_used, UNITS * j + 1)
                        for n, src in enumerate(weights(e)):
                            sp.dma_start(ring[:, n, :].rearrange("p (c n) -> p c n", n=src.shape[2]), src) \
                                .then_inc(more_loaded, 16)
                    with sp.Else():
                        sp.nop()
                    sp.nop()

        @block.gpsimd
        def _(pool):
            hold(pool, routed, 1, main.passed)
            gather(pool, main, 0, 0)
            with pool.Fori(0, NE // 2) as r:
                for b in range(2):
                    e = r * 2 + b
                    hold(pool, main.x_turned, e + 1, main.passed)
                    gather(pool, main, 1 - b, e + 1)
                    add_rows(pool, main, b, e)
            if cfg["overflow"]:
                n_over = pool.value_load(over[0:1, 15:16], min_val=0, max_val=MAX_OVER)
                with pool.Fori(0, MAX_OVER) as j:
                    with pool.If(n_over > j):
                        gather(pool, more, 0, j)
                        add_rows(pool, more, 0, j)
                    with pool.Else():
                        pool.nop()
                    pool.nop()

        @block.scalar
        def _(act):
            route.scalar(act)
            keep_rows(act, main, 0)
            with act.Fori(0, NE // 2) as r:
                for b in range(2):
                    e = r * 2 + b
                    silu(act, main, RING + UNITS * e + 2 * U1, e)
                    keep_rows(act, main, e + 1)
                    keep_hidden(act, main, e)
            if cfg["overflow"]:
                act.wait_ge(routed, 1)
                n_over = act.value_load(over[0:1, 15:16], min_val=0, max_val=MAX_OVER)
                with act.Fori(0, MAX_OVER) as j:
                    with act.If(n_over > j):
                        keep_rows(act, more, j)
                        silu(act, more, 1 + UNITS * j + 2 * U1, j)
                        keep_hidden(act, more, j)
                    with act.Else():
                        act.nop()
                    act.nop()

        @block.vector
        def _(dve):
            dve.sem_inc(main.y_free, 1)
            dve.sem_inc(main.y_ready, 1)
            step = Steps(dve, main.vec)
            step.did(dve.memset(slot_of[:, :, NE:NE + 1], FAR))
            step.did(dve.memset(gate[:, :, NE:NE + 1], 0.0))
            step.did(dve.memset(what[:], 1.0))
            step.wait()
            step.did(dve.tensor_copy(what[:, :, 0:1], ks[:, K_TOKEN:K_TOKEN + NT].unsqueeze(2)))
            route.vector(dve, step)
            step.wait()
            dve.sem_inc(routed, 1)
            hits(dve, main, step, 0, None, 0)
            indices(dve, main, step, 0, 0, 1)
            with dve.Fori(0, NE // 2) as r:
                step.enter(r, 2 * 3)
                for b in range(2):
                    e = r * 2 + b
                    hits(dve, main, step, e + 1, None, e + 1)
                    indices(dve, main, step, 1 - b, e + 1, e + 1)
                    hidden(dve, main, e)
                    weighted(dve, main, b, e)
                step.leave(NE // 2)
            if cfg["overflow"]:
                dve.sem_inc(more.y_free, 1)
                dve.sem_inc(more.y_ready, 1)
                o_step = Steps(dve, more.vec)
                n_over = dve.value_load(over[0:1, 15:16], min_val=0, max_val=MAX_OVER)
                with dve.Fori(0, MAX_OVER) as j:
                    with dve.If(n_over > j):
                        o_step.enter(j, 4)
                        e = dve.value_load(over[0:1, bass.ds(j, 1)], min_val=0, max_val=NE - 1)
                        hits(dve, more, o_step, e, over_from[:, bass.ds(j, 1)], j)
                        indices(dve, more, o_step, 0, j, j + 1)
                        hidden(dve, more, j)
                        weighted(dve, more, 0, j)
                        assert o_step.n == 4
                    with dve.Else():
                        dve.nop()
                    dve.nop()

        @block.tensor
        def _(pe):
            pe.sem_inc(main.units_used, RING)
            route.tensor(pe)
            identify(pe, main, 0)
            turn_rows(pe, main, 0, 16, 0)
            with pe.Fori(0, NE // 2) as r:
                for b in range(2):
                    e = r * 2 + b
                    at = b * UNITS if TOGETHER == 2 else 0
                    arrived = main_arrived(r if TOGETHER == 2 else e)
                    pe.wait_ge(main.xT_ready, e + 1)
                    identify(pe, main, e + 1)
                    up(pe, main, e, at, arrived)
                    turn_rows(pe, main, 1 - b, 16 * r + (16 if b == 0 else 32), e + 1)
                    turn_hidden(pe, main, e, e + 2)
                    down(pe, main, e, at, arrived)
                    pe.wait_ge(main.y_done, e + 1)
                    pe.sem_inc(main.units_used, 1)
            if cfg["overflow"]:
                pe.wait_ge(routed, 1)
                pe.sem_inc(more.units_used, 1)
                n_over = pe.value_load(over[0:1, 15:16], min_val=0, max_val=MAX_OVER)
                with pe.Fori(0, MAX_OVER) as j:
                    with pe.If(n_over > j):
                        def arrived(pe, slot):
                            pe.wait_ge(more_loaded, 16 * UNITS * j + 16 * UNITS)
                        identify(pe, more, j)
                        turn_rows(pe, more, 0, 16 * j + 16, j)
                        up(pe, more, j, 0, arrived)
                        turn_hidden(pe, more, j, None)
                        down(pe, more, j, 0, arrived)
                        pe.wait_ge(more.y_done, j + 1)
                        pe.sem_inc(more.units_used, 1)
                    with pe.Else():
                        pe.nop()
                    pe.nop()


class GroupRouting:

    def __init__(self, keep):
        self.keep = keep

    def buffers(self, ph, o):
        self.o = o
        self.w = {n: ph.sb(n, [P, NT * E1]) for n in
                  "le ml hot1 hot2 sel before".split()}
        self.g = {n: ph.sb(n, [P, NT * G1]) for n in "lg eq hotg away".split()}
        self.t = {n: ph.sb(n, [P, NT]) for n in "mg mt gw m1 m2 g1 g2 ed".split()}
        self.c = {n: ph.sb(n, [P, E1]) for n in "total counts extra ends ones".split()}
        self.over_w = ph.sb("over_w", [P, 2, MAX_OVER * E1])
        self.over_n = ph.sb("over_n", [P, 2, 16])
        self.onesm = ph.sb("onesm", [P, P])
        self.s = ph.sems("ranks_in ranks_done shifted group_exp pair_exp", ns=True)

    def sync(self, sp):
        pass

    def scalar(self, act):
        act.wait_ge(self.s.shifted, 1)
        act.activation(self.g["eq"][:], self.g["eq"][:], ACT.Exp).then_inc(self.s.group_exp, 1)
        act.wait_ge(self.s.shifted, 2)
        act.activation(self.t["ed"][:], self.t["ed"][:], ACT.Exp).then_inc(self.s.pair_exp, 1)

    def tensor(self, pe):
        pe.wait_ge(self.s.ranks_in, 1)
        n = NT * E1
        ranks, totals = self.o.pa[:, 0, 0:n], self.o.pb[:, 0, 0:E1]
        before = self.keep["consts"][:, K_BEFORE:K_BEFORE + P]
        pe.matmul(ranks, before, self.w["sel"][:], start=True, stop=False)
        pe.matmul(ranks, self.onesm[:], self.w["before"][:], start=False, stop=True)
        pe.matmul(totals, self.onesm[:], self.c["total"][:], start=True, stop=True).then_inc(self.s.ranks_done, 1)

    def vector(self, dve, step):
        w, g, t, c, o, s = self.w, self.g, self.t, self.c, self.o, self.s
        ks, logits = self.keep["consts"], self.keep["logits"]

        def do(instruction):
            step.did(instruction)
            step.wait()

        def tiles(x, n):
            return x[:].rearrange("p (t e) -> p t e", e=n)

        def first_of(hot, x, top, n):
            rev = ks[:, K_REV32 + 32 - n:K_REV32 + 32]
            do(dve.tensor_reduce(top[:], tiles(x, n), AX, ALU.max))
            do(dve.tensor_tensor(tiles(hot, n), tiles(x, n), spread(top[:], n), ALU.is_equal))
            do(dve.tensor_tensor(tiles(hot, n), tiles(hot, n), tiled(rev, NT), ALU.mult))
            do(dve.tensor_reduce(t["mt"][:], tiles(hot, n), AX, ALU.max))
            do(dve.tensor_tensor(tiles(hot, n), tiles(hot, n), spread(t["mt"][:], n), ALU.is_equal))

        do(dve.memset(self.onesm[:], 1.0))
        do(dve.memset(c["ones"][:], 1.0))
        do(dve.tensor_copy(tiles(g["lg"], G1), logits[:, :, 0:G1]))
        do(dve.tensor_copy(tiles(w["le"], E1), logits[:, :, G1:LOGITS]))
        first_of(g["hotg"], g["lg"], t["mg"], G1)
        step.did(dve.tensor_tensor(tiles(g["eq"], G1), tiles(g["lg"], G1), spread(t["mg"][:], G1), ALU.subtract))
        step.wait()
        dve.sem_inc(s.shifted, 1)
        do(dve.tensor_scalar(g["away"][:], g["hotg"][:], -1.0, -MASKED, ALU.add, ALU.mult))
        do(dve.tensor_tensor(tiles(w["ml"], PER_G), tiles(w["le"], PER_G), spread(g["hotg"][:], PER_G), ALU.mult))
        do(dve.tensor_tensor(tiles(w["ml"], PER_G), tiles(w["ml"], PER_G), spread(g["away"][:], PER_G), ALU.add))
        first_of(w["hot1"], w["ml"], t["m1"], E1)
        do(dve.scalar_tensor_tensor(w["ml"][:], w["hot1"][:], 10 * MASKED, w["ml"][:], ALU.mult, ALU.add))
        first_of(w["hot2"], w["ml"], t["m2"], E1)
        do(dve.tensor_tensor(t["ed"][:], t["m2"][:], t["m1"][:], ALU.subtract))
        dve.sem_inc(s.shifted, 1)
        do(dve.tensor_tensor(w["sel"][:], w["hot1"][:], w["hot2"][:], ALU.add))
        sel, before = tiles(w["sel"], E1), tiles(w["before"], E1)
        do(dve.memset(before[:, 0, :], 0.0))
        for n in range(1, NT):
            do(dve.tensor_tensor(before[:, n, :], before[:, n - 1, :], sel[:, n - 1, :], ALU.add))
        do(dve.tensor_tensor(c["total"][:], before[:, NT - 1, :], sel[:, NT - 1, :], ALU.add))
        dve.sem_inc(s.ranks_in, 1)
        dve.wait_ge(s.group_exp, 1)
        do(dve.tensor_reduce(t["gw"][:], tiles(g["eq"], G1), AX, ALU.add))
        dve.wait_ge(s.pair_exp, 1)
        do(dve.tensor_scalar(t["g1"][:], t["ed"][:], 1.0, None, ALU.add))
        do(dve.tensor_tensor(t["g1"][:], t["g1"][:], t["gw"][:], ALU.mult))
        do(dve.reciprocal(t["g1"][:], t["g1"][:]))
        do(dve.tensor_tensor(t["g2"][:], t["g1"][:], t["ed"][:], ALU.mult))
        do(dve.tensor_tensor(tiles(w["hot1"], E1), tiles(w["hot1"], E1), spread(t["g1"][:], E1), ALU.mult))
        do(dve.tensor_tensor(tiles(w["hot2"], E1), tiles(w["hot2"], E1), spread(t["g2"][:], E1), ALU.mult))
        do(dve.tensor_tensor(o.gate[:, :, 0:E1], tiles(w["hot1"], E1), tiles(w["hot2"], E1), ALU.add))
        dve.wait_ge(s.ranks_done, 1)
        do(dve.tensor_scalar(w["sel"][:], w["sel"][:], -FAR, FAR, ALU.mult, ALU.add))
        do(dve.tensor_tensor(o.slot_of[:, :, 0:E1], self.o.pa[:, 0, 0:NT * E1].rearrange("p (t e) -> p t e", e=E1),
                             sel, ALU.add))
        do(dve.tensor_copy(c["counts"][:], o.pb[:, 0, 0:E1]))
        do(dve.memset(c["extra"][:], 0.0))
        for n in range(1, T // P):
            do(dve.scalar_tensor_tensor(c["extra"][:], c["counts"][:], float(n * P), c["extra"][:], ALU.is_gt,
                                        ALU.add))
        do(dve.tensor_tensor_scan(c["ends"][:], c["ones"][:], c["extra"][:], 0.0, ALU.mult, ALU.add))
        past = self.over_w[:, 0, :].rearrange("p (j e) -> p j e", e=E1)
        gone = self.over_w[:, 1, :].rearrange("p (j e) -> p j e", e=E1)
        iota = ks[:, K_IOTA:K_IOTA + MAX_OVER]
        do(dve.tensor_tensor(past, spread(iota, E1), tiled(c["ends"][:], MAX_OVER), ALU.is_ge))
        do(dve.tensor_tensor(gone, past, tiled(c["extra"][:], MAX_OVER), ALU.mult))
        do(dve.tensor_reduce(self.over_n[:, 0, 0:MAX_OVER], past, AX, ALU.add))
        do(dve.tensor_reduce(self.over_n[:, 1, 0:MAX_OVER], gone, AX, ALU.add))
        do(dve.tensor_scalar(self.over_n[:, 0, 0:MAX_OVER], self.over_n[:, 0, 0:MAX_OVER], float(E1 - 1), None,
                             ALU.min))
        do(dve.tensor_tensor(self.over_n[:, 1, 0:MAX_OVER], iota, self.over_n[:, 1, 0:MAX_OVER], ALU.subtract))
        do(dve.tensor_scalar(o.over_from[:, 0:MAX_OVER], self.over_n[:, 1, 0:MAX_OVER], 1.0, float(P), ALU.add,
                             ALU.mult))
        do(dve.tensor_copy(o.over[:, 0:MAX_OVER], self.over_n[:, 0, 0:MAX_OVER]))
        do(dve.tensor_copy(o.over[:, 15:16], c["ends"][:, E1 - 1:E1]))


def columns(v):
    return v.rearrange("(c p) -> p c", p=P)


def phase_second_norm(nc, io, keep):
    ks, hT, yT, zT, mod = keep["consts"], keep["hT"], keep["yT"], keep["zT"], keep["mod"]
    ident = ks[:, K_IDENT:K_IDENT + P]
    HALF = T // 2
    with Phase(nc, "norm2") as ph:
        w = ph.sb("w", [P, NC, 2 * LRU])
        mod1 = ph.sb("mod1", [P, 2, D])
        v = keep["v"][:].rearrange("p t n -> p (t n)").rearrange("p (a n) -> p a n", n=D)
        xt, hn2 = v[:, 0:2, :], v[:, 2:4, :]
        junk, g12 = keep["qT"][:, 0:2, :], keep["kT"][:, 0:2, :]
        part, b_mod = keep["kT"][:, 2:3, :], keep["kT"][:, 3:4, :]
        part = part.rearrange("p a n -> p (a n)").rearrange("p (a n) -> p a n", n=512)
        b_mod = b_mod.rearrange("p a n -> p (a n)").rearrange("p (a n) -> p a n", n=512)
        st = ph.sb("st", [P, 4])
        ones = ph.sb("ones", [P, P])
        banks = ph.ps("banks", [P, 8, 512])
        tp2 = [banks[:, 2 * n:2 * n + 2, :].rearrange("p a (c n) -> p (a c) n", n=P) for n in range(2)]
        s = ph.sems("gains_loaded w_loaded part0 part1 bias0 bias1 ones_ready summed added ready "
                    "x_loaded0 x_loaded1 x_free squared rms normed turned hT_ready vec pool_steps passed "
                    "z_done x_done z_read x_read", ns=True)
        part_loaded, bias_loaded, x_loaded = [s.part0, s.part1], [s.bias0, s.bias1], [s.x_loaded0, s.x_loaded1]
        home = [mod1[:, 0, :], mod1[:, 1, :]] + [mod[:, n, :] for n in range(4)]
        block = ph.block()

        @block.sync
        def _(sp):
            for n, name in enumerate(("g_norm1_2", "g_norm2_2")):
                sp.dma_start(g12[:, n, :], io[name][0].partition_broadcast(P)).then_inc(s.gains_loaded, 16)
            for n in range(MOD // 512):
                if n >= 2:
                    sp.wait_ge(s.added, n - 1)
                sp.dma_start(part[:, n % 2, :], keep["mod_part"][:, n * 512:(n + 1) * 512]) \
                    .then_inc(part_loaded[n % 2], 16)
                sp.dma_start(b_mod[:, n % 2, :], io["b_mod_2"][0, n * 512:(n + 1) * 512].partition_broadcast(P)) \
                    .then_inc(bias_loaded[n % 2], 16)
            with sp.Fori(0, NT // 2) as r:
                for h in range(2):
                    sp.wait_ge(s.x_free, 2 * r + h + 1)
                    sp.dma_start(xt[:, h, :], keep["acc"][bass.ds(r * (2 * P) + h * P, P), :]) \
                        .then_inc(x_loaded[h], 16)
            sp.dma_start(w[:], rows_by_partition(io["w_in_2"][0][:, 0:2 * LRU])).then_inc(s.w_loaded, 16)

        @block.gpsimd
        def _(pool):
            step = Steps(pool, s.pool_steps)
            with pool.Fori(0, NT // 2) as r:
                step.enter(r, 2)
                for h in range(2):
                    hold(pool, s.squared, 2 * r + h + 1, s.passed)
                    inverse_root(pool, step, st[:, 2 + h:3 + h], st[:, h:h + 1], keep["minus_half"]) \
                        .then_inc(s.rms, 1)
                step.leave(NT // 2)

        @block.scalar
        def _(act):
            with act.Fori(0, NT // 2) as r:
                for h in range(2):
                    act.wait_ge(x_loaded[h], 16 * r + 16)
                    act.activation(junk[:, h, :], xt[:, h, :], ACT.Square, scale=D ** -0.5,
                                   accum_out=st[:, h:h + 1]).then_inc(s.squared, 1)
                for h in range(2):
                    hold(act, s.turned, 2 * r + h + 1, s.passed)
                    act.copy(hT[:, :, bass.ds(r * (2 * P) + h * P, P)], tp2[h]).then_inc(s.hT_ready, 1)
            with act.Fori(0, 2) as n:
                for j in range(LC):
                    hold(act, s.z_done, LC * n + j + 1, s.passed)
                    act.activation(zT[:, j, bass.ds(n * HALF, HALF)], banks[:, LC + j, :],
                                   ACT.Gelu_apprx_tanh).then_inc(s.z_read, 1)

        @block.vector
        def _(dve):
            step = Steps(dve, s.vec)
            dve.memset(ones[:], 1.0).then_inc(s.ones_ready, 1)
            dve.sem_inc(s.x_free, 2)
            dve.sem_inc(s.x_read, LC)
            dve.sem_inc(s.z_read, LC)
            for n in range(MOD // 512):
                dve.wait_ge(s.summed, n + 1)
                dve.wait_ge(bias_loaded[n % 2], 16 * (n // 2 + 1))
                dve.tensor_tensor(home[n // 2][:, n % 2 * 512:(n % 2 + 1) * 512], banks[:, n % 2, :],
                                  b_mod[:, n % 2, :], ALU.add).then_inc(s.added, 1)
            dve.wait_ge(s.added, MOD // 512)
            dve.wait_ge(s.gains_loaded, 32)
            step.did(dve.scalar_tensor_tensor(home[1], home[1], 1.0, g12[:, 0, :], ALU.add, ALU.mult))
            step.did(dve.scalar_tensor_tensor(home[4], home[4], 1.0, g12[:, 1, :], ALU.add, ALU.mult))
            step.wait()
            with dve.Fori(0, NT // 2) as r:
                step.enter(r, 2)
                for h in range(2):
                    dve.wait_ge(s.rms, 2 * r + h + 1)
                    dve.wait_ge(s.x_free, 2 * r + h + 1)
                    step.did(dve.scalar_tensor_tensor(hn2[:, h, :], xt[:, h, :], st[:, 2 + h:3 + h], home[1],
                                                      ALU.mult, ALU.mult))
                    step.wait()
                    dve.tensor_tensor(hn2[:, h, :], hn2[:, h, :], home[0], ALU.add).then_inc(s.normed, 1)
                for h in range(2):
                    dve.wait_ge(s.turned, 2 * r + h + 1)
                    dve.sem_inc(s.x_free, 1)
                step.leave(NT // 2)
            with dve.Fori(0, 2) as n:
                for j in range(LC):
                    dve.wait_ge(s.x_done, LC * n + j + 1)
                    dve.tensor_scalar(yT[:, j, bass.ds(n * HALF, HALF)], banks[:, j, :], 1.0, None,
                                      ALU.mult).then_inc(s.x_read, 1)

        @block.tensor
        def _(pe):
            pe.wait_ge(s.ones_ready, 1)
            for n in range(MOD // 512):
                pe.wait_ge(part_loaded[n % 2], 16 * (n // 2 + 1))
                if n >= 2:
                    pe.wait_ge(s.added, n - 1)
                pe.matmul(banks[:, n % 2, :], ones[:], part[:, n % 2, :], start=True, stop=True).then_inc(s.summed, 1)
            pe.wait_ge(s.added, MOD // 512)
            with pe.Fori(0, NT // 2) as r:
                for h in range(2):
                    pe.wait_ge(s.normed, 2 * r + h + 1)
                    transpose_tile(pe, tp2[h], hn2[:, h, :], ident).then_inc(s.turned, 1)
            pe.wait_ge(s.hT_ready, NT)
            pe.wait_ge(s.w_loaded, 16)
            with pe.Fori(0, 2) as n:
                for j in range(2 * LC):
                    done, read = (s.x_done, s.x_read) if j < LC else (s.z_done, s.z_read)
                    pe.wait_ge(read, LC * n + j % LC + 1)
                    for c in range(NC):
                        last = pe.matmul(banks[:, j, :], w[:, c, j * P:(j + 1) * P],
                                         hT[:, c, bass.ds(n * HALF, HALF)], start=(c == 0), stop=(c == NC - 1))
                    last.then_inc(done, 1)


def phase_lru(nc, io, keep):
    yT, zT = keep["yT"], keep["zT"]
    with Phase(nc, "lru") as ph:
        taps = ph.sb("taps", [P, 4, LC])
        conv_b = ph.sb("conv_b", [P, LC])
        lam = ph.sb("lam", [P, 2 * LC])
        sig = ph.sb("sig", [P, 4, 2 * LC])
        biases = ph.sb("biases", [P, 2, 2 * LC])
        blocks = ph.sb("blocks", [P, 2, 2 * LC, P])
        xc = ph.sb("xc", [P, 2, T])
        tr = ph.sb("tr", [P, 2, T])
        ti = ph.sb("ti", [P, 2, T])
        a = ph.sb("a", [P, 2, T])
        th = ph.sb("th", [P, 2, T])
        om = ph.sb("om", [P, 2, T])
        u, hs = keep["qT"][:, 0:2, :], keep["qT"][:, 2:4, :]
        gates = [ph.ps(f"gates{n}", [P, 2, 2, 512]) for n in range(2)]
        s = ph.sems("loaded blocks_clear blocks_loaded lam_ready convolved gates_done gates_read decays "
                    "squares roots vec passed half_ready scans", ns=True)
        block = ph.block()
        turns = [(j, d) for j in range(LC) for d in range(2)]

        @block.sync
        def _(sp):
            def one(dst, src):
                sp.dma_start(dst, src, allow_slow_non_contiguous=True).then_inc(s.loaded, 16)
            for k in range(4):
                one(taps[:, k, :], columns(io["conv_w_2"][0, k, 0]))
            one(conv_b[:], columns(io["conv_b_2"][0]))
            for d in range(2):
                one(lam[:, d * LC:(d + 1) * LC], columns(io["lru_lambda_2"][0, d]))
                one(biases[:, 0, d * LC:(d + 1) * LC], columns(io["lru_b_a_2"][0, d]))
                one(biases[:, 1, d * LC:(d + 1) * LC], columns(io["lru_b_x_2"][0, d]))
            sp.wait_ge(s.blocks_clear, 1)
            for g, name in enumerate(("lru_w_a_2", "lru_w_x_2")):
                for d in range(2):
                    for e in range(2):
                        sp.dma_start(blocks[e * 64:(e + 1) * 64, g, d * LC:(d + 1) * LC, e * 64:(e + 1) * 64],
                                     io[name][0, d].rearrange("(j e) c n -> e c j n", e=2)[e]) \
                            .then_inc(s.blocks_loaded, 16)

        @block.gpsimd
        def _(pool):
            pool.memset(blocks[:], 0.0).then_inc(s.blocks_clear, 1)

        @block.scalar
        def _(act):
            act.wait_ge(s.loaded, 16 * 11)
            act.activation(sig[:, 1, :], lam[:], ACT.Abs).then_inc(s.half_ready, 1)
            act.wait_ge(s.half_ready, 1)
            act.activation(sig[:, 1, :], sig[:, 1, :], ACT.Exp, scale=-1.0).then_inc(s.half_ready, 1)
            for n in range(2):
                act.mul(biases[:, n, :], biases[:, n, :], 0.5).then_inc(s.half_ready, 1)
            act.wait_ge(s.half_ready, 4)
            act.wait_ge(s.lam_ready, 1)
            for m, (j, d) in enumerate(turns):
                at = d * LC + j
                act.wait_ge(s.gates_done, m + 1)
                if m >= 2:
                    act.wait_ge(s.scans, m - 1)
                for g, t in ((0, tr), (1, ti)):
                    act.activation(t[:, d, :].rearrange("p (a n) -> p a n", n=512), gates[m % 2][:, g, :, :],
                                   ACT.Tanh, scale=0.5, bias=biases[:, g, at:at + 1]).then_inc(s.gates_read, 1)
                act.wait_ge(s.gates_read, 2 * m + 1)
                act.activation(a[:, d, :], tr[:, d, :], ACT.Exp, scale=sig[:, 0, at:at + 1],
                               bias=sig[:, 0, at:at + 1])
                act.activation(th[:, d, :], tr[:, d, :], ACT.Tanh, scale=sig[:, 0, at:at + 1],
                               bias=sig[:, 0, at:at + 1]).then_inc(s.decays, 1)
                if d:
                    for e in range(2):
                        act.wait_ge(s.squares, m + e)
                        act.activation(om[:, e, :], om[:, e, :], ACT.Sqrt, scale=-2.0).then_inc(s.roots, 1)

        @block.vector
        def _(dve):
            step = Steps(dve, s.vec)

            def do(instruction):
                step.did(instruction)
                step.wait()

            dve.wait_ge(s.half_ready, 2)
            do(dve.tensor_scalar(sig[:, 2, :], sig[:, 1, :], 2.0, None, ALU.add))
            do(dve.reciprocal(sig[:, 2, :], sig[:, 2, :]))
            do(dve.tensor_tensor(sig[:, 1, :], sig[:, 1, :], sig[:, 2, :], ALU.mult))
            do(dve.tensor_tensor(sig[:, 2, :], sig[:, 1, :], sig[:, 1, :], ALU.mult))
            do(dve.memset(sig[:, 3, :], 1.0 / 17))
            for k in range(15, 0, -2):
                do(dve.tensor_tensor(sig[:, 3, :], sig[:, 3, :], sig[:, 2, :], ALU.mult))
                do(dve.tensor_scalar(sig[:, 3, :], sig[:, 3, :], 1.0 / k, None, ALU.add))
            do(dve.tensor_tensor(sig[:, 3, :], sig[:, 3, :], sig[:, 1, :], ALU.mult))
            do(dve.tensor_scalar(sig[:, 0, :], lam[:], 0.0, None, ALU.min))
            do(dve.scalar_tensor_tensor(sig[:, 0, :], sig[:, 3, :], -2.0, sig[:, 0, :], ALU.mult, ALU.add))
            do(dve.tensor_scalar(sig[:, 0, :], sig[:, 0, :], 4.0, None, ALU.mult))
            dve.sem_inc(s.lam_ready, 1)
            dve.wait_ge(s.loaded, 16 * 11)

            def convolve(j):
                x, out = yT[:, j, :], xc[:, j % 2, :]
                do(dve.tensor_scalar(out, x, taps[:, 2, j:j + 1], conv_b[:, j:j + 1], ALU.mult, ALU.add))
                do(dve.scalar_tensor_tensor(out[:, 2:T], x[:, 0:T - 2], taps[:, 0, j:j + 1], out[:, 2:T], ALU.mult,
                                            ALU.add))
                do(dve.scalar_tensor_tensor(out[:, 1:T], x[:, 0:T - 1], taps[:, 1, j:j + 1], out[:, 1:T], ALU.mult,
                                            ALU.add))
                dve.scalar_tensor_tensor(out[:, 0:T - 1], x[:, 1:T], taps[:, 3, j:j + 1], out[:, 0:T - 1], ALU.mult,
                                         ALU.add).then_inc(s.convolved, 1)

            convolve(0)
            for j in range(LC):
                if j + 1 < LC:
                    if j:
                        dve.wait_ge(s.gates_done, 2 * j)
                    convolve(j + 1)
                dve.wait_ge(s.convolved, j + 1)
                for d in range(2):
                    dve.wait_ge(s.decays, 2 * j + d + 1)
                    do(dve.tensor_scalar(om[:, d, :], th[:, d, :], -1.0, 1.0, ALU.mult, ALU.add))
                    do(dve.reciprocal(om[:, d, :], om[:, d, :]))
                    dve.tensor_tensor(om[:, d, :], om[:, d, :], th[:, d, :], ALU.mult).then_inc(s.squares, 1)
                    step.did(dve.scalar_tensor_tensor(u[:, d, :], ti[:, d, :], 1.0, xc[:, j % 2, :], ALU.add,
                                                      ALU.mult))
                step.wait()
                for d in range(2):
                    dve.wait_ge(s.roots, 2 * j + d + 1)
                    do(dve.scalar_tensor_tensor(u[:, d, :], om[:, d, :], 0.5, u[:, d, :], ALU.mult, ALU.mult))
                    way = slice(None, None, -1) if d else slice(None)
                    dve.tensor_tensor_scan(hs[:, d, :][:, way], a[:, d, :][:, way], u[:, d, :][:, way], 0.0,
                                           ALU.mult, ALU.add).then_inc(s.scans, 1)
                dve.wait_ge(s.scans, 2 * j + 2)
                do(dve.tensor_tensor(hs[:, 0, :], hs[:, 0, :], hs[:, 1, :], ALU.add))
                do(dve.tensor_tensor(yT[:, j, :], hs[:, 0, :], zT[:, j, :], ALU.mult))

        @block.tensor
        def _(pe):
            pe.wait_ge(s.blocks_loaded, 16 * 8)
            for m, (j, d) in enumerate(turns):
                pe.wait_ge(s.convolved, j + 1)
                if m >= 2:
                    pe.wait_ge(s.gates_read, 2 * (m - 1))
                for g in range(2):
                    for n in range(2):
                        last = pe.matmul(gates[m % 2][:, g, n, :], blocks[:, g, d * LC + j, :],
                                         xc[:, j % 2, n * 512:(n + 1) * 512], start=True, stop=True)
                last.then_inc(s.gates_done, 1)


def phase_qkv(nc, io, keep):
    ks, hT, qT, kT, v = keep["consts"], keep["hT"], keep["qT"], keep["kT"], keep["v"]
    ident = ks[:, K_IDENT:K_IDENT + P]
    QW = AH * 2 * DK
    GROUPS = 2 * QW // DK
    with Phase(nc, "qkv") as ph:
        w = ph.sb("w", [P, NC, 3 * QW])
        h2 = ph.sb("h", [P, 2, NC, P])
        gains = ph.sb("gains", [P, 2])
        qk_gain = ph.sb("qk_gain", [P, 1])
        work = ph.sb("work", [P, 2, 2 * QW])
        ss = ph.sb("ss", [P, 2, 2 * GROUPS])
        out2 = [ph.ps(f"out{n}", [P, 3, 512]) for n in range(2)]
        tp = ph.ps("tp", [P, 2 * AH, P])
        s = ph.sems("gains_loaded w_loaded taken qkv_done squared summed rms normed turned q_ready k_ready v_ready "
                    "pool_steps passed vec", ns=True)
        block = ph.block()

        @block.sync
        def _(sp):
            for r in range(2):
                for n, name in enumerate(("g_q_2", "g_k_2")):
                    sp.dma_start(gains[r * DK:(r + 1) * DK, n:n + 1], io[name].rearrange("o p -> p o")) \
                        .then_inc(s.gains_loaded, 16)
            sp.dma_start(w[:], rows_by_partition(io["w_in_2"][0][:, 2 * LRU:2 * LRU + 3 * QW])).then_inc(s.w_loaded, 16)

        @block.gpsimd
        def _(pool):
            step = Steps(pool, s.pool_steps)
            with pool.Fori(0, NT // 2) as r:
                step.enter(r, 2)
                for h in range(2):
                    hold(pool, s.summed, 2 * r + h + 1, s.passed)
                    inverse_root(pool, step, ss[:, h, GROUPS:2 * GROUPS], ss[:, h, 0:GROUPS], keep["minus_half"]) \
                        .then_inc(s.rms, 1)
                step.leave(NT // 2)

        @block.scalar
        def _(act):
            with act.Fori(0, NT // 2) as r:
                for h in range(2):
                    t = 2 * r + h
                    act.wait_ge(s.qkv_done, t + 1)
                    act.activation(work[:, h, :].rearrange("p (a n) -> p a n", n=512), out2[h][:, 0:2, :],
                                   ACT.Square, scale=DK ** -0.5).then_inc(s.squared, 1)
                    act.copy(tile_of(v, t), out2[h][:, 2, :]).then_inc(s.v_ready, 1)
                for h in range(2):
                    t = 2 * r + h
                    hold(act, s.turned, t + 1, s.passed)
                    act.copy(qT[:, :, bass.ds(t * P, P)], tp[:, 0:AH, :]).then_inc(s.q_ready, 1)

        @block.vector
        def _(dve):
            step = Steps(dve, s.vec)
            dve.wait_ge(s.gains_loaded, 64)
            step.did(dve.scalar_tensor_tensor(qk_gain[:], gains[:, 0:1], DK ** -0.5, gains[:, 1:2], ALU.mult,
                                              ALU.mult))
            step.wait()
            dve.sem_inc(s.v_ready, 2)
            with dve.Fori(0, NT // 2) as r:
                for h in range(2):
                    t = 2 * r + h
                    dve.wait_ge(s.v_ready, t + 1)
                    dve.tensor_scalar(h2[:, h, :, :], hT[:, :, bass.ds(t * P, P)], 1.0, None, ALU.mult) \
                        .then_inc(s.taken, 1)
                for h in range(2):
                    t = 2 * r + h
                    dve.wait_ge(s.squared, t + 1)
                    dve.tensor_reduce(ss[:, h, 0:GROUPS], work[:, h, :].rearrange("p (g d) -> p g d", d=DK), AX,
                                      ALU.add).then_inc(s.summed, 1)
                for h in range(2):
                    t = 2 * r + h
                    dve.wait_ge(s.rms, t + 1)
                    dve.tensor_tensor(work[:, h, :].rearrange("p (g d) -> p g d", d=DK),
                                      out2[h][:, 0:2, :].rearrange("p a (g d) -> p (a g) d", d=DK),
                                      spread(ss[:, h, GROUPS:2 * GROUPS], DK), ALU.mult).then_inc(s.normed, 1)
                for h in range(2):
                    t = 2 * r + h
                    dve.wait_ge(s.turned, t + 1)
                    dve.tensor_scalar(kT[:, :, bass.ds(t * P, P)], tp[:, AH:2 * AH, :], qk_gain[:], None,
                                      ALU.mult).then_inc(s.k_ready, 1)

        @block.tensor
        def _(pe):
            pe.sem_inc(s.q_ready, 1)
            pe.sem_inc(s.k_ready, 1)
            pe.wait_ge(s.w_loaded, 16)
            with pe.Fori(0, NT // 2) as r:
                for h in range(2):
                    t = 2 * r + h
                    pe.wait_ge(s.taken, t + 1)
                    for n in range(3):
                        last = product(pe, out2[h][:, n, :], h2[:, h, :, :], w[:, :, n * 512:(n + 1) * 512])
                    last.then_inc(s.qkv_done, 1)
                for h in range(2):
                    t = 2 * r + h
                    pe.wait_ge(s.normed, t + 1)
                    pe.wait_ge(s.q_ready, t + 1)
                    pe.wait_ge(s.k_ready, t + 1)
                    for c in range(2 * AH):
                        last = pe.transpose(tp[:, c, :], work[:, h, c * P:(c + 1) * P], ident)
                    last.then_inc(s.turned, 1)


WIDE = 2 * T - P
NEAR = 3 * P


def phase_attention(nc, io, keep):
    ks, qT, kT, v, o = keep["consts"], keep["qT"], keep["kT"], keep["v"], keep["o"]
    ident = ks[:, K_IDENT:K_IDENT + P]
    with Phase(nc, "att") as ph:
        bias = ph.sb("bias", [P, AH, WIDE])
        stage = ph.sb("stage", [P, 2, T])
        pr = ph.sb("pr", [P, 2, 2, T])
        wT = ph.sb("wT", [P, 2, NT, P])
        qs = ph.sb("qs", [P, 2, AH, P])
        table = ph.sb("table", [BUCKETS, AH])
        spread_table = ph.sb("spread_table", [P, BUCKETS * AH])
        line = ph.sb("line", [AH, 512])
        lq = ph.sb("lq", [P, 4, DK])
        st = ph.sb("st", [P, 8])
        sm = ph.sb("sm", [P, 2, 8])
        sc = [ph.ps(f"sc{n}", [P, 2, 512]) for n in range(2)]
        tp = ph.ps("tp", [P, NT, P])
        po = [ph.ps(f"po{n}", [P, 512]) for n in range(2)]
        s = ph.sems("table_loaded line_done line_ready line_stored near_loaded constants_ready lam_summed lam_exp "
                    "lam_ready taken staged stage_free scored tops exps weighted w_turned wT_ready o_done o_read "
                    "vec passed q_free", ns=True)
        line_dram = keep["line"]
        block = ph.block()

        @block.sync
        def _(sp):
            sp.dma_start(table[:], io["rel_bias_2"]).then_inc(s.table_loaded, 16)
            sp.dma_start(spread_table[:], io["rel_bias_2"].rearrange("b h -> (b h)").partition_broadcast(P)) \
                .then_inc(s.table_loaded, 16)
            sp.dma_start(lq[:], io["lambda_qk_2"][0].rearrange("a d -> (a d)").partition_broadcast(P)) \
                .then_inc(s.table_loaded, 16)
            sp.wait_ge(s.line_ready, 1)
            sp.dma_start(line_dram, tiled(line[:], P)).then_inc(s.line_stored, 16)
            sp.wait_ge(s.line_stored, 16)
            for h in range(AH):
                sp.dma_start(bias[:, h, 768:768 + NEAR],
                             bass.AP(line_dram.tensor, h * P * 512 + P - 1, [[511, P], [1, NEAR]])) \
                    .then_inc(s.near_loaded, 16)

        @block.gpsimd
        def _(pool):
            pool.wait_ge(s.near_loaded, 16 * AH)
            pool.wait_ge(s.constants_ready, 1)
            with pool.Fori(0, NT // 2) as r:
                for n in range(2 * AH):
                    hold(pool, s.stage_free, 2 * AH * r + n + 1, s.passed)
                    pool.tensor_copy(stage[:, n % 2, :],
                                     bias[:, n % AH, bass.ds((NT - 1) * P - n // AH * P - r * (2 * P), T)]) \
                        .then_inc(s.staged, 1)

        @block.scalar
        def _(act):
            act.wait_ge(s.line_done, 1)
            act.copy(line[:], po[0][0:AH, :]).then_inc(s.line_ready, 1)
            act.wait_ge(s.lam_summed, 1)
            act.activation(st[:, 2:4], st[:, 0:2], ACT.Exp).then_inc(s.lam_exp, 1)
            act.wait_ge(s.lam_exp, 1)
            with act.Fori(0, NT // 2) as r:
                at = 2 * AH * r
                for n in range(2 * AH + 1):
                    b = n % 2
                    if n < 2 * AH:
                        act.wait_ge(s.tops, at + n + 1)
                        for j in range(2):
                            last = act.activation(pr[:, b, j, :], pr[:, b, j, :], ACT.Exp, bias=sm[:, b, j + 2:j + 3],
                                                  accum_out=sm[:, b, j + 4:j + 5])
                        last.then_inc(s.exps, 1)
                    if n:
                        act.wait_ge(s.w_turned, at + n)
                        act.copy(wT[:, 1 - b, :, :], tp[:]).then_inc(s.wT_ready, 1)

        @block.vector
        def _(dve):
            step = Steps(dve, s.vec)
            dve.wait_ge(s.table_loaded, 48)
            for n in range(2):
                step.did(dve.tensor_tensor(lq[:, 2 * n, :], lq[:, 2 * n, :], lq[:, 2 * n + 1, :], ALU.mult))
            step.wait()
            for n in range(2):
                step.did(dve.tensor_reduce(st[:, n:n + 1], lq[:, 2 * n, :], AX, ALU.add))
            step.wait()
            dve.sem_inc(s.lam_summed, 1)
            for h in range(AH):
                for lo, hi, bucket in ((0, 768, 15), (768 + NEAR, WIDE, 31)):
                    step.did(dve.tensor_copy(bias[:, h, lo:hi],
                                             spread_table[:, bucket * AH + h:bucket * AH + h + 1]
                                             .broadcast_to([P, hi - lo])))
            step.wait()
            dve.sem_inc(s.constants_ready, 1)
            dve.wait_ge(s.lam_exp, 1)
            step.did(dve.tensor_tensor(st[:, 4:5], st[:, 3:4], st[:, 2:3], ALU.subtract))
            step.wait()
            step.did(dve.tensor_scalar(st[:, 4:5], st[:, 4:5], -LAM_INIT, None, ALU.add))
            step.wait()
            dve.sem_inc(s.stage_free, 2)
            with dve.Fori(0, NT // 2) as r:
                at = 2 * AH * r
                step.enter(r, 6 * AH * 2)
                for n in range(2 * AH + 1):
                    b = n % 2
                    if n % AH == 0 and n < 2 * AH:
                        i = n // AH
                        if i == 0:
                            dve.wait_ge(s.q_free, r + 1)
                            for m in range(2):
                                dve.tensor_scalar(qs[:, m, :, :], qT[:, :, bass.ds(r * (2 * P) + m * P, P)], 1.0, None,
                                                  ALU.mult).then_inc(s.taken, 1)
                    if n < 2 * AH:
                        hold(dve, s.scored, at + n + 1, s.passed)
                        hold(dve, s.staged, at + n + 1, s.passed)
                        for j in range(2):
                            step.did(dve.tensor_tensor_reduce(pr[:, b, j, :], sc[j][:].rearrange("p a n -> p (a n)"),
                                                              stage[:, b, :], 1.0, -3e38, ALU.add, ALU.max,
                                                              sm[:, b, j:j + 1]))
                        step.wait()
                        dve.sem_inc(s.stage_free, 1)
                        dve.tensor_scalar(sm[:, b, 2:4], sm[:, b, 0:2], -1.0, None, ALU.mult).then_inc(s.tops, 1)
                    if n:
                        c = 1 - b
                        dve.wait_ge(s.exps, at + n)
                        step.did(dve.reciprocal(sm[:, c, 6:8], sm[:, c, 4:6]))
                        step.wait()
                        step.did(dve.tensor_tensor(sm[:, c, 7:8], sm[:, c, 7:8], st[:, 4:5], ALU.mult))
                        step.wait()
                        step.did(dve.tensor_scalar(pr[:, c, 1, :], pr[:, c, 1, :], sm[:, c, 7:8], None, ALU.mult))
                        step.wait()
                        dve.scalar_tensor_tensor(pr[:, c, 0, :], pr[:, c, 0, :], sm[:, c, 6:7], pr[:, c, 1, :],
                                                 ALU.mult, ALU.add).then_inc(s.weighted, 1)
                        dve.wait_ge(s.o_done, at + n)
                        h = (n - 1) % AH
                        step.did(dve.tensor_scalar(
                            tile_of(o, 2 * r + (n - 1) // AH)[:, h * DV:(h + 1) * DV], po[c][:, 0:DV], 1.0, None,
                            ALU.mult))
                        step.wait()
                        dve.sem_inc(s.o_read, 1)
                step.leave(NT // 2)

        @block.tensor
        def _(pe):
            pe.wait_ge(s.table_loaded, 48)
            pe.matmul(po[0][0:AH, :], table[:], ks[0:BUCKETS, K_BUCKET:K_BUCKET + 512], start=True,
                      stop=True).then_inc(s.line_done, 1)
            pe.sem_inc(s.q_free, 1)
            pe.wait_ge(s.line_ready, 1)
            with pe.Fori(0, NT // 2) as r:
                at = 2 * AH * r
                for n in range(2 * AH + 1):
                    if n < 2 * AH:
                        i, h = n // AH, n % AH
                        if h == 0:
                            pe.wait_ge(s.taken, 2 * r + i + 1)
                        if n:
                            pe.wait_ge(s.tops, at + n)
                        for m in range(2):
                            for j in range(2):
                                last = pe.matmul(sc[j][:, m, :], qs[j * DK:(j + 1) * DK, i, h, :],
                                                 kT[j * DK:(j + 1) * DK, h, m * 512:(m + 1) * 512], start=True,
                                                 stop=True)
                        last.then_inc(s.scored, 1)
                    if n:
                        c, h = (n - 1) % 2, (n - 1) % AH
                        pe.wait_ge(s.weighted, at + n)
                        for m in range(NT):
                            last = pe.transpose(tp[:, m, :], pr[:, c, 0, m * P:(m + 1) * P], ident)
                        last.then_inc(s.w_turned, 1)
                        pe.wait_ge(s.wT_ready, at + n)
                        for m in range(NT):
                            last = pe.matmul(po[c][:, 0:DV], wT[:, c, m, :], v[:, m, h * DV:(h + 1) * DV],
                                             start=(m == 0), stop=(m == NT - 1))
                        last.then_inc(s.o_done, 1)
                pe.sem_inc(s.q_free, 1)
                pe.wait_ge(s.o_read, at + 2 * AH)


def phase_second_out(nc, io, keep):
    ks, yT, o, mod, logits = keep["consts"], keep["yT"], keep["o"], keep["mod"], keep["logits2"]
    ident = ks[:, K_IDENT:K_IDENT + P]
    with Phase(nc, "out2") as ph:
        w = ph.sb("w", [P, NC, D])
        wr = ph.sb("wr", [P, NC, E2])
        o_gain = ph.sb("o_gain", [P, DV])
        xt = ph.sb("xt", [P, 2, D])
        left = ph.sb("left", [P, 2, NC, P])
        on = ph.sb("on", [P, 2, AH * DV])
        junk = ph.sb("junk", [P, 2, D])
        hn2 = ph.sb("hn", [P, 2, D])
        hT2 = ph.sb("hT", [P, 2, NC, P])
        st = ph.sb("st", [P, 2, 16])
        tp2 = [ph.ps(f"tp{n}", [P, NC, P]) for n in range(2)]
        acc2 = [ph.ps(f"acc{n}", [P, 2, 512]) for n in range(2)]
        s = ph.sems("gain_loaded w_loaded wr_loaded x_loaded0 x_loaded1 o_squared o_summed o_rms o_normed o_turned "
                    "left_ready y_taken out_done scaled x_ready x_squared x_rms rows_ready turned hT_ready logits_done "
                    "logits_ready stored pool_steps passed vec free", ns=True)
        x_loaded = [s.x_loaded0, s.x_loaded1]
        block = ph.block()

        @block.sync
        def _(sp):
            sp.dma_start(o_gain[:], io["g_attn_out_2"][0].partition_broadcast(P)).then_inc(s.gain_loaded, 16)
            sp.dma_start(w[:], io["w_out_2"][0].rearrange("(c p) n -> p c n", p=P)).then_inc(s.w_loaded, 16)
            sp.dma_start(wr[:], rows_by_partition(io["w_router_2"][0])).then_inc(s.wr_loaded, 16)
            with sp.Fori(0, NT // 2) as r:
                for h in range(2):
                    sp.wait_ge(s.stored, 64 * r + 64)
                    sp.dma_start(xt[:, h, :], keep["acc"][bass.ds(r * (2 * P) + h * P, P), :]) \
                        .then_inc(x_loaded[h], 16)
                for h in range(2):
                    sp.wait_ge(s.rows_ready, 2 * r + h + 1)
                    sp.dma_start(keep["rows"][bass.ds(r * (2 * P) + h * P, P), :], hn2[:, h, :]).then_inc(s.stored, 16)
                    sp.dma_start(io["out"][0, bass.ds(r * (2 * P) + h * P, P), :], xt[:, h, :]) \
                        .then_inc(s.stored, 16)
            sp.wait_ge(s.stored, 64 + 32 * NT)

        @block.gpsimd
        def _(pool):
            step = Steps(pool, s.pool_steps)
            pool.sem_inc(s.stored, 64)
            with pool.Fori(0, NT // 2) as r:
                step.enter(r, 4)
                for h in range(2):
                    hold(pool, s.o_summed, 2 * r + h + 1, s.passed)
                    inverse_root(pool, step, st[:, h, 4:8], st[:, h, 0:4], keep["minus_half"]).then_inc(s.o_rms, 1)
                for h in range(2):
                    hold(pool, s.x_squared, 2 * r + h + 1, s.passed)
                    inverse_root(pool, step, st[:, h, 9:10], st[:, h, 8:9], keep["minus_half"]).then_inc(s.x_rms, 1)
                step.leave(NT // 2)

        @block.scalar
        def _(act):
            with act.Fori(0, NT // 2) as r:
                for h in range(2):
                    t = 2 * r + h
                    hold(act, s.free, t + 1, s.passed)
                    act.activation(junk[:, h, 0:AH * DV], tile_of(o, t), ACT.Square, scale=DV ** -0.5) \
                        .then_inc(s.o_squared, 1)
                for h in range(2):
                    t = 2 * r + h
                    act.wait_ge(s.o_turned, t + 1)
                    act.copy(left[:, h, LC:NC, :], tp2[h][:, 0:AH, :]).then_inc(s.left_ready, 1)
                for h in range(2):
                    t = 2 * r + h
                    act.wait_ge(s.x_ready, t + 1)
                    act.activation(junk[:, h, :], xt[:, h, :], ACT.Square, scale=D ** -0.5,
                                   accum_out=st[:, h, 8:9]).then_inc(s.x_squared, 1)
                for h in range(2):
                    t = 2 * r + h
                    act.wait_ge(s.turned, t + 1)
                    act.copy(hT2[:, h, :, :], tp2[h][:]).then_inc(s.hT_ready, 1)

        @block.vector
        def _(dve):
            step = Steps(dve, s.vec)
            dve.sem_inc(s.free, 2)
            dve.wait_ge(s.gain_loaded, 16)
            step.did(dve.tensor_scalar(o_gain[:], o_gain[:], 1.0 - LAM_INIT, None, ALU.mult))
            step.wait()
            with dve.Fori(0, NT // 2) as r:
                step.enter(r, 2 * 3)
                for h in range(2):
                    t = 2 * r + h
                    dve.wait_ge(s.free, t + 1)
                    dve.tensor_scalar(left[:, h, 0:LC, :], yT[:, :, bass.ds(t * P, P)], 1.0, None, ALU.mult) \
                        .then_inc(s.y_taken, 1)
                    dve.wait_ge(s.o_squared, t + 1)
                    dve.tensor_reduce(st[:, h, 0:4], junk[:, h, 0:AH * DV].rearrange("p (g d) -> p g d", d=DV), AX,
                                      ALU.add).then_inc(s.o_summed, 1)
                for h in range(2):
                    t = 2 * r + h
                    dve.wait_ge(s.o_rms, t + 1)
                    step.did(dve.tensor_tensor(on[:, h, :].rearrange("p (g d) -> p g d", d=DV),
                                               tile_of(o, t).rearrange("p (g d) -> p g d", d=DV),
                                               spread(st[:, h, 4:8], DV), ALU.mult))
                    step.wait()
                    dve.tensor_tensor(on[:, h, :].rearrange("p (g d) -> p g d", d=DV),
                                      on[:, h, :].rearrange("p (g d) -> p g d", d=DV), tiled(o_gain[:], AH),
                                      ALU.mult).then_inc(s.o_normed, 1)
                for h in range(2):
                    t = 2 * r + h
                    dve.wait_ge(s.out_done, t + 1)
                    step.did(dve.tensor_tensor(junk[:, h, :], acc2[h][:].rearrange("p a n -> p (a n)"), mod[:, 0, :],
                                               ALU.mult))
                    step.wait()
                    dve.wait_ge(x_loaded[h], 16 * r + 16)
                    dve.tensor_tensor(xt[:, h, :], xt[:, h, :], junk[:, h, :], ALU.add).then_inc(s.x_ready, 1)
                for h in range(2):
                    t = 2 * r + h
                    dve.wait_ge(s.x_rms, t + 1)
                    step.did(dve.scalar_tensor_tensor(hn2[:, h, :], xt[:, h, :], st[:, h, 9:10], mod[:, 2, :],
                                                      ALU.mult, ALU.mult))
                    step.wait()
                    dve.tensor_tensor(hn2[:, h, :], hn2[:, h, :], mod[:, 1, :], ALU.add).then_inc(s.rows_ready, 1)
                for h in range(2):
                    t = 2 * r + h
                    dve.wait_ge(s.logits_done, t + 1)
                    dve.wait_ge(s.stored, 64 + 64 * r)
                    dve.tensor_scalar(tile_of(logits, t), acc2[h][:, 0, 0:E2], 1.0, None,
                                      ALU.mult).then_inc(s.free, 1)
                step.leave(NT // 2)

        @block.tensor
        def _(pe):
            pe.wait_ge(s.w_loaded, 16)
            pe.wait_ge(s.wr_loaded, 16)
            with pe.Fori(0, NT // 2) as r:
                for h in range(2):
                    pe.wait_ge(s.o_normed, 2 * r + h + 1)
                    for c in range(AH):
                        last = pe.transpose(tp2[h][:, c, :], on[:, h, c * DV:(c + 1) * DV], ident)
                    last.then_inc(s.o_turned, 1)
                for h in range(2):
                    pe.wait_ge(s.left_ready, 2 * r + h + 1)
                    pe.wait_ge(s.y_taken, 2 * r + h + 1)
                    for n in range(2):
                        last = product(pe, acc2[h][:, n, :], left[:, h, :, :], w[:, :, n * 512:(n + 1) * 512])
                    last.then_inc(s.out_done, 1)
                for h in range(2):
                    pe.wait_ge(s.rows_ready, 2 * r + h + 1)
                    transpose_tile(pe, tp2[h], hn2[:, h, :], ident).then_inc(s.turned, 1)
                for h in range(2):
                    pe.wait_ge(s.hT_ready, 2 * r + h + 1)
                    product(pe, acc2[h][:, 0, 0:E2], hT2[:, h, :, :], wr).then_inc(s.logits_done, 1)
                pe.wait_ge(s.free, 2 * r + 4)


class ChoiceRouting:

    def __init__(self, keep):
        self.keep = keep

    def buffers(self, ph, o):
        self.o = o
        self.aff = o.gate[:, :, 0:E2]
        self.t = {n: ph.sb(n, [P, NT]) for n in "top total".split()}
        self.w = {n: ph.sb(n, [E2, T]) for n in "affT work above tied count".split()}
        self.one = ph.sb("one_row", [E2, T])
        self.top8 = ph.sb("top8", [E2, 8])
        self.need = ph.sb("need", [E2, 1])
        self.s = ph.sems("shifted exps affinities turned taken chosen slots_turned", ns=True)

    def sync(self, sp):
        pass

    def scalar(self, act):
        act.wait_ge(self.s.shifted, 1)
        act.activation(self.keep["logits2"][:], self.keep["logits2"][:], ACT.Exp).then_inc(self.s.exps, 1)

    def tensor(self, pe):
        ident = self.keep["consts"][:, K_IDENT:K_IDENT + P]
        pe.wait_ge(self.s.affinities, 1)
        for t in range(NT):
            last = pe.transpose(self.o.pa[0:E2, t // 4, t % 4 * P:(t % 4 + 1) * P], self.o.gate[:, t, 0:E2], ident)
        last.then_inc(self.s.turned, 1)
        pe.wait_ge(self.s.chosen, 1)
        for t in range(NT):
            last = pe.transpose(self.o.pb[:, 0, t * E2:(t + 1) * E2], self.w["count"][:, t * P:(t + 1) * P],
                                ident[0:E2, 0:E2])
        last.then_inc(self.s.slots_turned, 1)

    def vector(self, dve, step):
        w, t, o, s = self.w, self.t, self.o, self.s
        logits = self.keep["logits2"][:]

        def do(instruction):
            step.did(instruction)
            step.wait()

        do(dve.memset(self.one[:], 1.0))
        do(dve.tensor_reduce(t["top"][:], logits, AX, ALU.max))
        do(dve.tensor_tensor(logits, logits, spread(t["top"][:], E2), ALU.subtract))
        dve.sem_inc(s.shifted, 1)
        dve.wait_ge(s.exps, 1)
        do(dve.tensor_reduce(t["total"][:], logits, AX, ALU.add))
        do(dve.reciprocal(t["total"][:], t["total"][:]))
        do(dve.tensor_tensor(self.aff, logits, spread(t["total"][:], E2), ALU.mult))
        dve.sem_inc(s.affinities, 1)
        dve.wait_ge(s.turned, 1)
        do(dve.tensor_copy(w["affT"][:], o.pa[0:E2, :, :].rearrange("p a n -> p (a n)")))
        do(dve.tensor_copy(w["work"][:], w["affT"][:]))
        for n in range(CAP // 8):
            do(dve.max(self.top8[:], w["work"][:]))
            if n < CAP // 8 - 1:
                do(dve.match_replace(w["work"][:], self.top8[:], w["work"][:], -1.0))
        least = self.top8[:, 7:8]
        do(dve.tensor_scalar(w["above"][:], w["affT"][:], least, None, ALU.is_gt))
        do(dve.tensor_scalar(w["tied"][:], w["affT"][:], least, None, ALU.is_equal))
        do(dve.tensor_reduce(self.need[:], w["above"][:], AX, ALU.add))
        do(dve.tensor_scalar(self.need[:], self.need[:], -1.0, float(CAP), ALU.mult, ALU.add))
        do(dve.tensor_tensor_scan(w["count"][:], self.one[:], w["tied"][:], 0.0, ALU.mult, ALU.add))
        do(dve.tensor_scalar(w["count"][:], w["count"][:], self.need[:], None, ALU.is_le))
        do(dve.tensor_tensor(w["tied"][:], w["tied"][:], w["count"][:], ALU.mult))
        do(dve.tensor_tensor(w["above"][:], w["above"][:], w["tied"][:], ALU.add))
        do(dve.tensor_tensor_scan(w["count"][:], self.one[:], w["above"][:], -1.0, ALU.mult, ALU.add))
        do(dve.tensor_scalar(w["above"][:], w["above"][:], -FAR, FAR, ALU.mult, ALU.add))
        do(dve.tensor_tensor(w["count"][:], w["count"][:], w["above"][:], ALU.add))
        dve.sem_inc(s.chosen, 1)
        dve.wait_ge(s.slots_turned, 1)
        do(dve.tensor_copy(o.slot_of[:, :, 0:E2], o.pb[:, 0, 0:NT * E2].rearrange("p (t e) -> p t e", e=E2)))


def build(nc, io):
    keep = {}
    with ExitStack() as ctx:
        sb = lambda name, shape, dt=F32: ctx.enter_context(nc.sbuf_tensor(name, shape, dt))
        keep["consts"] = sb("consts", [P, K_ALL])
        keep["minus_half"] = sb("minus_half", [P, 1])[:, :]
        keep["zero"] = sb("zero", [P, 1])[:, :]
        keep["rows"] = nc.dram_tensor("expert_rows", (T, D), F32).ap()
        keep["acc"] = nc.dram_tensor("moe_sums", (T + P, D), F32).ap()
        keep["mod_part"] = nc.dram_tensor("mod_part", (P, MOD), F32).ap()
        keep["logits"] = sb("logits", [P, NT, LOGITS])
        with ExitStack() as first:
            keep["x"] = first.enter_context(nc.sbuf_tensor("x_res", [P, NT, D], F32))
            keep["kmT"] = first.enter_context(nc.sbuf_tensor("kmT", [P, NC, MEM], F32))
            keep["vm"] = first.enter_context(nc.sbuf_tensor("vm", [P, MEM // P, D], F32))
            phase_memory(nc, io, keep)
            phase_mix(nc, io, keep)
            phase_cross(nc, io, keep)
        phase_experts(nc, io, keep, dict(name="moe1", experts=E1, width=F1, rows=keep["rows"], sums=keep["acc"],
                                         w1="w1", w3="w3", w2="w2", out_scale=None, overflow=True,
                                         pick=lambda w, e: w[bass.ds(e, 1), :, :].rearrange("a k n -> (a k) n")),
                      GroupRouting(keep))
        keep["mod"] = sb("mod", [P, 4, D])
        keep["logits2"] = sb("logits2", [P, NT, E2])
        keep["line"] = nc.dram_tensor("bias_line", (AH, P, 512), F32).ap()
        with ExitStack() as second:
            own = lambda name, shape: second.enter_context(nc.sbuf_tensor(name, shape, F32))
            keep["yT"] = own("yT", [P, LC, T])
            with ExitStack() as attended:
                keep["qT"] = attended.enter_context(nc.sbuf_tensor("qT", [P, AH, T], F32))
                keep["kT"] = attended.enter_context(nc.sbuf_tensor("kT", [P, AH, T], F32))
                keep["v"] = attended.enter_context(nc.sbuf_tensor("v", [P, NT, AH * DV], F32))
                with ExitStack() as inner:
                    keep["hT"] = inner.enter_context(nc.sbuf_tensor("hT", [P, NC, T], F32))
                    with ExitStack() as gate:
                        keep["zT"] = gate.enter_context(nc.sbuf_tensor("zT", [P, LC, T], F32))
                        phase_second_norm(nc, io, keep)
                        phase_lru(nc, io, keep)
                    phase_qkv(nc, io, keep)
                keep["o"] = attended.enter_context(nc.sbuf_tensor("o", [P, NT, AH * DV], F32))
                phase_attention(nc, io, keep)
                phase_second_out(nc, io, keep)
        phase_experts(nc, io, keep, dict(name="moe2", experts=E2, width=F2, rows=keep["rows"], sums=io["out"][0],
                                         w1="w1_2", w3="w3_2", w2="w2_2", out_scale=keep["mod"][:, 3, :],
                                         overflow=False,
                                         pick=lambda w, e: w[0][bass.ds(e, 1), :, :].rearrange("a k n -> (a k) n")),
                      ChoiceRouting(keep))


INPUTS = ["x", "mem", "norm_mix", "w_in", "q_norm", "k_norm", "attn_sinks", "sgu_norm", "sgu_w", "sgu_b",
          "out_norm_attn", "out_norm_sgu", "w_out", "norm_cross", "norm_mem", "w_cq", "w_ck", "w_cv", "cq_norm",
          "ck_norm", "w_co", "norm_ffn", "w_router_group", "w_router_expert", "w1", "w3", "w2", "c_2", "w_mod_2",
          "b_mod_2", "g_norm1_2", "w_in_2", "conv_w_2", "conv_b_2", "lru_w_a_2", "lru_b_a_2", "lru_w_x_2",
          "lru_b_x_2", "lru_lambda_2", "g_q_2", "g_k_2", "lambda_qk_2", "g_attn_out_2", "rel_bias_2", "w_out_2",
          "g_norm2_2", "w_router_2", "w1_2", "w3_2", "w2_2"]


def kernel(**inputs):
    from concourse import bacc
    from concourse.bass_utils import run_bass_kernel_spmd

    nc = bacc.Bacc("TRN2", target_bir_lowering=False, num_devices=1)
    arrays, io = {}, {}
    for name in INPUTS:
        a = np.ascontiguousarray(inputs[name])
        arrays[f"in_{name}"] = a
        io[name] = nc.dram_tensor(f"in_{name}", a.shape, mybir.dt.from_np(a.dtype), kind="ExternalInput").ap()
    arrays["in_consts"] = constants()
    io["consts"] = nc.dram_tensor("in_consts", (P, K_ALL), F32, kind="ExternalInput").ap()
    io["out"] = nc.dram_tensor("out", (1, T, D), F32, kind="ExternalOutput").ap()
    build(nc, io)
    r = run_bass_kernel_spmd(nc, [arrays], core_ids=[0])
    return r.results[0]["out"]
```

```python
from collections import namedtuple
from contextlib import ExitStack

import numpy as np

import concourse.bass as bass
from concourse import mybir

F32 = mybir.dt.float32
I32 = mybir.dt.int32
ALU = mybir.AluOpType
ACT = mybir.ActivationFunctionType
AX = mybir.AxisListType.X

P = 128
T = 1024
NT = T // P
D = 1024
NC = D // P
EPS = 1e-6
MASKED = -1e30

HD = 64
QH = 8
KVH = 2
REP = QH // KVH
ATT = QH * HD
SG = 512
GRP = 8
MEM = 256
XH = 4
XD = D // XH
G1 = 4
E1 = 32
PER_G = E1 // G1
F1 = 512
MAX_OVER = 2 * T // P - 1

LRU = 512
LC = LRU // P
AH = 4
DK = 64
DV = 128
E2 = 16
F2 = 1024
CAP = 2 * T // E2
LAM_INIT = 0.8 - 0.6
BUCKETS = 32
BUCKET_FROM = [0, 1, 2, 3, 4, 5, 6, 7, 8, 12, 16, 23, 32, 46, 64, 91]

K_IDENT = 0
K_BEFORE = 128
K_IOTA = 256
K_UPTO = 384
K_ODD = 512
K_EVEN = 768
K_TOKEN = K_EVEN + 2 * 256
K_SPARE = K_TOKEN + 8
K_REV32 = K_SPARE + 2
K_BUCKET = K_REV32 + 32
K_ALL = K_BUCKET + 512


def constants():
    k = np.zeros((P, K_ALL), np.float32)
    p = np.arange(P)[:, None]
    c = np.arange(P)[None, :]
    k[:, K_IDENT:K_IDENT + P] = p == c
    k[:, K_BEFORE:K_BEFORE + P] = p < c
    k[:, K_IOTA:K_IOTA + P] = c
    k[:, K_UPTO:K_UPTO + P] = p <= c
    own = np.where(c <= p, 0.0, MASKED)
    previous = np.where(c > p, 0.0, MASKED)
    k[:, K_ODD:K_ODD + 256] = np.concatenate([previous, own], 1)
    for n in range(2):
        k[:, K_EVEN + 256 * n:K_EVEN + 256 * n + 256] = np.concatenate(
            [own, previous if n else np.full((P, P), MASKED)], 1)
    k[:, K_TOKEN:K_TOKEN + NT] = p + P * np.arange(NT)[None, :]
    k[:, K_SPARE] = T + np.arange(P)
    k[:, K_SPARE + 1] = -(T + np.arange(P))
    k[:, K_REV32:K_REV32 + 32] = 32 - np.arange(32)[None, :]
    for m in range(511):
        away = m - 255
        n = max(b for b in range(16) if BUCKET_FROM[b] <= abs(away))
        k[n + (16 if away > 0 else 0), K_BUCKET + m] = 1.0
    return k


class Steps:

    def __init__(self, eng, sem):
        self.eng, self.sem, self.base, self.n, self.round = eng, sem, 0, 0, None

    def did(self, instruction):
        instruction.then_inc(self.sem, 1)
        self.n += 1

    def wait(self, n=None):
        n = self.n if n is None else n
        value = self.base + n if self.round is None else self.round + (self.base + n)
        self.eng.wait_ge(self.sem, value)

    def enter(self, i, per):
        self.base, self.n, self.per, self.round = self.base + self.n, 0, per, i * per

    def leave(self, rounds):
        assert self.n == self.per, ("steps in a round", self.n)
        self.base, self.n, self.round = self.base + self.per * rounds, 0, None


class Phase:

    def __init__(self, nc, name):
        self.nc, self.name, self.ctx, self.used = nc, name, ExitStack(), []

    def __enter__(self):
        self.ctx.__enter__()
        return self

    def __exit__(self, *failed):
        self.ctx.__exit__(*failed)
        if failed[0] is None:
            self.nc.clear_and_free_semaphores(self.used)
            self.nc.all_engine_barrier()

    def sb(self, name, shape, dt=F32):
        return self.ctx.enter_context(self.nc.sbuf_tensor(f"{self.name}_{name}", shape, dt))

    def ps(self, name, shape):
        return self.ctx.enter_context(self.nc.psum_tensor(f"{self.name}_{name}", shape, F32))

    def sems(self, names, ns=False, prefix=""):
        names = names.split()
        found = [self.nc.alloc_semaphore(f"{self.name}_{prefix}{n}") for n in names]
        self.used += found
        return namedtuple("Semaphores", names)(*found) if ns else found

    def block(self):
        return self.ctx.enter_context(self.nc.Block())


def rows_by_partition(w, rows_each=NC):
    return w.rearrange("(p c) n -> p c n", c=rows_each)


def spread(ap, n):
    return ap.unsqueeze(2).broadcast_to([ap.shape[0], ap.shape[1], n])


def tiled(ap, n):
    return ap.unsqueeze(1).broadcast_to([ap.shape[0], n, ap.shape[1]])


def tile_of(x, t):
    return x[:, bass.ds(t, 1), :].rearrange("p a d -> p (a d)")


def strided(x):
    return x.rearrange("p (d c) -> p c d", c=NC)


def transpose_tile(pe, out, src, ident):
    for c in range(NC):
        last = pe.transpose(out[:, c, :], strided(src)[:, c, :], ident)
    return last


def product(pe, out, left, right, chunks=NC):
    for c in range(chunks):
        last = pe.matmul(out, left[:, c, :], right[:, c, :], start=(c == 0), stop=(c == chunks - 1))
    return last


def hold(eng, sem, value, passed):
    eng.wait_ge(sem, value)
    eng.sem_inc(passed, 1)


def inverse_root(pool, step, out, mean, minus_half):
    step.did(pool.tensor_scalar(mean, mean, EPS, None, ALU.add))
    step.wait()
    return pool.tensor_tensor(out, mean, minus_half.broadcast_to([P, mean.shape[1]]), ALU.pow)


def all_tiles(eng, tile, step=None, steps=0):
    tile(0, 0)
    with eng.Fori(0, NT // 2 - 1) as r:
        if step:
            step.enter(r, 2 * steps)
        for n in (1, 2):
            tile(r * 2 + n, n % 2)
        if step:
            step.leave(NT // 2 - 1)
    tile(NT - 1, 1)


def is_first(t):
    return isinstance(t, int) and t == 0


def is_last(t):
    return isinstance(t, int) and t == NT - 1


def phase_memory(nc, io, keep):
    kmT, vm, ks = keep["kmT"], keep["vm"], keep["consts"]
    ident = ks[:, K_IDENT:K_IDENT + P]
    MT = MEM // P
    with Phase(nc, "mem") as ph:
        mem = ph.sb("mem", [P, MT, D])
        gain = ph.sb("gain", [P, D])
        xgain = ph.sb("xgain", [P, 2, XD])
        gg = ph.sb("gg", [P, XD])
        wk = ph.sb("wk", [P, NC, D])
        wv = ph.sb("wv", [P, NC, D])
        junk = ph.sb("junk", [P, D])
        normed = ph.sb("normed", [P, MT, D])
        mT = ph.sb("mT", [P, NC, MEM])
        kn = ph.sb("kn", [P, MT, D])
        stat = ph.sb("stat", [P, 4 * MT + 2 * XH * MT])
        tp = ph.ps("tp", [P, NC, P])
        kv = ph.ps("kv", [P, 2, 2, 512])
        (loaded, wk_loaded, wv_loaded, squared, rms, mem_normed, turned, mT_ready, k_done, v_done,
         k_squared, k_rms, k_normed, k_turned, vec, kept, pool_steps, x_loaded) = ph.sems(
            "loaded wk_loaded wv_loaded squared rms mem_normed turned mT_ready k_done v_done "
            "k_squared k_rms k_normed k_turned vec kept pool_steps x_loaded")
        ms = stat[:, 0:MT]
        rstd = stat[:, MT:2 * MT]
        kms = stat[:, 8:8 + XH * MT]
        krstd = stat[:, 8 + XH * MT:8 + 2 * XH * MT]
        block = ph.block()

        @block.sync
        def _(sp):
            sp.dma_start(mem[:], io["mem"].rearrange("a (t p) d -> p (a t) d", p=P)).then_inc(loaded, 16)
            sp.dma_start(ks[:], io["consts"]).then_inc(loaded, 16)
            sp.dma_start(gain[:], io["norm_mem"].partition_broadcast(P)).then_inc(loaded, 16)
            sp.dma_start(xgain[:, 0, :], io["cq_norm"].partition_broadcast(P)).then_inc(loaded, 16)
            sp.dma_start(xgain[:, 1, :], io["ck_norm"].partition_broadcast(P)).then_inc(loaded, 16)
            sp.dma_start(wk[:], rows_by_partition(io["w_ck"])).then_inc(wk_loaded, 16)
            sp.dma_start(wv[:], rows_by_partition(io["w_cv"])).then_inc(wv_loaded, 16)
            sp.dma_start(keep["x"][:], io["x"].rearrange("a (t p) d -> p (a t) d", p=P)).then_inc(x_loaded, 16)
            sp.wait_ge(x_loaded, 16)

        @block.scalar
        def _(act):
            act.wait_ge(loaded, 16 * 5)
            for t in range(MT):
                act.activation(junk[:], mem[:, t, :], ACT.Square, scale=D ** -0.5,
                               accum_out=ms[:, t:t + 1]).then_inc(squared, 1)
                act.wait_ge(squared, t + 1)
            for t in range(MT):
                act.wait_ge(turned, t + 1)
                act.copy(mT[:, :, t * P:(t + 1) * P], tp[:]).then_inc(mT_ready, 1)
            for t in range(MT):
                act.wait_ge(k_done, t + 1)
                for h in range(XH):
                    act.activation(junk[:, h * XD:(h + 1) * XD], kv[:, t, h // 2, (h % 2) * XD:(h % 2 + 1) * XD],
                                   ACT.Square, scale=XD ** -0.5,
                                   accum_out=kms[:, t * XH + h:t * XH + h + 1]).then_inc(k_squared, 1)
                    act.wait_ge(k_squared, XH * t + h + 1)
            for t in range(MT):
                act.wait_ge(k_turned, t + 1)
                act.copy(kmT[:, :, t * P:(t + 1) * P], tp[:]).then_inc(kept, 1)
            for t in range(MT):
                act.wait_ge(v_done, t + 1)
                act.copy(vm[:, t, :], kv[:, t, :, :].rearrange("p a n -> p (a n)")).then_inc(kept, 1)
            act.wait_ge(kept, 2 * MT)

        @block.gpsimd
        def _(pool):
            step = Steps(pool, pool_steps)
            half = keep["minus_half"]
            step.did(pool.memset(half, -0.5))
            step.did(pool.memset(keep["zero"], 0.0))
            for t in range(MT):
                pool.wait_ge(squared, t + 1)
                inverse_root(pool, step, rstd[:, t:t + 1], ms[:, t:t + 1], half).then_inc(rms, 1)
            for t in range(MT):
                pool.wait_ge(k_squared, XH * (t + 1))
                inverse_root(pool, step, krstd[:, XH * t:XH * t + XH],
                             kms[:, XH * t:XH * t + XH], half).then_inc(k_rms, 1)

        @block.vector
        def _(dve):
            step = Steps(dve, vec)
            dve.wait_ge(loaded, 16 * 5)
            dve.scalar_tensor_tensor(gg[:], xgain[:, 0, :], XD ** -0.5, xgain[:, 1, :], ALU.mult, ALU.mult) \
                .then_inc(vec, 1)
            step.n = 1
            for t in range(MT):
                dve.wait_ge(rms, t + 1)
                dve.scalar_tensor_tensor(normed[:, t, :], mem[:, t, :], rstd[:, t:t + 1], gain[:], ALU.mult,
                                         ALU.mult).then_inc(mem_normed, 1)
            for t in range(MT):
                dve.wait_ge(k_rms, t + 1)
                step.did(dve.tensor_tensor(kn[:, t, :].rearrange("p (h d) -> p h d", h=XH),
                                           kv[:, t, :, :].rearrange("p a (h d) -> p (a h) d", d=XD),
                                           spread(krstd[:, XH * t:XH * t + XH], XD), ALU.mult))
                step.wait()
                dve.tensor_tensor(kn[:, t, :].rearrange("p (h d) -> p h d", h=XH),
                                  kn[:, t, :].rearrange("p (h d) -> p h d", h=XH), tiled(gg[:], XH),
                                  ALU.mult).then_inc(k_normed, 1)

        @block.tensor
        def _(pe):
            pe.wait_ge(loaded, 16 * 5)
            for t in range(MT):
                pe.wait_ge(mem_normed, t + 1)
                if t:
                    pe.wait_ge(mT_ready, t)
                transpose_tile(pe, tp, normed[:, t, :], ident).then_inc(turned, 1)
            pe.wait_ge(mT_ready, MT)
            pe.wait_ge(wk_loaded, 16)
            for t in range(MT):
                for n in range(2):
                    last = product(pe, kv[:, t, n, :], mT[:, :, t * P:(t + 1) * P], wk[:, :, n * 512:(n + 1) * 512])
                last.then_inc(k_done, 1)
            for t in range(MT):
                pe.wait_ge(k_normed, t + 1)
                if t:
                    pe.wait_ge(kept, t)
                for c in range(NC):
                    last = pe.transpose(tp[:, c, :], kn[:, t, c * P:(c + 1) * P], ident)
                last.then_inc(k_turned, 1)
            pe.wait_ge(wv_loaded, 16)
            for t in range(MT):
                for n in range(2):
                    last = product(pe, kv[:, t, n, :], mT[:, :, t * P:(t + 1) * P], wv[:, :, n * 512:(n + 1) * 512])
                last.then_inc(v_done, 1)


IN_W = ATT + 2 * KVH * HD + 2 * SG


def phase_mix(nc, io, keep):
    x, ks = keep["x"], keep["consts"]
    ident = ks[:, K_IDENT:K_IDENT + P]
    NQK = QH + KVH
    KV = KVH * HD
    with Phase(nc, "mix") as ph:
        w_in = ph.sb("w_in", [P, NC, IN_W])
        w_out = ph.sb("w_out", [P, NC, D])
        gain = ph.sb("gain", [P, D])
        out_gain = ph.sb("out_gain", [P, D])
        sgu_gain = ph.sb("sgu_gain", [P, SG])
        qk_gain = ph.sb("qk_gain", [P, 2])
        qk = ph.sb("qk", [P, 1])
        sinks = ph.sb("sinks", [P, QH])
        brow = ph.sb("brow", [GRP, P])
        bcol = ph.sb("bcol", [P, GRP])
        wT = ph.sb("wT", [P, GRP, P])
        junk = ph.sb("junk", [P, D])
        hn = ph.sb("hn", [P, D])
        hT = ph.sb("hT", [P, NC, P])
        mx = ph.sb("mx", [P, D])
        mT = ph.sb("mT", [P, NC, P])
        qn = ph.sb("qn", [P, ATT])
        kn = ph.sb("kn", [P, KV])
        v = ph.sb("v", [P, 2, KV])
        u = ph.sb("u", [P, SG])
        g = ph.sb("g", [P, SG])
        qT = ph.sb("qT", [P, REP, P])
        kT = ph.sb("kT", [P, 2, P])
        pr = ph.sb("pr", [P, QH, 2 * P])
        pT = ph.sb("pT", [P, QH * 2, P])
        wraw = pT[:, 0:GRP, :]
        ss = ph.sb("ss", [P, NQK])
        rqk = ph.sb("rqk", [P, NQK])
        st = ph.sb("st", [P, 64])
        ms, rstd, gms, grstd, ams, arstd, sms, srstd = (st[:, n:n + 1] for n in range(8))
        top, ntop, total, esink, den, rden = (st[:, 8 + 8 * n:16 + 8 * n] for n in range(6))
        w0, w1, w2, w3 = (ph.ps(f"w{n}", [P, 2, 512]) for n in range(4))
        chunks = lambda w: w[:].rearrange("p a (c n) -> p (a c) n", n=P)
        PQ, PKV, PU, PG = w1[:, 0, :], w1[:, 1, 0:2 * KV], w2[:, 0, :], w2[:, 1, :]
        halves = (w3, w1)
        scores = [w[:].rearrange("p a (h k) -> p (a h) k", k=2 * P) for w in halves]
        s = ph.sems("loaded w_in_loaded w_out_loaded spatial_turned spatial_ready squared rms normed turned "
                    "hT_ready q_projected g_projected u_projected qk_squared qk_summed qk_rms qk_normed v_ready gelus g_squared "
                    "g_rms gate_in qk_turned q_ready k_ready scored top_ready exps p_turned p_ready0 p_ready1 attended "
                    "att_ready att_squared gated gated_ready sg_squared mix_rms mixed mix_turned mT_ready out_done "
                    "x_done vec pool_steps passed", ns=True)
        block = ph.block()

        @block.sync
        def _(sp):
            def one(dst, src):
                sp.dma_start(dst, src).then_inc(s.loaded, 16)
            one(gain[:], io["norm_mix"].partition_broadcast(P))
            one(out_gain[:, 0:ATT], io["out_norm_attn"].partition_broadcast(P))
            one(out_gain[:, ATT:D], io["out_norm_sgu"].partition_broadcast(P))
            one(sgu_gain[:], io["sgu_norm"].partition_broadcast(P))
            one(sinks[:], io["attn_sinks"].partition_broadcast(P))
            for r in range(2):
                one(qk_gain[r * HD:(r + 1) * HD, 0:1], io["q_norm"].rearrange("(p o) -> p o", o=1))
                one(qk_gain[r * HD:(r + 1) * HD, 1:2], io["k_norm"].rearrange("(p o) -> p o", o=1))
            one(brow[:], io["sgu_b"])
            one(wraw, io["sgu_w"].rearrange("g i j -> i g j"))
            sp.dma_start(w_in[:], rows_by_partition(io["w_in"])).then_inc(s.w_in_loaded, 16)
            sp.dma_start(w_out[:], rows_by_partition(io["w_out"])).then_inc(s.w_out_loaded, 16)

        @block.scalar
        def _(act):
            def square_x(t):
                act.activation(junk[:], tile_of(x, t), ACT.Square, scale=D ** -0.5, accum_out=ms) \
                    .then_inc(s.squared, 1)

            def keep_input(t):
                act.wait_ge(s.turned, t + 1)
                act.copy(hT[:], chunks(w2)).then_inc(s.hT_ready, 1)

            def square_qk(t):
                act.wait_ge(s.q_projected, t + 1)
                act.activation(junk[:, 0:ATT], PQ, ACT.Square, scale=HD ** -0.5)
                act.activation(junk[:, ATT:ATT + KV], PKV[:, 0:KV], ACT.Square,
                               scale=HD ** -0.5).then_inc(s.qk_squared, 1)

            def tile(t, half):
                act.wait_ge(s.g_projected, t + 1)
                act.activation(g[:], PG, ACT.Gelu_apprx_tanh).then_inc(s.gelus, 1)
                act.wait_ge(s.gelus, t * 2 + 1)
                act.wait_ge(s.qk_summed, t + 1)
                act.activation(junk[:, 0:SG], g[:], ACT.Square, scale=SG ** -0.5,
                               accum_out=gms).then_inc(s.g_squared, 1)
                act.wait_ge(s.qk_turned, t + 1)
                act.copy(qT[:], w0[:, 0, :].rearrange("p (a n) -> p a n", n=P)).then_inc(s.q_ready, 1)
                act.wait_ge(s.u_projected, t + 1)
                act.activation(u[:], PU, ACT.Gelu_apprx_tanh).then_inc(s.gelus, 1)
                act.wait_ge(s.g_squared, t + 1)
                if not is_last(t):
                    square_x(t + 1)
                act.wait_ge(s.top_ready, t + 1)
                for h in range(QH):
                    act.activation(pr[:, h, :], pr[:, h, :], ACT.Exp, bias=ntop[:, h:h + 1],
                                   accum_out=total[:, h:h + 1])
                act.activation(esink, esink, ACT.Exp).then_inc(s.exps, 1)
                act.wait_ge(s.gated_ready, t + 1)
                act.wait_ge(s.squared, NT if is_last(t) else t + 2)
                act.activation(junk[:, ATT:D], mx[:, ATT:D], ACT.Square, scale=SG ** -0.5,
                               accum_out=sms).then_inc(s.sg_squared, 1)
                act.wait_ge(s.p_turned, t * 2 + 1)
                act.copy(pT[:, 0:QH, :], chunks(w3)).then_inc(s.p_ready0, 1)
                if not is_last(t):
                    keep_input(t + 1)
                act.wait_ge(s.att_ready, t + 1)
                act.activation(junk[:, 0:ATT], mx[:, 0:ATT], ACT.Square, scale=ATT ** -0.5,
                               accum_out=ams).then_inc(s.att_squared, 1)
                act.wait_ge(s.att_squared, t + 1)
                act.wait_ge(s.sg_squared, t + 1)
                if not is_last(t):
                    square_qk(t + 1)
                act.wait_ge(s.mix_turned, t + 1)
                act.copy(mT[:], chunks(w3)).then_inc(s.mT_ready, 1)

            act.wait_ge(s.loaded, 16 * 11)
            square_x(0)
            act.wait_ge(s.squared, 1)
            keep_input(0)
            square_qk(0)
            all_tiles(act, tile)

        @block.gpsimd
        def _(pool):
            step = Steps(pool, s.pool_steps)
            mh = keep["minus_half"]

            def tile(t, half):
                hold(pool, s.qk_summed, t + 1, s.passed)
                inverse_root(pool, step, rqk[:], ss[:], mh).then_inc(s.qk_rms, 1)
                hold(pool, s.g_squared, t + 1, s.passed)
                inverse_root(pool, step, grstd, gms, mh).then_inc(s.g_rms, 1)
                if not is_last(t):
                    hold(pool, s.squared, t + 2, s.passed)
                    inverse_root(pool, step, rstd, ms, mh).then_inc(s.rms, 1)
                hold(pool, s.sg_squared, t + 1, s.passed)
                inverse_root(pool, step, srstd, sms, mh).then_inc(s.mix_rms, 1)
                hold(pool, s.att_squared, t + 1, s.passed)
                inverse_root(pool, step, arstd, ams, mh).then_inc(s.mix_rms, 1)

            hold(pool, s.squared, 1, s.passed)
            inverse_root(pool, step, rstd, ms, mh).then_inc(s.rms, 1)
            all_tiles(pool, tile, step, 5)

        @block.vector
        def _(dve):
            step = Steps(dve, s.vec)

            def norm_input(t):
                dve.wait_ge(s.rms, t + 1)
                dve.scalar_tensor_tensor(hn[:], tile_of(x, t), rstd, gain[:], ALU.mult, ALU.mult) \
                    .then_inc(s.normed, 1)

            def add_output(t):
                dve.wait_ge(s.out_done, t + 1)
                dve.tensor_tensor(tile_of(x, t), w2[:].rearrange("p a n -> p (a n)"), tile_of(x, t),
                                  ALU.add).then_inc(s.x_done, 1)

            def tile(t, half):
                dve.wait_ge(s.qk_squared, t + 1)
                dve.tensor_reduce(ss[:], junk[:, 0:ATT + KV].rearrange("p (h d) -> p h d", d=HD), AX,
                                  ALU.add).then_inc(s.qk_summed, 1)
                dve.wait_ge(s.qk_rms, t + 1)
                dve.tensor_tensor(qn[:].rearrange("p (a k d) -> p k a d", k=KVH, d=HD),
                                  PQ.rearrange("p (k a d) -> p k a d", k=KVH, d=HD),
                                  rqk[:, 0:QH].rearrange("p (k a) -> p k a", k=KVH).unsqueeze(3)
                                  .broadcast_to([P, KVH, REP, HD]), ALU.mult)
                dve.tensor_tensor(kn[:].rearrange("p (h d) -> p h d", d=HD),
                                  PKV[:, 0:KV].rearrange("p (h d) -> p h d", d=HD),
                                  spread(rqk[:, QH:NQK], HD), ALU.mult).then_inc(s.qk_normed, 1)
                dve.tensor_copy(v[:, half, :], PKV[:, KV:2 * KV]).then_inc(s.v_ready, 1)
                dve.wait_ge(s.qk_turned, t + 1)
                dve.tensor_scalar(kT[:, half, :], w0[:, 1, 0:P], qk[:], None, ALU.mult).then_inc(s.k_ready, 1)
                dve.wait_ge(s.g_rms, t + 1)
                dve.scalar_tensor_tensor(g[:], g[:], grstd, sgu_gain[:], ALU.mult, ALU.mult).then_inc(s.gate_in, 1)
                dve.wait_ge(s.scored, t + 1)
                mask = K_ODD if half else K_EVEN if is_first(t) else K_EVEN + 2 * P
                for n in range(2):
                    step.did(dve.tensor_tensor(pr[:, n * REP:(n + 1) * REP, :], scores[n],
                                               tiled(ks[:, mask:mask + 2 * P], REP), ALU.add))
                step.wait()
                step.did(dve.tensor_reduce(top, pr[:], AX, ALU.max))
                step.wait()
                step.did(dve.tensor_tensor(top, top, sinks[:], ALU.max))
                step.wait()
                step.did(dve.tensor_tensor(esink, sinks[:], top, ALU.subtract))
                dve.tensor_scalar(ntop, top, -1.0, None, ALU.mult).then_inc(s.top_ready, 1)
                dve.wait_ge(s.gated, t + 1)
                step.did(dve.tensor_tensor(mx[:, ATT:D].rearrange("p (h d) -> p h d", h=GRP),
                                           w0[:, 1, :].rearrange("p (h d) -> p h d", h=GRP),
                                           spread(bcol[:], SG // GRP), ALU.add))
                step.wait()
                dve.wait_ge(s.gelus, t * 2 + 2)
                dve.tensor_tensor(mx[:, ATT:D], mx[:, ATT:D], u[:], ALU.mult).then_inc(s.gated_ready, 1)
                if not is_last(t):
                    norm_input(t + 1)
                dve.wait_ge(s.exps, t + 1)
                step.did(dve.tensor_tensor(den, total, esink, ALU.add))
                step.wait()
                step.did(dve.reciprocal(rden, den))
                if not is_first(t):
                    add_output(t - 1)
                dve.wait_ge(s.p_turned, t * 2 + 2)
                dve.tensor_copy(pT[:, QH:2 * QH, :], chunks(w1)).then_inc(s.p_ready1, 1)
                step.wait()
                dve.wait_ge(s.attended, t + 1)
                dve.tensor_tensor(mx[:, 0:ATT].rearrange("p (h d) -> p h d", d=HD),
                                  w0[:, 0, :].rearrange("p (h d) -> p h d", d=HD), spread(rden, HD),
                                  ALU.mult).then_inc(s.att_ready, 1)
                dve.wait_ge(s.mix_rms, t * 2 + 2)
                dve.scalar_tensor_tensor(mx[:, 0:ATT], mx[:, 0:ATT], arstd, out_gain[:, 0:ATT], ALU.mult, ALU.mult)
                dve.scalar_tensor_tensor(mx[:, ATT:D], mx[:, ATT:D], srstd, out_gain[:, ATT:D], ALU.mult,
                                         ALU.mult).then_inc(s.mixed, 1)

            dve.wait_ge(s.loaded, 16 * 11)
            step.did(dve.memset(kT[:], 0.0))
            step.did(dve.memset(v[:], 0.0))
            step.did(dve.scalar_tensor_tensor(qk[:], qk_gain[:, 0:1], HD ** -0.5, qk_gain[:, 1:2], ALU.mult,
                                              ALU.mult))
            dve.wait_ge(s.spatial_turned, 1)
            step.did(dve.tensor_tensor(wT[:], chunks(w3), tiled(ks[:, K_UPTO:K_UPTO + P], GRP), ALU.mult))
            step.did(dve.tensor_copy(bcol[:], w0[:, 0, 0:GRP]))
            step.wait()
            dve.sem_inc(s.spatial_ready, 1)
            norm_input(0)
            all_tiles(dve, tile, step, 8)
            add_output(NT - 1)

        @block.tensor
        def _(pe):
            def project(t):
                pe.wait_ge(s.hT_ready, t + 1)
                product(pe, PQ, hT, w_in[:, :, 0:ATT])
                product(pe, PKV, hT, w_in[:, :, ATT:ATT + 2 * KV]).then_inc(s.q_projected, 1)

            def output(t):
                for n in range(2):
                    last = product(pe, w2[:, n, :], mT, w_out[:, :, n * 512:(n + 1) * 512])
                last.then_inc(s.out_done, 1)

            def tile(t, half):
                product(pe, PG, hT, w_in[:, :, ATT + 2 * KV + SG:IN_W]).then_inc(s.g_projected, 1)
                pe.wait_ge(s.qk_normed, t + 1)
                for a in range(REP):
                    pe.transpose(w0[:, 0, a * P:(a + 1) * P], qn[:, a * P:(a + 1) * P], ident)
                pe.transpose(w0[:, 1, 0:P], kn[:], ident).then_inc(s.qk_turned, 1)
                product(pe, PU, hT, w_in[:, :, ATT + 2 * KV:ATT + 2 * KV + SG]).then_inc(s.u_projected, 1)
                if not is_first(t):
                    pe.wait_ge(s.mT_ready, t)
                pe.wait_ge(s.q_ready, t + 1)
                pe.wait_ge(s.k_ready, t + 1)
                pe.wait_ge(s.v_ready, t + 1)
                for h in range(QH):
                    a = h // REP * HD
                    last = pe.matmul(scores[h // REP][:, h % REP, :], qT[a:a + HD, h % REP, :],
                                     kT[a:a + HD, :, :].rearrange("p a n -> p (a n)"), start=True, stop=True)
                last.then_inc(s.scored, 1)
                pe.wait_ge(s.gate_in, t + 1)
                for n in range(GRP):
                    w = SG // GRP
                    last = pe.matmul(w0[:, 1, n * w:(n + 1) * w], wT[:, n, :], g[:, n * w:(n + 1) * w],
                                     start=True, stop=True)
                last.then_inc(s.gated, 1)
                pe.wait_ge(s.gelus, t * 2 + 2)
                if not is_first(t):
                    output(t - 1)
                pe.wait_ge(s.exps, t + 1)
                for h in range(QH):
                    for b in range(2):
                        last = pe.transpose(chunks(halves[h // REP])[:, 2 * (h % REP) + b, :],
                                            pr[:, h, b * P:(b + 1) * P], ident)
                    if h % REP == REP - 1:
                        last.then_inc(s.p_turned, 1)
                if not is_last(t):
                    pe.wait_ge(s.normed, t + 2)
                    if not is_first(t):
                        pe.wait_ge(s.x_done, t)
                    transpose_tile(pe, chunks(w2), hn[:], ident).then_inc(s.turned, 1)
                for h in range(QH):
                    if h % REP == 0:
                        pe.wait_ge((s.p_ready0, s.p_ready1)[h // REP], t + 1)
                    for b in range(2):
                        last = pe.matmul(w0[:, 0, h * HD:(h + 1) * HD], pT[:, 2 * h + b, :],
                                         v[:, b, h // REP * HD:(h // REP + 1) * HD], start=(b == 0),
                                         stop=(b == 1))
                last.then_inc(s.attended, 1)
                if not is_last(t):
                    project(t + 1)
                pe.wait_ge(s.mixed, t + 1)
                transpose_tile(pe, chunks(w3), mx[:], ident).then_inc(s.mix_turned, 1)

            pe.wait_ge(s.loaded, 16 * 11)
            for n in range(GRP):
                pe.transpose(chunks(w3)[:, n, :], wraw[:, n, :], ident)
            pe.transpose(w0[:, 0, 0:GRP], brow[:], ident[0:GRP, 0:GRP]).then_inc(s.spatial_turned, 1)
            pe.wait_ge(s.spatial_ready, 1)
            pe.wait_ge(s.normed, 1)
            transpose_tile(pe, chunks(w2), hn[:], ident).then_inc(s.turned, 1)
            pe.wait_ge(s.w_in_loaded, 16)
            project(0)
            pe.wait_ge(s.w_out_loaded, 16)
            all_tiles(pe, tile)
            pe.wait_ge(s.mT_ready, NT)
            output(NT - 1)


MOD = 6 * D
PIECE = MOD // NT
LOGITS = G1 + E1


def phase_cross(nc, io, keep):
    x, ks, kmT, vm, logits = keep["x"], keep["consts"], keep["kmT"], keep["vm"], keep["logits"]
    ident = ks[:, K_IDENT:K_IDENT + P]
    with Phase(nc, "cross") as ph:
        wq = ph.sb("wq", [P, NC, D])
        wo = ph.sb("wo", [P, NC, D])
        wr = ph.sb("wr", [P, NC, LOGITS])
        gain = ph.sb("gain", [P, D])
        ffn_gain = ph.sb("ffn_gain", [P, D])
        junk = ph.sb("junk", [P, D])
        qjunk = ph.sb("qjunk", [P, D])
        hn = ph.sb("hn", [P, D])
        qn = ph.sb("qn", [P, D])
        on = ph.sb("on", [P, D])
        rows = ph.sb("rows", [P, D])
        pr = ph.sb("pr", [P, D])
        hT = ph.sb("hT", [P, NC, P])
        poT = ph.sb("poT", [P, NC, P])
        qbT = ph.sb("qbT", [P, NC, P])
        st = ph.sb("st", [P, 64])
        csilu = ph.sb("csilu", [P, NC])
        pieces = ph.sb("pieces", [P, 4, PIECE])
        sums = ph.sb("sums", [P, 2, PIECE])
        wa, wb, wc, wd = (ph.ps(f"w{n}", [P, 2, 512]) for n in "abcd")
        chunks = lambda w: w[:].rearrange("p a (c n) -> p (a c) n", n=P)
        heads = lambda w: w[:].rearrange("p a (h n) -> p (a h) n", n=XD)
        s = ph.sems("loaded wq_loaded wo_loaded wr_loaded squared rms normed turned hT_ready q_done q_squared q_rms "
                    "q_normed q_turned qT_ready scored top_ready exps p_turned pT_ready attended o_ready o_turned "
                    "oT_ready0 oT_ready1 out_done x_done b_squared b_rms rows_ready b_turned bT_ready logits_done "
                    "logits_ready stored vec pool_steps passed piece_loaded0 piece_loaded1 piece_loaded2 "
                    "piece_loaded3 piece_free sums_ready sums_stored0 sums_stored1 silu_ready", ns=True)
        piece_loaded = [s.piece_loaded0, s.piece_loaded1, s.piece_loaded2, s.piece_loaded3]
        sums_stored = [s.sums_stored0, s.sums_stored1]
        ms, rstd, bms, brstd = (st[:, n:n + 1] for n in range(4))
        qms, qrstd, top, ntop, total, rden = (st[:, 8 + 4 * n:12 + 4 * n] for n in range(6))
        block = ph.block()

        @block.sync
        def _(sp):
            def one(dst, src):
                sp.dma_start(dst, src).then_inc(s.loaded, 16)
            one(gain[:], io["norm_cross"].partition_broadcast(P))
            one(ffn_gain[:], io["norm_ffn"].partition_broadcast(P))
            one(csilu[:], io["c_2"].rearrange("a (p c) -> p (a c)", c=NC))
            sp.dma_start(wq[:], rows_by_partition(io["w_cq"])).then_inc(s.wq_loaded, 16)
            sp.dma_start(wr[:, :, 0:G1], rows_by_partition(io["w_router_group"])).then_inc(s.wr_loaded, 16)
            for g in range(G1):
                sp.dma_start(wr[:, :, G1 + g * PER_G:G1 + (g + 1) * PER_G],
                             rows_by_partition(io["w_router_expert"][g])).then_inc(s.wr_loaded, 16)
            sp.dma_start(wo[:], rows_by_partition(io["w_co"])).then_inc(s.wo_loaded, 16)
            w_mod = io["w_mod_2"][0].rearrange("(p c) n -> p c n", c=NC)

            def store(t):
                sp.wait_ge(s.rows_ready, t + 1)
                sp.dma_start(keep["rows"][bass.ts(t, P), :], rows[:]).then_inc(s.stored, 16)
                sp.dma_start(keep["acc"][bass.ts(t, P), :], tile_of(x, t)).then_inc(s.stored, 16)

            def tile(t, half):
                for n in range(NC):
                    sp.wait_ge(s.piece_free, t * NC + n + 1)
                    sp.dma_start(pieces[:, n % 4, :], w_mod[:, n, bass.ts(t, PIECE)]) \
                        .then_inc(piece_loaded[n % 4], 16)
                    if n == 3 and not is_first(t):
                        store(t - 1)
                sp.wait_ge(s.sums_ready, t + 1)
                sp.dma_start(keep["mod_part"][:, bass.ts(t, PIECE)], sums[:, half, :]).then_inc(sums_stored[half], 16)

            all_tiles(sp, tile)
            store(NT - 1)
            sp.dma_start(keep["acc"][T:T + P, :], tile_of(x, 0)).then_inc(s.stored, 16)
            sp.wait_ge(s.stored, 32 + 16 * (2 * NT + 1))
            for half in range(2):
                sp.wait_ge(sums_stored[half], 16 + 16 * NT // 2)

        @block.gpsimd
        def _(pool):
            step = Steps(pool, s.pool_steps)
            mh = keep["minus_half"]

            def root(squared, value, rms, out, mean):
                hold(pool, squared, value, s.passed)
                inverse_root(pool, step, out, mean, mh).then_inc(rms, 1)

            def tile(t, half):
                if not is_last(t):
                    root(s.squared, t + 2, s.rms, rstd, ms)
                if not is_first(t):
                    root(s.b_squared, t, s.b_rms, brstd, bms)
                if not is_last(t):
                    root(s.q_squared, t + 2, s.q_rms, qrstd, qms)

            root(s.squared, 1, s.rms, rstd, ms)
            root(s.q_squared, 1, s.q_rms, qrstd, qms)
            all_tiles(pool, tile, step, 3)
            root(s.b_squared, NT, s.b_rms, brstd, bms)

        @block.scalar
        def _(act):
            def square_x(t):
                act.activation(junk[:], tile_of(x, t), ACT.Square, scale=D ** -0.5, accum_out=ms) \
                    .then_inc(s.squared, 1)

            def square_q(t):
                act.wait_ge(s.q_done, t + 1)
                for n in range(XH):
                    last = act.activation(qjunk[:, n * XD:(n + 1) * XD], heads(wa)[:, n, :], ACT.Square,
                                          scale=XD ** -0.5, accum_out=qms[:, n:n + 1])
                last.then_inc(s.q_squared, 1)

            def square_b(t):
                hold(act, s.x_done, t + 1, s.passed)
                act.activation(junk[:], tile_of(x, t), ACT.Square, scale=D ** -0.5, accum_out=bms) \
                    .then_inc(s.b_squared, 1)

            def take(turned, t, out, src, ready):
                act.wait_ge(turned, t + 1)
                act.copy(out, src).then_inc(ready, 1)

            def tile(t, half):
                if not is_last(t):
                    square_x(t + 1)
                    take(s.turned, t + 1, hT[:], chunks(wc), s.hT_ready)
                    act.wait_ge(s.squared, t + 2)
                if not is_first(t):
                    square_b(t - 1)
                    act.wait_ge(s.b_squared, t)
                act.wait_ge(s.top_ready, t + 1)
                for n in range(XH):
                    last = act.activation(pr[:, n * MEM:(n + 1) * MEM], heads(wd)[:, n, :], ACT.Exp,
                                          bias=ntop[:, n:n + 1], accum_out=total[:, n:n + 1])
                last.then_inc(s.exps, 1)
                take(s.p_turned, t, poT[:], chunks(wb), s.pT_ready)
                if not is_last(t):
                    square_q(t + 1)
                take(s.o_turned, t, poT[:, 0:4, :], chunks(wc)[:, 0:4, :], s.oT_ready0)
                if not is_last(t):
                    take(s.q_turned, t + 1, qbT[:], chunks(wd), s.qT_ready)

            act.wait_ge(s.loaded, 48)
            act.activation(csilu[:], csilu[:], ACT.Silu).then_inc(s.silu_ready, 1)
            square_x(0)
            take(s.turned, 0, hT[:], chunks(wc), s.hT_ready)
            square_q(0)
            take(s.q_turned, 0, qbT[:], chunks(wd), s.qT_ready)
            all_tiles(act, tile)
            square_b(NT - 1)

        @block.vector
        def _(dve):
            step = Steps(dve, s.vec)

            def norm_input(t):
                dve.wait_ge(s.rms, t + 1)
                dve.scalar_tensor_tensor(hn[:], tile_of(x, t), rstd, gain[:], ALU.mult, ALU.mult) \
                    .then_inc(s.normed, 1)

            def norm_q(t):
                dve.wait_ge(s.q_rms, t + 1)
                dve.tensor_tensor(qn[:].rearrange("p (h d) -> p h d", h=XH), heads(wa), spread(qrstd, XD),
                                  ALU.mult).then_inc(s.q_normed, 1)

            def add_output(t):
                dve.wait_ge(s.out_done, t + 1)
                dve.tensor_tensor(tile_of(x, t), wb[:].rearrange("p a n -> p (a n)"), tile_of(x, t),
                                  ALU.add).then_inc(s.x_done, 1)

            def norm_rows(t):
                dve.wait_ge(s.b_rms, t + 1)
                dve.wait_ge(s.stored, t * 32 + 32)
                dve.scalar_tensor_tensor(rows[:], tile_of(x, t), brstd, ffn_gain[:], ALU.mult,
                                         ALU.mult).then_inc(s.rows_ready, 1)

            def take_rows(t):
                dve.wait_ge(s.b_turned, t + 1)
                dve.tensor_copy(qbT[:], chunks(wc)).then_inc(s.bT_ready, 1)

            def take_logits(t):
                dve.wait_ge(s.logits_done, t + 1)
                dve.tensor_tensor(tile_of(logits, t), wb[:, 0, 0:LOGITS], keep["zero"].broadcast_to([P, LOGITS]),
                                  ALU.add).then_inc(s.logits_ready, 1)

            def add_pieces(t, half, ns):
                for n in ns:
                    dve.wait_ge(piece_loaded[n % 4], t * 32 + 16 * (n // 4 + 1))
                    out, piece = sums[:, half, :], pieces[:, n % 4, :]
                    if n == 0:
                        dve.wait_ge(sums_stored[half], (t - half) * 8 + 16)
                        last = dve.tensor_scalar(out, piece, csilu[:, 0:1], None, ALU.mult)
                    else:
                        step.wait()
                        last = dve.scalar_tensor_tensor(out, piece, csilu[:, n:n + 1], out, ALU.mult, ALU.add)
                    step.did(last)
                step.wait()
                dve.sem_inc(s.piece_free, len(ns))

            def tile(t, half):
                if not is_last(t):
                    norm_input(t + 1)
                add_pieces(t, half, range(4))
                if not is_first(t):
                    add_output(t - 1)
                dve.wait_ge(s.scored, t + 1)
                step.did(dve.tensor_reduce(top, heads(wd), AX, ALU.max))
                step.wait()
                dve.tensor_scalar(ntop, top, -1.0, None, ALU.mult).then_inc(s.top_ready, 1)
                if not is_first(t):
                    norm_rows(t - 1)
                add_pieces(t, half, range(4, NC))
                dve.sem_inc(s.sums_ready, 1)
                dve.wait_ge(s.exps, t + 1)
                step.did(dve.reciprocal(rden, total))
                if not is_first(t):
                    take_rows(t - 1)
                step.wait()
                dve.wait_ge(s.attended, t + 1)
                dve.tensor_tensor(on[:].rearrange("p (h d) -> p h d", h=XH), heads(wd), spread(rden, XD),
                                  ALU.mult).then_inc(s.o_ready, 1)
                if not is_first(t):
                    take_logits(t - 1)
                if not is_last(t):
                    norm_q(t + 1)
                dve.wait_ge(s.o_turned, t + 1)
                dve.tensor_copy(poT[:, 4:NC, :], chunks(wc)[:, 4:NC, :]).then_inc(s.oT_ready1, 1)

            dve.sem_inc(s.piece_free, 4)
            dve.sem_inc(s.stored, 32)
            for half in range(2):
                dve.sem_inc(sums_stored[half], 16)
            dve.wait_ge(s.loaded, 48)
            norm_input(0)
            norm_q(0)
            dve.wait_ge(s.silu_ready, 1)
            all_tiles(dve, tile, step, NC + 2)
            add_output(NT - 1)
            norm_rows(NT - 1)
            take_rows(NT - 1)
            take_logits(NT - 1)

        @block.tensor
        def _(pe):
            def turn(out, src):
                for c in range(NC):
                    last = pe.transpose(chunks(out)[:, c, :], src[:, c * P:(c + 1) * P], ident)
                return last

            def turn_input(t):
                pe.wait_ge(s.normed, t + 1)
                transpose_tile(pe, chunks(wc), hn[:], ident).then_inc(s.turned, 1)

            def project(t):
                pe.wait_ge(s.hT_ready, t + 1)
                for n in range(2):
                    last = product(pe, wa[:, n, :], hT, wq[:, :, n * 512:(n + 1) * 512])
                last.then_inc(s.q_done, 1)

            def turn_q(t):
                pe.wait_ge(s.q_normed, t + 1)
                turn(wd, qn).then_inc(s.q_turned, 1)

            def turn_rows(t):
                pe.wait_ge(s.rows_ready, t + 1)
                transpose_tile(pe, chunks(wc), rows[:], ident).then_inc(s.b_turned, 1)

            def route(t):
                pe.wait_ge(s.bT_ready, t + 1)
                product(pe, wb[:, 0, 0:LOGITS], qbT, wr).then_inc(s.logits_done, 1)

            def tile(t, half):
                if not is_last(t):
                    turn_input(t + 1)
                pe.wait_ge(s.qT_ready, t + 1)
                for n in range(XH):
                    for c in range(2):
                        last = pe.matmul(heads(wd)[:, n, :], qbT[:, 2 * n + c, :], kmT[:, 2 * n + c, :],
                                         start=(c == 0), stop=(c == 1))
                last.then_inc(s.scored, 1)
                if not is_last(t):
                    project(t + 1)
                if not is_first(t):
                    pe.wait_ge(s.x_done, t)
                pe.wait_ge(s.exps, t + 1)
                turn(wb, pr).then_inc(s.p_turned, 1)
                if not is_first(t):
                    turn_rows(t - 1)
                pe.wait_ge(s.pT_ready, t + 1)
                for n in range(XH):
                    for c in range(2):
                        last = pe.matmul(heads(wd)[:, n, :], poT[:, 2 * n + c, :], vm[:, c, n * XD:(n + 1) * XD],
                                         start=(c == 0), stop=(c == 1))
                last.then_inc(s.attended, 1)
                if not is_first(t):
                    route(t - 1)
                pe.wait_ge(s.o_ready, t + 1)
                transpose_tile(pe, chunks(wc), on[:], ident).then_inc(s.o_turned, 1)
                if not is_last(t):
                    turn_q(t + 1)
                if not is_first(t):
                    pe.wait_ge(s.logits_ready, t)
                pe.wait_ge(s.oT_ready0, t + 1)
                pe.wait_ge(s.oT_ready1, t + 1)
                for n in range(2):
                    last = product(pe, wb[:, n, :], poT, wo[:, :, n * 512:(n + 1) * 512])
                last.then_inc(s.out_done, 1)

            turn_input(0)
            pe.wait_ge(s.wq_loaded, 16)
            project(0)
            turn_q(0)
            pe.wait_ge(s.wr_loaded, 16 * (1 + G1))
            pe.wait_ge(s.wo_loaded, 16)
            all_tiles(pe, tile)
            turn_rows(NT - 1)
            pe.wait_ge(s.x_done, NT)
            route(NT - 1)


UNIT = 4096
RING = 6
FAR = 1e6
AHEAD = 3
Shared = namedtuple("Shared", "slot_of gate over over_from pa pb")


def phase_experts(nc, io, keep, cfg, route):
    NE, F = cfg["experts"], cfg["width"]
    FC = F // P
    HALVES = F // 512
    PER_UNIT = UNIT // F
    U1 = NC // PER_UNIT
    U2 = FC * D // UNIT
    UNITS = 2 * U1 + U2
    TOGETHER = RING // UNITS
    ks = keep["consts"]
    ident = ks[:, K_IDENT:K_IDENT + P]
    rows, sums = cfg["rows"], cfg["sums"]
    with Phase(nc, cfg["name"]) as ph:
        ring = ph.sb("ring", [P, RING, UNIT])
        xg = ph.sb("xg", [P, 2, D])
        xT = ph.sb("xT", [P, NC, P])
        hit = ph.sb("hit", [P, NT, P])
        act_out = ph.sb("act_out", [P, F])
        hid = ph.sb("hid", [P, F])
        hidT = ph.sb("hidT", [P, FC, P])
        y = ph.sb("y", [P, D])
        what = ph.sb("what", [P, NT, 4])
        found = ph.sb("found", [P, 4])
        slots = ph.sb("slots", [P, 2, 4])
        gidx = ph.sb("gidx", [P, 2], I32)
        sidx = ph.sb("sidx", [P, 2], I32)
        local = ph.sb("local", [P, NT])
        over = ph.sb("over", [P, 16], I32)
        over_from = ph.sb("over_from", [P, 16])
        slot_of = ph.sb("slot_of", [P, NT, NE + AHEAD])
        gate = ph.sb("gate", [P, NT, NE + AHEAD])
        tp = ph.ps("tp", [P, NC, P])
        pa = ph.ps("pa", [P, 2, 512])
        pb = ph.ps("pb", [P, 2, 512])
        py = ph.ps("py", [P, 2, 512])
        pa_chunks = pa[:].rearrange("p a (c n) -> p (a c) n", n=P)
        names = ("hits_ready ids_done ids_ready targets_ready gathered0 gathered1 x_turned xT_ready silu_done "
                 "hid_ready hid_turned hidT_ready y_ready y_free added vec passed units_used")
        main = ph.sems(names, ns=True)
        more = ph.sems(names, ns=True, prefix="o_")
        more_loaded, = ph.sems("o_loaded")
        unit_loaded = ph.sems(" ".join(f"unit{n}_loaded" for n in range(RING)))
        routed, = ph.sems("routed")
        route.buffers(ph, Shared(slot_of=slot_of, gate=gate, over=over, over_from=over_from, pa=pa, pb=pb))
        block = ph.block()


        def hits(dve, S, step, e, start):
            slot = slot_of[:, :, bass.ds(e, 1)].rearrange("p t a -> p (t a)")
            if start is not None:
                step.did(dve.tensor_scalar(local[:], slot, start, None, ALU.subtract))
                step.wait()
                slot = local[:]
            dve.tensor_tensor(hit[:], tiled(ks[:, K_IOTA:K_IOTA + P], NT), spread(slot, P), ALU.is_equal)
            dve.tensor_scalar(what[:, :, 1:2], gate[:, :, bass.ds(e, 1)], 1.0, None, ALU.mult) \
                .then_inc(S.hits_ready, 1)

        def to_gather(dve, S, step, par, k):
            dve.wait_ge(S.ids_done, k + 1)
            step.did(dve.tensor_copy(found[:, 0:3], pb[:, 0, 0:3]))
            step.wait()
            dve.tensor_copy(gidx[:, par:par + 1], found[:, 0:1]).then_inc(S.ids_ready, 1)

        def to_add(dve, S, step, par, added):
            dve.wait_ge(S.y_ready, added)
            step.did(dve.tensor_copy(slots[:, par, 0:3], found[:, 0:3]))
            step.wait()
            step.did(dve.scalar_tensor_tensor(slots[:, par, 3:4], slots[:, par, 2:3],
                                              ks[:, K_SPARE + 1:K_SPARE + 2], slots[:, par, 0:1], ALU.mult,
                                              ALU.add))
            step.wait()
            dve.wait_ge(S.y_free, added)
            dve.tensor_tensor(sidx[:, par:par + 1], slots[:, par, 3:4], ks[:, K_SPARE:K_SPARE + 1], ALU.add) \
                .then_inc(S.targets_ready, 1)


        def used(S, k, n):
            return (RING if S is main else 1) + UNITS * k + n

        def hidden(dve, S, k):
            dve.wait_ge(S.silu_done, k + 1)
            dve.wait_ge(S.units_used, used(S, k, 2 * U1))
            dve.tensor_tensor(hid[:].rearrange("p (a n) -> p a n", n=512), pb[:, 0:HALVES, :],
                              act_out[:].rearrange("p (a n) -> p a n", n=512), ALU.mult).then_inc(S.hid_ready, 1)

        def weighted(dve, S, par, k):
            dve.wait_ge(S.units_used, used(S, k, UNITS))
            dve.wait_ge(S.y_free, k + 1)
            if cfg["out_scale"] is None:
                last = dve.tensor_scalar(y[:], py[:].rearrange("p a n -> p (a n)"), slots[:, par, 1:2], None, ALU.mult)
            else:
                last = dve.scalar_tensor_tensor(y[:], py[:].rearrange("p a n -> p (a n)"), slots[:, par, 1:2],
                                                cfg["out_scale"], ALU.mult, ALU.mult)
            last.then_inc(S.y_ready, 1)

        def identify(pe, S, k):
            pe.wait_ge(S.hits_ready, k + 1)
            for t in range(NT):
                last = pe.matmul(pb[:, 0, 0:4], hit[:, t, :], what[:, t, :], start=(t == 0), stop=(t == NT - 1))
            last.then_inc(S.ids_done, 1)

        def turn_rows(pe, S, par, loads, k):
            pe.wait_ge((S.gathered0, S.gathered1)[par], loads)
            transpose_tile(pe, tp, xg[:, par, :], ident).then_inc(S.x_turned, 1)

        def up(pe, S, k, slot_at, arrived, identified):
            pe.wait_ge(S.xT_ready, k + 1)
            pe.wait_ge(S.ids_ready, identified)
            for u in range(2 * U1):
                out = pb if u % 2 else pa
                w = ring[:, slot_at + u, :].rearrange("p (c n) -> p c n", n=F)
                arrived(pe, slot_at + u)
                for n in range(HALVES):
                    for c in range(PER_UNIT):
                        at = u // 2 * PER_UNIT + c
                        last = pe.matmul(out[:, n, :], xT[:, at, :], w[:, c, n * 512:(n + 1) * 512],
                                         start=(at == 0), stop=(at == NC - 1))
                last.then_inc(S.units_used, 1)

        def turn_hidden(pe, S, k):
            pe.wait_ge(S.hid_ready, k + 1)
            for c in range(FC):
                last = pe.transpose(pa_chunks[:, c, :], hid[:].rearrange("p (d c) -> p c d", c=FC)[:, c, :], ident)
            last.then_inc(S.hid_turned, 1)

        def down(pe, S, k, slot_at, arrived):
            pe.wait_ge(S.hidT_ready, k + 1)
            pe.wait_ge(S.y_ready, k + 1)
            for u in range(U2):
                w = ring[:, slot_at + 2 * U1 + u, :].rearrange("p (c n) -> p c n", n=D)
                arrived(pe, slot_at + 2 * U1 + u)
                for n in range(2):
                    for c in range(4):
                        at = 4 * u + c
                        last = pe.matmul(py[:, n, :], hidT[:, at, :], w[:, c, n * 512:(n + 1) * 512],
                                         start=(at == 0), stop=(at == FC - 1))
                last.then_inc(S.units_used, 1)

        def silu(act, S, k):
            act.wait_ge(S.units_used, used(S, k, 2 * U1 - 1))
            act.activation(act_out[:].rearrange("p (a n) -> p a n", n=512), pa[:, 0:HALVES, :],
                           ACT.Silu).then_inc(S.silu_done, 1)

        def keep_rows(act, S, k):
            act.wait_ge(S.x_turned, k + 1)
            act.copy(xT[:], tp[:]).then_inc(S.xT_ready, 1)

        def keep_hidden(act, S, k):
            act.wait_ge(S.hid_turned, k + 1)
            act.copy(hidT[:], pa_chunks[:, 0:FC, :]).then_inc(S.hidT_ready, 1)

        def gather(pool, S, par, k):
            hold(pool, S.ids_ready, k + 1, S.passed)
            pool.indirect_dma_start(xg[:, par, :], None, rows,
                                    bass.IndirectOffsetOnAxis(ap=gidx[:, par:par + 1], axis=0)) \
                .then_inc((S.gathered0, S.gathered1)[par], 16)

        def add_rows(pool, S, par, k):
            hold(pool, S.targets_ready, k + 1, S.passed)
            hold(pool, S.y_ready, k + 2, S.passed)
            pool.indirect_dma_start(sums, bass.IndirectOffsetOnAxis(ap=sidx[:, par:par + 1], axis=0), y[:], None,
                                    compute_op=ALU.add).then_inc(S.added, 16)
            hold(pool, S.added, 16 * k + 16, S.passed)
            pool.sem_inc(S.y_free, 1)

        def main_arrived(r):
            return lambda pe, slot: pe.wait_ge(unit_loaded[slot], 16 * r + 16)

        ROUNDS = NE // TOGETHER

        def weights(e):
            found = []
            for u in range(U1):
                for w in (io[cfg["w1"]], io[cfg["w3"]]):
                    found.append(cfg["pick"](w, e).rearrange("(p c) n -> p c n", c=NC)
                                 [:, u * PER_UNIT:(u + 1) * PER_UNIT, :])
            for u in range(U2):
                found.append(cfg["pick"](io[cfg["w2"]], e).rearrange("(p c) n -> p c n", c=FC)[:, 4 * u:4 * u + 4, :])
            return found

        @block.sync
        def _(sp):
            route.sync(sp)
            with sp.Fori(0, ROUNDS) as r:
                for b in range(TOGETHER):
                    for n, src in enumerate(weights(r * TOGETHER + b)):
                        slot = b * UNITS + n
                        sp.wait_ge(main.units_used, RING * r + slot + 1)
                        sp.dma_start(ring[:, slot, :].rearrange("p (c n) -> p c n", n=src.shape[2]), src) \
                            .then_inc(unit_loaded[slot], 16)
            if cfg["overflow"]:
                sp.wait_ge(routed, 1)
                n_over = sp.value_load(over[0:1, 15:16], min_val=0, max_val=MAX_OVER)
                sp.wait_ge(main.units_used, RING * (ROUNDS + 1))
                with sp.Fori(0, MAX_OVER) as j:
                    with sp.If(n_over > j):
                        e = sp.value_load(over[0:1, bass.ds(j, 1)], min_val=0, max_val=NE - 1)
                        sp.wait_ge(more.units_used, UNITS * j + 1)
                        for n, src in enumerate(weights(e)):
                            sp.dma_start(ring[:, n, :].rearrange("p (c n) -> p c n", n=src.shape[2]), src) \
                                .then_inc(more_loaded, 16)
                    with sp.Else():
                        sp.nop()
                    sp.nop()

        @block.gpsimd
        def _(pool):
            hold(pool, routed, 1, main.passed)
            for e in range(2):
                gather(pool, main, e, e)
            with pool.Fori(0, NE // 2) as r:
                for b in range(2):
                    e = r * 2 + b
                    gather(pool, main, b, e + 2)
                    add_rows(pool, main, b, e)
            for b in range(2):
                hold(pool, (main.gathered0, main.gathered1)[b], 16 * (NE // 2 + 1), main.passed)
            if cfg["overflow"]:
                n_over = pool.value_load(over[0:1, 15:16], min_val=0, max_val=MAX_OVER)
                with pool.Fori(0, MAX_OVER) as j:
                    with pool.If(n_over > j):
                        gather(pool, more, 0, j)
                        add_rows(pool, more, 0, j)
                    with pool.Else():
                        pool.nop()
                    pool.nop()

        @block.scalar
        def _(act):
            route.scalar(act)
            keep_rows(act, main, 0)
            with act.Fori(0, NE // 2) as r:
                for b in range(2):
                    e = r * 2 + b
                    silu(act, main, e)
                    keep_rows(act, main, e + 1)
                    keep_hidden(act, main, e)
            if cfg["overflow"]:
                act.wait_ge(routed, 1)
                n_over = act.value_load(over[0:1, 15:16], min_val=0, max_val=MAX_OVER)
                with act.Fori(0, MAX_OVER) as j:
                    with act.If(n_over > j):
                        keep_rows(act, more, j)
                        silu(act, more, j)
                        keep_hidden(act, more, j)
                    with act.Else():
                        act.nop()
                    act.nop()

        @block.vector
        def _(dve):
            dve.sem_inc(main.y_free, 1)
            dve.sem_inc(main.y_ready, 1)
            step = Steps(dve, main.vec)
            step.did(dve.memset(slot_of[:, :, NE:NE + AHEAD], FAR))
            step.did(dve.memset(gate[:, :, NE:NE + AHEAD], 0.0))
            step.did(dve.memset(what[:], 1.0))
            step.wait()
            step.did(dve.tensor_copy(what[:, :, 0:1], ks[:, K_TOKEN:K_TOKEN + NT].unsqueeze(2)))
            route.vector(dve, step)
            step.wait()
            dve.sem_inc(routed, 1)
            hits(dve, main, step, 0, None)
            for e in range(2):
                to_gather(dve, main, step, e, e)
                hits(dve, main, step, e + 1, None)
                to_add(dve, main, step, e, 1)
            with dve.Fori(0, NE // 2) as r:
                step.enter(r, 2 * 3)
                for b in range(2):
                    e = r * 2 + b
                    hidden(dve, main, e)
                    to_gather(dve, main, step, b, e + 2)
                    weighted(dve, main, b, e)
                    hits(dve, main, step, e + 3, None)
                    to_add(dve, main, step, b, e + 2)
                step.leave(NE // 2)
            if cfg["overflow"]:
                dve.sem_inc(more.y_free, 1)
                dve.sem_inc(more.y_ready, 1)
                o_step = Steps(dve, more.vec)
                n_over = dve.value_load(over[0:1, 15:16], min_val=0, max_val=MAX_OVER)
                with dve.Fori(0, MAX_OVER) as j:
                    with dve.If(n_over > j):
                        o_step.enter(j, 4)
                        e = dve.value_load(over[0:1, bass.ds(j, 1)], min_val=0, max_val=NE - 1)
                        hits(dve, more, o_step, e, over_from[:, bass.ds(j, 1)])
                        to_gather(dve, more, o_step, 0, j)
                        to_add(dve, more, o_step, 0, j + 1)
                        hidden(dve, more, j)
                        weighted(dve, more, 0, j)
                        assert o_step.n == 4
                    with dve.Else():
                        dve.nop()
                    dve.nop()

        @block.tensor
        def _(pe):
            pe.sem_inc(main.units_used, RING)
            route.tensor(pe)
            identify(pe, main, 0)
            pe.wait_ge(main.ids_ready, 1)
            identify(pe, main, 1)
            turn_rows(pe, main, 0, 16, 0)
            with pe.Fori(0, NE // 2) as r:
                for b in range(2):
                    e = r * 2 + b
                    at = b * UNITS if TOGETHER == 2 else 0
                    arrived = main_arrived(r if TOGETHER == 2 else e)
                    up(pe, main, e, at, arrived, e + 2)
                    turn_rows(pe, main, 1 - b, 16 * r + (16 if b == 0 else 32), e + 1)
                    turn_hidden(pe, main, e)
                    identify(pe, main, e + 2)
                    down(pe, main, e, at, arrived)
            if cfg["overflow"]:
                pe.wait_ge(routed, 1)
                pe.sem_inc(more.units_used, 1)
                n_over = pe.value_load(over[0:1, 15:16], min_val=0, max_val=MAX_OVER)
                with pe.Fori(0, MAX_OVER) as j:
                    with pe.If(n_over > j):
                        def arrived(pe, slot):
                            pe.wait_ge(more_loaded, 16 * UNITS * j + 16 * UNITS)
                        identify(pe, more, j)
                        turn_rows(pe, more, 0, 16 * j + 16, j)
                        up(pe, more, j, 0, arrived, j + 1)
                        turn_hidden(pe, more, j)
                        down(pe, more, j, 0, arrived)
                    with pe.Else():
                        pe.nop()
                    pe.nop()


class GroupRouting:

    def __init__(self, keep):
        self.keep = keep

    def buffers(self, ph, o):
        self.o = o
        self.w = {n: ph.sb(n, [P, NT * E1]) for n in
                  "le ml hot1 hot2 sel before".split()}
        self.g = {n: ph.sb(n, [P, NT * G1]) for n in "lg eq hotg away".split()}
        self.t = {n: ph.sb(n, [P, NT]) for n in "mg mt gw m1 m2 g1 g2 ed".split()}
        self.c = {n: ph.sb(n, [P, E1]) for n in "total counts extra ends ones".split()}
        self.over_w = ph.sb("over_w", [P, 2, MAX_OVER * E1])
        self.over_n = ph.sb("over_n", [P, 2, 16])
        self.onesm = ph.sb("onesm", [P, P])
        self.s = ph.sems("ranks_in ranks_done shifted group_exp pair_exp", ns=True)

    def sync(self, sp):
        pass

    def scalar(self, act):
        act.wait_ge(self.s.shifted, 1)
        act.activation(self.g["eq"][:], self.g["eq"][:], ACT.Exp).then_inc(self.s.group_exp, 1)
        act.wait_ge(self.s.shifted, 2)
        act.activation(self.t["ed"][:], self.t["ed"][:], ACT.Exp).then_inc(self.s.pair_exp, 1)

    def tensor(self, pe):
        pe.wait_ge(self.s.ranks_in, 1)
        n = NT * E1
        ranks, totals = self.o.pa[:, 0, 0:n], self.o.pb[:, 0, 0:E1]
        before = self.keep["consts"][:, K_BEFORE:K_BEFORE + P]
        pe.matmul(ranks, before, self.w["sel"][:], start=True, stop=False)
        pe.matmul(ranks, self.onesm[:], self.w["before"][:], start=False, stop=True)
        pe.matmul(totals, self.onesm[:], self.c["total"][:], start=True, stop=True).then_inc(self.s.ranks_done, 1)

    def vector(self, dve, step):
        w, g, t, c, o, s = self.w, self.g, self.t, self.c, self.o, self.s
        ks, logits = self.keep["consts"], self.keep["logits"]

        def do(instruction):
            step.did(instruction)
            step.wait()

        def tiles(x, n):
            return x[:].rearrange("p (t e) -> p t e", e=n)

        def first_of(hot, x, top, n):
            rev = ks[:, K_REV32 + 32 - n:K_REV32 + 32]
            do(dve.tensor_reduce(top[:], tiles(x, n), AX, ALU.max))
            do(dve.tensor_tensor(tiles(hot, n), tiles(x, n), spread(top[:], n), ALU.is_equal))
            do(dve.tensor_tensor(tiles(hot, n), tiles(hot, n), tiled(rev, NT), ALU.mult))
            do(dve.tensor_reduce(t["mt"][:], tiles(hot, n), AX, ALU.max))
            do(dve.tensor_tensor(tiles(hot, n), tiles(hot, n), spread(t["mt"][:], n), ALU.is_equal))

        do(dve.memset(self.onesm[:], 1.0))
        do(dve.memset(c["ones"][:], 1.0))
        do(dve.tensor_copy(tiles(g["lg"], G1), logits[:, :, 0:G1]))
        do(dve.tensor_copy(tiles(w["le"], E1), logits[:, :, G1:LOGITS]))
        first_of(g["hotg"], g["lg"], t["mg"], G1)
        step.did(dve.tensor_tensor(tiles(g["eq"], G1), tiles(g["lg"], G1), spread(t["mg"][:], G1), ALU.subtract))
        step.wait()
        dve.sem_inc(s.shifted, 1)
        do(dve.tensor_scalar(g["away"][:], g["hotg"][:], -1.0, -MASKED, ALU.add, ALU.mult))
        do(dve.tensor_tensor(tiles(w["ml"], PER_G), tiles(w["le"], PER_G), spread(g["hotg"][:], PER_G), ALU.mult))
        do(dve.tensor_tensor(tiles(w["ml"], PER_G), tiles(w["ml"], PER_G), spread(g["away"][:], PER_G), ALU.add))
        first_of(w["hot1"], w["ml"], t["m1"], E1)
        do(dve.scalar_tensor_tensor(w["ml"][:], w["hot1"][:], 10 * MASKED, w["ml"][:], ALU.mult, ALU.add))
        first_of(w["hot2"], w["ml"], t["m2"], E1)
        do(dve.tensor_tensor(t["ed"][:], t["m2"][:], t["m1"][:], ALU.subtract))
        dve.sem_inc(s.shifted, 1)
        do(dve.tensor_tensor(w["sel"][:], w["hot1"][:], w["hot2"][:], ALU.add))
        sel, before = tiles(w["sel"], E1), tiles(w["before"], E1)
        do(dve.memset(before[:, 0, :], 0.0))
        for n in range(1, NT):
            do(dve.tensor_tensor(before[:, n, :], before[:, n - 1, :], sel[:, n - 1, :], ALU.add))
        do(dve.tensor_tensor(c["total"][:], before[:, NT - 1, :], sel[:, NT - 1, :], ALU.add))
        dve.sem_inc(s.ranks_in, 1)
        dve.wait_ge(s.group_exp, 1)
        do(dve.tensor_reduce(t["gw"][:], tiles(g["eq"], G1), AX, ALU.add))
        dve.wait_ge(s.pair_exp, 1)
        do(dve.tensor_scalar(t["g1"][:], t["ed"][:], 1.0, None, ALU.add))
        do(dve.tensor_tensor(t["g1"][:], t["g1"][:], t["gw"][:], ALU.mult))
        do(dve.reciprocal(t["g1"][:], t["g1"][:]))
        do(dve.tensor_tensor(t["g2"][:], t["g1"][:], t["ed"][:], ALU.mult))
        do(dve.tensor_tensor(tiles(w["hot1"], E1), tiles(w["hot1"], E1), spread(t["g1"][:], E1), ALU.mult))
        do(dve.tensor_tensor(tiles(w["hot2"], E1), tiles(w["hot2"], E1), spread(t["g2"][:], E1), ALU.mult))
        do(dve.tensor_tensor(o.gate[:, :, 0:E1], tiles(w["hot1"], E1), tiles(w["hot2"], E1), ALU.add))
        dve.wait_ge(s.ranks_done, 1)
        do(dve.tensor_scalar(w["sel"][:], w["sel"][:], -FAR, FAR, ALU.mult, ALU.add))
        do(dve.tensor_tensor(o.slot_of[:, :, 0:E1], self.o.pa[:, 0, 0:NT * E1].rearrange("p (t e) -> p t e", e=E1),
                             sel, ALU.add))
        do(dve.tensor_copy(c["counts"][:], o.pb[:, 0, 0:E1]))
        do(dve.memset(c["extra"][:], 0.0))
        for n in range(1, T // P):
            do(dve.scalar_tensor_tensor(c["extra"][:], c["counts"][:], float(n * P), c["extra"][:], ALU.is_gt,
                                        ALU.add))
        do(dve.tensor_tensor_scan(c["ends"][:], c["ones"][:], c["extra"][:], 0.0, ALU.mult, ALU.add))
        past = self.over_w[:, 0, :].rearrange("p (j e) -> p j e", e=E1)
        gone = self.over_w[:, 1, :].rearrange("p (j e) -> p j e", e=E1)
        iota = ks[:, K_IOTA:K_IOTA + MAX_OVER]
        do(dve.tensor_tensor(past, spread(iota, E1), tiled(c["ends"][:], MAX_OVER), ALU.is_ge))
        do(dve.tensor_tensor(gone, past, tiled(c["extra"][:], MAX_OVER), ALU.mult))
        do(dve.tensor_reduce(self.over_n[:, 0, 0:MAX_OVER], past, AX, ALU.add))
        do(dve.tensor_reduce(self.over_n[:, 1, 0:MAX_OVER], gone, AX, ALU.add))
        do(dve.tensor_scalar(self.over_n[:, 0, 0:MAX_OVER], self.over_n[:, 0, 0:MAX_OVER], float(E1 - 1), None,
                             ALU.min))
        do(dve.tensor_tensor(self.over_n[:, 1, 0:MAX_OVER], iota, self.over_n[:, 1, 0:MAX_OVER], ALU.subtract))
        do(dve.tensor_scalar(o.over_from[:, 0:MAX_OVER], self.over_n[:, 1, 0:MAX_OVER], 1.0, float(P), ALU.add,
                             ALU.mult))
        do(dve.tensor_copy(o.over[:, 0:MAX_OVER], self.over_n[:, 0, 0:MAX_OVER]))
        do(dve.tensor_copy(o.over[:, 15:16], c["ends"][:, E1 - 1:E1]))


def columns(v):
    return v.rearrange("(c p) -> p c", p=P)


def phase_second_norm(nc, io, keep):
    ks, hT, yT, zT, mod = keep["consts"], keep["hT"], keep["yT"], keep["zT"], keep["mod"]
    ident = ks[:, K_IDENT:K_IDENT + P]
    HALF = T // 2
    with Phase(nc, "norm2") as ph:
        w = ph.sb("w", [P, NC, 2 * LRU])
        mod1 = ph.sb("mod1", [P, 2, D])
        v = keep["v"][:].rearrange("p t n -> p (t n)").rearrange("p (a n) -> p a n", n=D)
        xt, hn2 = v[:, 0:2, :], v[:, 2:4, :]
        junk, g12 = keep["qT"][:, 0:2, :], keep["kT"][:, 0:2, :]
        part, b_mod = keep["kT"][:, 2:3, :], keep["kT"][:, 3:4, :]
        part = part.rearrange("p a n -> p (a n)").rearrange("p (a n) -> p a n", n=512)
        b_mod = b_mod.rearrange("p a n -> p (a n)").rearrange("p (a n) -> p a n", n=512)
        st = ph.sb("st", [P, 4])
        ones = ph.sb("ones", [P, P])
        banks = ph.ps("banks", [P, 8, 512])
        tp2 = [banks[:, 2 * n:2 * n + 2, :].rearrange("p a (c n) -> p (a c) n", n=P) for n in range(2)]
        s = ph.sems("gains_loaded w_loaded part0 part1 bias0 bias1 ones_ready summed added ready "
                    "x_loaded0 x_loaded1 x_free squared rms normed turned hT_ready vec pool_steps passed "
                    "z_done x_done z_read x_read", ns=True)
        part_loaded, bias_loaded, x_loaded = [s.part0, s.part1], [s.bias0, s.bias1], [s.x_loaded0, s.x_loaded1]
        home = [mod1[:, 0, :], mod1[:, 1, :]] + [mod[:, n, :] for n in range(4)]
        block = ph.block()

        @block.sync
        def _(sp):
            for n, name in enumerate(("g_norm1_2", "g_norm2_2")):
                sp.dma_start(g12[:, n, :], io[name][0].partition_broadcast(P)).then_inc(s.gains_loaded, 16)
            for n in range(MOD // 512):
                if n >= 2:
                    sp.wait_ge(s.added, n - 1)
                sp.dma_start(part[:, n % 2, :], keep["mod_part"][:, n * 512:(n + 1) * 512]) \
                    .then_inc(part_loaded[n % 2], 16)
                sp.dma_start(b_mod[:, n % 2, :], io["b_mod_2"][0, n * 512:(n + 1) * 512].partition_broadcast(P)) \
                    .then_inc(bias_loaded[n % 2], 16)
            with sp.Fori(0, NT // 2) as r:
                for h in range(2):
                    sp.wait_ge(s.x_free, 2 * r + h + 1)
                    sp.dma_start(xt[:, h, :], keep["acc"][bass.ds(r * (2 * P) + h * P, P), :]) \
                        .then_inc(x_loaded[h], 16)
            sp.dma_start(w[:], rows_by_partition(io["w_in_2"][0][:, 0:2 * LRU])).then_inc(s.w_loaded, 16)

        @block.gpsimd
        def _(pool):
            step = Steps(pool, s.pool_steps)
            with pool.Fori(0, NT // 2) as r:
                step.enter(r, 2)
                for h in range(2):
                    hold(pool, s.squared, 2 * r + h + 1, s.passed)
                    inverse_root(pool, step, st[:, 2 + h:3 + h], st[:, h:h + 1], keep["minus_half"]) \
                        .then_inc(s.rms, 1)
                step.leave(NT // 2)

        @block.scalar
        def _(act):
            with act.Fori(0, NT // 2) as r:
                for h in range(2):
                    act.wait_ge(x_loaded[h], 16 * r + 16)
                    act.activation(junk[:, h, :], xt[:, h, :], ACT.Square, scale=D ** -0.5,
                                   accum_out=st[:, h:h + 1]).then_inc(s.squared, 1)
                for h in range(2):
                    hold(act, s.turned, 2 * r + h + 1, s.passed)
                    act.copy(hT[:, :, bass.ds(r * (2 * P) + h * P, P)], tp2[h]).then_inc(s.hT_ready, 1)
            with act.Fori(0, 2) as n:
                for j in range(LC):
                    hold(act, s.z_done, LC * n + j + 1, s.passed)
                    act.activation(zT[:, j, bass.ds(n * HALF, HALF)], banks[:, LC + j, :],
                                   ACT.Gelu_apprx_tanh).then_inc(s.z_read, 1)

        @block.vector
        def _(dve):
            step = Steps(dve, s.vec)
            dve.memset(ones[:], 1.0).then_inc(s.ones_ready, 1)
            dve.sem_inc(s.x_free, 2)
            dve.sem_inc(s.x_read, LC)
            dve.sem_inc(s.z_read, LC)
            for n in range(MOD // 512):
                dve.wait_ge(s.summed, n + 1)
                dve.wait_ge(bias_loaded[n % 2], 16 * (n // 2 + 1))
                dve.tensor_tensor(home[n // 2][:, n % 2 * 512:(n % 2 + 1) * 512], banks[:, n % 2, :],
                                  b_mod[:, n % 2, :], ALU.add).then_inc(s.added, 1)
            dve.wait_ge(s.added, MOD // 512)
            dve.wait_ge(s.gains_loaded, 32)
            step.did(dve.scalar_tensor_tensor(home[1], home[1], 1.0, g12[:, 0, :], ALU.add, ALU.mult))
            step.did(dve.scalar_tensor_tensor(home[4], home[4], 1.0, g12[:, 1, :], ALU.add, ALU.mult))
            step.wait()
            with dve.Fori(0, NT // 2) as r:
                step.enter(r, 2)
                for h in range(2):
                    dve.wait_ge(s.rms, 2 * r + h + 1)
                    dve.wait_ge(s.x_free, 2 * r + h + 1)
                    step.did(dve.scalar_tensor_tensor(hn2[:, h, :], xt[:, h, :], st[:, 2 + h:3 + h], home[1],
                                                      ALU.mult, ALU.mult))
                    step.wait()
                    dve.tensor_tensor(hn2[:, h, :], hn2[:, h, :], home[0], ALU.add).then_inc(s.normed, 1)
                for h in range(2):
                    dve.wait_ge(s.turned, 2 * r + h + 1)
                    dve.sem_inc(s.x_free, 1)
                step.leave(NT // 2)
            with dve.Fori(0, 2) as n:
                for j in range(LC):
                    dve.wait_ge(s.x_done, LC * n + j + 1)
                    dve.tensor_scalar(yT[:, j, bass.ds(n * HALF, HALF)], banks[:, j, :], 1.0, None,
                                      ALU.mult).then_inc(s.x_read, 1)

        @block.tensor
        def _(pe):
            pe.wait_ge(s.ones_ready, 1)
            for n in range(MOD // 512):
                pe.wait_ge(part_loaded[n % 2], 16 * (n // 2 + 1))
                if n >= 2:
                    pe.wait_ge(s.added, n - 1)
                pe.matmul(banks[:, n % 2, :], ones[:], part[:, n % 2, :], start=True, stop=True).then_inc(s.summed, 1)
            pe.wait_ge(s.added, MOD // 512)
            with pe.Fori(0, NT // 2) as r:
                for h in range(2):
                    pe.wait_ge(s.normed, 2 * r + h + 1)
                    transpose_tile(pe, tp2[h], hn2[:, h, :], ident).then_inc(s.turned, 1)
            pe.wait_ge(s.hT_ready, NT)
            pe.wait_ge(s.w_loaded, 16)
            with pe.Fori(0, 2) as n:
                for j in range(2 * LC):
                    done, read = (s.x_done, s.x_read) if j < LC else (s.z_done, s.z_read)
                    pe.wait_ge(read, LC * n + j % LC + 1)
                    for c in range(NC):
                        last = pe.matmul(banks[:, j, :], w[:, c, j * P:(j + 1) * P],
                                         hT[:, c, bass.ds(n * HALF, HALF)], start=(c == 0), stop=(c == NC - 1))
                    last.then_inc(done, 1)


def phase_lru(nc, io, keep):
    yT, zT = keep["yT"], keep["zT"]
    with Phase(nc, "lru") as ph:
        taps = ph.sb("taps", [P, 4, LC])
        conv_b = ph.sb("conv_b", [P, LC])
        lam = ph.sb("lam", [P, 2 * LC])
        sig = ph.sb("sig", [P, 4, 2 * LC])
        biases = ph.sb("biases", [P, 2, 2 * LC])
        blocks = ph.sb("blocks", [P, 2, 2 * LC, P])
        xc = ph.sb("xc", [P, 2, T])
        tr = ph.sb("tr", [P, 2, T])
        ti = ph.sb("ti", [P, 2, T])
        a = ph.sb("a", [P, 2, T])
        th = ph.sb("th", [P, 2, T])
        om = ph.sb("om", [P, 2, T])
        u, hs = keep["qT"][:, 0:2, :], keep["qT"][:, 2:4, :]
        gates = [ph.ps(f"gates{n}", [P, 2, 2, 512]) for n in range(2)]
        s = ph.sems("loaded blocks_clear blocks_loaded lam_ready convolved gates_done gates_read decays "
                    "squares roots vec passed half_ready scans", ns=True)
        block = ph.block()
        turns = [(j, d) for j in range(LC) for d in range(2)]

        @block.sync
        def _(sp):
            def one(dst, src):
                sp.dma_start(dst, src, allow_slow_non_contiguous=True).then_inc(s.loaded, 16)
            for k in range(4):
                one(taps[:, k, :], columns(io["conv_w_2"][0, k, 0]))
            one(conv_b[:], columns(io["conv_b_2"][0]))
            for d in range(2):
                one(lam[:, d * LC:(d + 1) * LC], columns(io["lru_lambda_2"][0, d]))
                one(biases[:, 0, d * LC:(d + 1) * LC], columns(io["lru_b_a_2"][0, d]))
                one(biases[:, 1, d * LC:(d + 1) * LC], columns(io["lru_b_x_2"][0, d]))
            sp.wait_ge(s.blocks_clear, 1)
            for g, name in enumerate(("lru_w_a_2", "lru_w_x_2")):
                for d in range(2):
                    for e in range(2):
                        sp.dma_start(blocks[e * 64:(e + 1) * 64, g, d * LC:(d + 1) * LC, e * 64:(e + 1) * 64],
                                     io[name][0, d].rearrange("(j e) c n -> e c j n", e=2)[e]) \
                            .then_inc(s.blocks_loaded, 16)

        @block.gpsimd
        def _(pool):
            pool.memset(blocks[:], 0.0).then_inc(s.blocks_clear, 1)

        @block.scalar
        def _(act):
            act.wait_ge(s.loaded, 16 * 11)
            act.activation(sig[:, 1, :], lam[:], ACT.Abs).then_inc(s.half_ready, 1)
            act.wait_ge(s.half_ready, 1)
            act.activation(sig[:, 1, :], sig[:, 1, :], ACT.Exp, scale=-1.0).then_inc(s.half_ready, 1)
            for n in range(2):
                act.mul(biases[:, n, :], biases[:, n, :], 0.5).then_inc(s.half_ready, 1)
            act.wait_ge(s.half_ready, 4)
            act.wait_ge(s.lam_ready, 1)
            for m, (j, d) in enumerate(turns):
                at = d * LC + j
                act.wait_ge(s.gates_done, m + 1)
                if m >= 2:
                    act.wait_ge(s.scans, m - 1)
                for g, t in ((0, tr), (1, ti)):
                    act.activation(t[:, d, :].rearrange("p (a n) -> p a n", n=512), gates[m % 2][:, g, :, :],
                                   ACT.Tanh, scale=0.5, bias=biases[:, g, at:at + 1]).then_inc(s.gates_read, 1)
                act.wait_ge(s.gates_read, 2 * m + 1)
                act.activation(a[:, d, :], tr[:, d, :], ACT.Exp, scale=sig[:, 0, at:at + 1],
                               bias=sig[:, 0, at:at + 1])
                act.activation(th[:, d, :], tr[:, d, :], ACT.Tanh, scale=sig[:, 0, at:at + 1],
                               bias=sig[:, 0, at:at + 1]).then_inc(s.decays, 1)
                if d:
                    for e in range(2):
                        act.wait_ge(s.squares, m + e)
                        act.activation(om[:, e, :], om[:, e, :], ACT.Sqrt, scale=-2.0).then_inc(s.roots, 1)

        @block.vector
        def _(dve):
            step = Steps(dve, s.vec)

            def do(instruction):
                step.did(instruction)
                step.wait()

            dve.wait_ge(s.half_ready, 2)
            do(dve.tensor_scalar(sig[:, 2, :], sig[:, 1, :], 2.0, None, ALU.add))
            do(dve.reciprocal(sig[:, 2, :], sig[:, 2, :]))
            do(dve.tensor_tensor(sig[:, 1, :], sig[:, 1, :], sig[:, 2, :], ALU.mult))
            do(dve.tensor_tensor(sig[:, 2, :], sig[:, 1, :], sig[:, 1, :], ALU.mult))
            do(dve.memset(sig[:, 3, :], 1.0 / 17))
            for k in range(15, 0, -2):
                do(dve.tensor_tensor(sig[:, 3, :], sig[:, 3, :], sig[:, 2, :], ALU.mult))
                do(dve.tensor_scalar(sig[:, 3, :], sig[:, 3, :], 1.0 / k, None, ALU.add))
            do(dve.tensor_tensor(sig[:, 3, :], sig[:, 3, :], sig[:, 1, :], ALU.mult))
            do(dve.tensor_scalar(sig[:, 0, :], lam[:], 0.0, None, ALU.min))
            do(dve.scalar_tensor_tensor(sig[:, 0, :], sig[:, 3, :], -2.0, sig[:, 0, :], ALU.mult, ALU.add))
            do(dve.tensor_scalar(sig[:, 0, :], sig[:, 0, :], 4.0, None, ALU.mult))
            dve.sem_inc(s.lam_ready, 1)
            dve.wait_ge(s.loaded, 16 * 11)

            def convolve(j):
                x, out = yT[:, j, :], xc[:, j % 2, :]
                do(dve.tensor_scalar(out, x, taps[:, 2, j:j + 1], conv_b[:, j:j + 1], ALU.mult, ALU.add))
                do(dve.scalar_tensor_tensor(out[:, 2:T], x[:, 0:T - 2], taps[:, 0, j:j + 1], out[:, 2:T], ALU.mult,
                                            ALU.add))
                do(dve.scalar_tensor_tensor(out[:, 1:T], x[:, 0:T - 1], taps[:, 1, j:j + 1], out[:, 1:T], ALU.mult,
                                            ALU.add))
                dve.scalar_tensor_tensor(out[:, 0:T - 1], x[:, 1:T], taps[:, 3, j:j + 1], out[:, 0:T - 1], ALU.mult,
                                         ALU.add).then_inc(s.convolved, 1)

            convolve(0)
            for j in range(LC):
                if j + 1 < LC:
                    if j:
                        dve.wait_ge(s.gates_done, 2 * j)
                    convolve(j + 1)
                dve.wait_ge(s.convolved, j + 1)
                for d in range(2):
                    dve.wait_ge(s.decays, 2 * j + d + 1)
                    do(dve.tensor_scalar(om[:, d, :], th[:, d, :], -1.0, 1.0, ALU.mult, ALU.add))
                    do(dve.reciprocal(om[:, d, :], om[:, d, :]))
                    dve.tensor_tensor(om[:, d, :], om[:, d, :], th[:, d, :], ALU.mult).then_inc(s.squares, 1)
                    step.did(dve.scalar_tensor_tensor(u[:, d, :], ti[:, d, :], 1.0, xc[:, j % 2, :], ALU.add,
                                                      ALU.mult))
                step.wait()
                for d in range(2):
                    dve.wait_ge(s.roots, 2 * j + d + 1)
                    do(dve.scalar_tensor_tensor(u[:, d, :], om[:, d, :], 0.5, u[:, d, :], ALU.mult, ALU.mult))
                    way = slice(None, None, -1) if d else slice(None)
                    dve.tensor_tensor_scan(hs[:, d, :][:, way], a[:, d, :][:, way], u[:, d, :][:, way], 0.0,
                                           ALU.mult, ALU.add).then_inc(s.scans, 1)
                dve.wait_ge(s.scans, 2 * j + 2)
                do(dve.tensor_tensor(hs[:, 0, :], hs[:, 0, :], hs[:, 1, :], ALU.add))
                do(dve.tensor_tensor(yT[:, j, :], hs[:, 0, :], zT[:, j, :], ALU.mult))

        @block.tensor
        def _(pe):
            pe.wait_ge(s.blocks_loaded, 16 * 8)
            for m, (j, d) in enumerate(turns):
                pe.wait_ge(s.convolved, j + 1)
                if m >= 2:
                    pe.wait_ge(s.gates_read, 2 * (m - 1))
                for g in range(2):
                    for n in range(2):
                        last = pe.matmul(gates[m % 2][:, g, n, :], blocks[:, g, d * LC + j, :],
                                         xc[:, j % 2, n * 512:(n + 1) * 512], start=True, stop=True)
                last.then_inc(s.gates_done, 1)


def phase_qkv(nc, io, keep):
    ks, hT, qT, kT, v = keep["consts"], keep["hT"], keep["qT"], keep["kT"], keep["v"]
    ident = ks[:, K_IDENT:K_IDENT + P]
    QW = AH * 2 * DK
    GROUPS = 2 * QW // DK
    with Phase(nc, "qkv") as ph:
        w = ph.sb("w", [P, NC, 3 * QW])
        h2 = ph.sb("h", [P, 2, NC, P])
        gains = ph.sb("gains", [P, 2])
        qk_gain = ph.sb("qk_gain", [P, 1])
        work = ph.sb("work", [P, 2, 2 * QW])
        ss = ph.sb("ss", [P, 2, 2 * GROUPS])
        out2 = [ph.ps(f"out{n}", [P, 3, 512]) for n in range(2)]
        tp = ph.ps("tp", [P, 2 * AH, P])
        s = ph.sems("gains_loaded w_loaded taken qkv_done squared summed rms normed turned q_ready k_ready v_ready "
                    "pool_steps passed vec", ns=True)
        block = ph.block()

        @block.sync
        def _(sp):
            for r in range(2):
                for n, name in enumerate(("g_q_2", "g_k_2")):
                    sp.dma_start(gains[r * DK:(r + 1) * DK, n:n + 1], io[name].rearrange("o p -> p o")) \
                        .then_inc(s.gains_loaded, 16)
            sp.dma_start(w[:], rows_by_partition(io["w_in_2"][0][:, 2 * LRU:2 * LRU + 3 * QW])).then_inc(s.w_loaded, 16)

        @block.gpsimd
        def _(pool):
            step = Steps(pool, s.pool_steps)
            with pool.Fori(0, NT // 2) as r:
                step.enter(r, 2)
                for h in range(2):
                    hold(pool, s.summed, 2 * r + h + 1, s.passed)
                    inverse_root(pool, step, ss[:, h, GROUPS:2 * GROUPS], ss[:, h, 0:GROUPS], keep["minus_half"]) \
                        .then_inc(s.rms, 1)
                step.leave(NT // 2)

        @block.scalar
        def _(act):
            with act.Fori(0, NT // 2) as r:
                for h in range(2):
                    t = 2 * r + h
                    act.wait_ge(s.qkv_done, t + 1)
                    act.activation(work[:, h, :].rearrange("p (a n) -> p a n", n=512), out2[h][:, 0:2, :],
                                   ACT.Square, scale=DK ** -0.5).then_inc(s.squared, 1)
                    act.copy(tile_of(v, t), out2[h][:, 2, :]).then_inc(s.v_ready, 1)
                for h in range(2):
                    t = 2 * r + h
                    hold(act, s.turned, t + 1, s.passed)
                    act.copy(qT[:, :, bass.ds(t * P, P)], tp[:, 0:AH, :]).then_inc(s.q_ready, 1)

        @block.vector
        def _(dve):
            step = Steps(dve, s.vec)
            dve.wait_ge(s.gains_loaded, 64)
            step.did(dve.scalar_tensor_tensor(qk_gain[:], gains[:, 0:1], DK ** -0.5, gains[:, 1:2], ALU.mult,
                                              ALU.mult))
            step.wait()
            dve.sem_inc(s.v_ready, 2)
            with dve.Fori(0, NT // 2) as r:
                for h in range(2):
                    t = 2 * r + h
                    dve.wait_ge(s.v_ready, t + 1)
                    dve.tensor_scalar(h2[:, h, :, :], hT[:, :, bass.ds(t * P, P)], 1.0, None, ALU.mult) \
                        .then_inc(s.taken, 1)
                for h in range(2):
                    t = 2 * r + h
                    dve.wait_ge(s.squared, t + 1)
                    dve.tensor_reduce(ss[:, h, 0:GROUPS], work[:, h, :].rearrange("p (g d) -> p g d", d=DK), AX,
                                      ALU.add).then_inc(s.summed, 1)
                for h in range(2):
                    t = 2 * r + h
                    dve.wait_ge(s.rms, t + 1)
                    dve.tensor_tensor(work[:, h, :].rearrange("p (g d) -> p g d", d=DK),
                                      out2[h][:, 0:2, :].rearrange("p a (g d) -> p (a g) d", d=DK),
                                      spread(ss[:, h, GROUPS:2 * GROUPS], DK), ALU.mult).then_inc(s.normed, 1)
                for h in range(2):
                    t = 2 * r + h
                    dve.wait_ge(s.turned, t + 1)
                    dve.tensor_scalar(kT[:, :, bass.ds(t * P, P)], tp[:, AH:2 * AH, :], qk_gain[:], None,
                                      ALU.mult).then_inc(s.k_ready, 1)

        @block.tensor
        def _(pe):
            pe.sem_inc(s.q_ready, 1)
            pe.sem_inc(s.k_ready, 1)
            pe.wait_ge(s.w_loaded, 16)
            with pe.Fori(0, NT // 2) as r:
                for h in range(2):
                    t = 2 * r + h
                    pe.wait_ge(s.taken, t + 1)
                    for n in range(3):
                        last = product(pe, out2[h][:, n, :], h2[:, h, :, :], w[:, :, n * 512:(n + 1) * 512])
                    last.then_inc(s.qkv_done, 1)
                for h in range(2):
                    t = 2 * r + h
                    pe.wait_ge(s.normed, t + 1)
                    pe.wait_ge(s.q_ready, t + 1)
                    pe.wait_ge(s.k_ready, t + 1)
                    for c in range(2 * AH):
                        last = pe.transpose(tp[:, c, :], work[:, h, c * P:(c + 1) * P], ident)
                    last.then_inc(s.turned, 1)


WIDE = 2 * T - P
NEAR = 3 * P


def phase_attention(nc, io, keep):
    ks, qT, kT, v, o = keep["consts"], keep["qT"], keep["kT"], keep["v"], keep["o"]
    ident = ks[:, K_IDENT:K_IDENT + P]
    UNITS = 2 * NT
    LAG = 4
    with Phase(nc, "att") as ph:
        bias = ph.sb("bias", [P, AH, WIDE])
        stage = ph.sb("stage", [P, 2, WIDE])
        pr = ph.sb("pr", [P, 4, 2, T])
        wT = ph.sb("wT", [P, 2, NT, P])
        qs = ph.sb("qs", [P, 2, T])
        kh = ph.sb("kh", [P, 2, T])
        table = ph.sb("table", [BUCKETS, AH])
        spread_table = ph.sb("spread_table", [P, BUCKETS * AH])
        line = wT[0:AH, 0, 0:4, :].rearrange("p a n -> p (a n)")
        lq = ph.sb("lq", [P, 4, DK])
        st = ph.sb("st", [P, 8])
        neg_lam = st[:, 4:5]
        sm = ph.sb("sm", [P, 4, 16])
        sc = [ph.ps(f"sc{n}", [P, 2, 512]) for n in range(2)]
        tp = ph.ps("tp", [P, NT, P])
        po = [ph.ps(f"po{n}", [P, 512]) for n in range(2)]
        s = ph.sems("table_loaded line_done line_ready line_stored near_loaded constants_ready lam_summed lam_exp "
                    "lam_ready taken staged stage_free scored scores_read0 scores_read1 tops exps weighted w_turned "
                    "wT_ready o_done o_read vec passed", ns=True)
        scores_read = [s.scores_read0, s.scores_read1]
        line_dram = keep["line"]
        block = ph.block()

        @block.sync
        def _(sp):
            sp.dma_start(table[:], io["rel_bias_2"]).then_inc(s.table_loaded, 16)
            sp.dma_start(spread_table[:], io["rel_bias_2"].rearrange("b h -> (b h)").partition_broadcast(P)) \
                .then_inc(s.table_loaded, 16)
            sp.dma_start(lq[:], io["lambda_qk_2"][0].rearrange("a d -> (a d)").partition_broadcast(P)) \
                .then_inc(s.table_loaded, 16)
            sp.wait_ge(s.line_ready, 1)
            sp.dma_start(line_dram, tiled(line, P)).then_inc(s.line_stored, 16)
            sp.wait_ge(s.line_stored, 16)
            for h in range(AH):
                sp.dma_start(bias[:, h, 768:768 + NEAR],
                             bass.AP(line_dram.tensor, h * P * 512 + P - 1, [[511, P], [1, NEAR]])) \
                    .then_inc(s.near_loaded, 16)

        @block.gpsimd
        def _(pool):
            pool.wait_ge(s.near_loaded, 16 * AH)
            pool.wait_ge(s.constants_ready, 1)
            with pool.Fori(0, AH // 2) as r:
                for b in range(2):
                    hold(pool, s.stage_free, 2 * r + b + 1, s.passed)
                    pool.tensor_copy(stage[:, b, :], bias[:, bass.ds(2 * r + b, 1), :].rearrange("p a n -> p (a n)")) \
                        .then_inc(s.staged, 1)

        @block.scalar
        def _(act):
            act.wait_ge(s.line_done, 1)
            act.copy(line, po[0][0:AH, :]).then_inc(s.line_ready, 1)
            act.wait_ge(s.lam_summed, 1)
            act.activation(st[:, 2:4], st[:, 0:2], ACT.Exp).then_inc(s.lam_exp, 1)
            act.wait_ge(s.lam_exp, 1)
            with act.Fori(0, AH // 2) as r:
                at = UNITS * r
                for h in range(2):
                    act.copy(kh[:, h, :], kT[:, bass.ds(2 * r + h, 1), :].rearrange("p a n -> p (a n)")) \
                        .then_inc(s.taken, 1)
                for n in range(UNITS + 2):
                    if n >= 2:
                        act.wait_ge(s.w_turned, at + n - 1)
                        act.copy(wT[:, n % 2, :, :], tp[:]).then_inc(s.wT_ready, 1)
                    if n < UNITS:
                        b = n % 4
                        act.wait_ge(s.tops, at + n + 1)
                        for j in range(2):
                            last = act.activation(pr[:, b, j, :], pr[:, b, j, :], ACT.Exp, bias=sm[:, b, j + 2:j + 3],
                                                  accum_out=sm[:, b, j + 4:j + 5])
                        last.then_inc(s.exps, 1)

        @block.vector
        def _(dve):
            step = Steps(dve, s.vec)
            dve.wait_ge(s.table_loaded, 48)
            for n in range(2):
                step.did(dve.tensor_tensor(lq[:, 2 * n, :], lq[:, 2 * n, :], lq[:, 2 * n + 1, :], ALU.mult))
            step.wait()
            for n in range(2):
                step.did(dve.tensor_reduce(st[:, n:n + 1], lq[:, 2 * n, :], AX, ALU.add))
            step.wait()
            dve.sem_inc(s.lam_summed, 1)
            for h in range(AH):
                for lo, hi, bucket in ((0, 768, 15), (768 + NEAR, WIDE, 31)):
                    step.did(dve.tensor_copy(bias[:, h, lo:hi],
                                             spread_table[:, bucket * AH + h:bucket * AH + h + 1]
                                             .broadcast_to([P, hi - lo])))
            step.wait()
            dve.sem_inc(s.constants_ready, 1)
            dve.wait_ge(s.lam_exp, 1)
            step.did(dve.tensor_tensor(st[:, 5:6], st[:, 3:4], st[:, 2:3], ALU.subtract))
            step.wait()
            step.did(dve.tensor_scalar(neg_lam, st[:, 5:6], -LAM_INIT, None, ALU.add))
            step.wait()
            dve.sem_inc(s.stage_free, 2)
            for j in range(2):
                dve.sem_inc(scores_read[j], 1)
            with dve.Fori(0, AH // 2) as r:
                at = UNITS * r
                step.enter(r, 2 * UNITS)
                for h in range(2):
                    dve.tensor_scalar(qs[:, h, :], qT[:, bass.ds(2 * r + h, 1), :].rearrange("p a n -> p (a n)"), 1.0,
                                      None, ALU.mult).then_inc(s.taken, 1)
                for n in range(UNITS + LAG):
                    if n < UNITS:
                        b, h, i = n % 4, n // NT, n % NT
                        if i == 0:
                            hold(dve, s.staged, 2 * r + h + 1, s.passed)
                        for j in range(2):
                            hold(dve, s.scored, 2 * at + 2 * n + j + 1, s.passed)
                            dve.tensor_tensor_reduce(pr[:, b, j, :], sc[j][:].rearrange("p a n -> p (a n)"),
                                                     stage[:, h, (NT - 1 - i) * P:(NT - 1 - i) * P + T], 1.0, -3e38,
                                                     ALU.add, ALU.max, sm[:, b, j:j + 1]) \
                                .then_inc(scores_read[j], 1)
                        dve.wait_ge(s.scores_read1, at + n + 2)
                        dve.wait_ge(s.scores_read0, at + n + 2)
                        if i == NT - 1:
                            dve.sem_inc(s.stage_free, 1)
                        dve.tensor_scalar(sm[:, b, 2:4], sm[:, b, 0:2], -1.0, None, ALU.mult).then_inc(s.tops, 1)
                    if 1 <= n <= UNITS:
                        b = (n - 1) % 4
                        dve.wait_ge(s.exps, at + n)
                        dve.wait_ge(s.o_read, at + max(n - 2, 2))
                        step.did(dve.reciprocal(sm[:, b, 6:8], sm[:, b, 4:6]))
                        step.wait()
                        step.did(dve.scalar_tensor_tensor(sm[:, b, 8:9], sm[:, b, 7:8], neg_lam, sm[:, b, 4:5], ALU.mult,
                                                          ALU.mult))
                        step.wait()
                        dve.scalar_tensor_tensor(pr[:, b, 0, :], pr[:, b, 1, :], sm[:, b, 8:9], pr[:, b, 0, :], ALU.mult,
                                                 ALU.add).then_inc(s.weighted, 1)
                    if n >= LAG:
                        m = n - LAG
                        dve.wait_ge(s.o_done, at + m + 1)
                        dve.tensor_scalar(o[:, m % NT, bass.ds((2 * r + m // NT) * DV, DV)], po[m % 2][:, 0:DV],
                                          sm[:, m % 4, 6:7], None, ALU.mult).then_inc(s.o_read, 1)
                step.leave(AH // 2)

        @block.tensor
        def _(pe):
            pe.wait_ge(s.table_loaded, 48)
            pe.matmul(po[0][0:AH, :], table[:], ks[0:BUCKETS, K_BUCKET:K_BUCKET + 512], start=True,
                      stop=True).then_inc(s.line_done, 1)
            pe.wait_ge(s.line_ready, 1)
            pe.sem_inc(s.o_read, 2)
            with pe.Fori(0, AH // 2) as r:
                at = UNITS * r
                pe.wait_ge(s.taken, 4 * r + 4)
                for n in range(UNITS + 3):
                    if n < UNITS:
                        h, i = n // NT, n % NT
                        for j in range(2):
                            pe.wait_ge(scores_read[j], at + n + 1)
                            for m in range(2):
                                last = pe.matmul(sc[j][:, m, :], qs[j * DK:(j + 1) * DK, h, i * P:(i + 1) * P],
                                                 kh[j * DK:(j + 1) * DK, h, m * 512:(m + 1) * 512],
                                                 start=True, stop=True)
                            last.then_inc(s.scored, 1)
                    if 2 <= n < UNITS + 2:
                        pe.wait_ge(s.weighted, at + n - 1)
                        if n > 2:
                            pe.wait_ge(s.wT_ready, at + n - 2)
                        for m in range(NT):
                            last = pe.transpose(tp[:, m, :], pr[:, (n - 2) % 4, 0, m * P:(m + 1) * P], ident)
                        last.then_inc(s.w_turned, 1)
                    if n >= 3:
                        c, h = (n - 3) % 2, (n - 3) // NT
                        pe.wait_ge(s.wT_ready, at + n - 2)
                        pe.wait_ge(s.o_read, at + n - 2)
                        for m in range(NT):
                            last = pe.matmul(po[c][:, 0:DV], wT[:, (n - 1) % 2, m, :],
                                             v[:, m, bass.ds((2 * r + h) * DV, DV)], start=(m == 0),
                                             stop=(m == NT - 1))
                        last.then_inc(s.o_done, 1)


def phase_second_out(nc, io, keep):
    ks, yT, o, mod, logits = keep["consts"], keep["yT"], keep["o"], keep["mod"], keep["logits2"]
    ident = ks[:, K_IDENT:K_IDENT + P]
    with Phase(nc, "out2") as ph:
        w = ph.sb("w", [P, NC, D])
        wr = ph.sb("wr", [P, NC, E2])
        o_gain = ph.sb("o_gain", [P, DV])
        xt = ph.sb("xt", [P, 2, D])
        left = ph.sb("left", [P, 2, NC, P])
        on = ph.sb("on", [P, 2, AH * DV])
        junk = ph.sb("junk", [P, 2, D])
        hn2 = ph.sb("hn", [P, 2, D])
        hT2 = ph.sb("hT", [P, 2, NC, P])
        st = ph.sb("st", [P, 2, 16])
        tp2 = [ph.ps(f"tp{n}", [P, NC, P]) for n in range(2)]
        acc2 = [ph.ps(f"acc{n}", [P, 2, 512]) for n in range(2)]
        s = ph.sems("gain_loaded w_loaded wr_loaded x_loaded0 x_loaded1 o_squared o_summed o_rms o_normed o_turned "
                    "left_ready y_taken out_done scaled x_ready x_squared x_rms rows_ready turned hT_ready logits_done "
                    "logits_ready stored pool_steps passed vec free", ns=True)
        x_loaded = [s.x_loaded0, s.x_loaded1]
        block = ph.block()

        @block.sync
        def _(sp):
            sp.dma_start(o_gain[:], io["g_attn_out_2"][0].partition_broadcast(P)).then_inc(s.gain_loaded, 16)
            sp.dma_start(w[:], io["w_out_2"][0].rearrange("(c p) n -> p c n", p=P)).then_inc(s.w_loaded, 16)
            sp.dma_start(wr[:], rows_by_partition(io["w_router_2"][0])).then_inc(s.wr_loaded, 16)
            with sp.Fori(0, NT // 2) as r:
                for h in range(2):
                    sp.wait_ge(s.stored, 64 * r + 64)
                    sp.dma_start(xt[:, h, :], keep["acc"][bass.ds(r * (2 * P) + h * P, P), :]) \
                        .then_inc(x_loaded[h], 16)
                for h in range(2):
                    sp.wait_ge(s.rows_ready, 2 * r + h + 1)
                    sp.dma_start(keep["rows"][bass.ds(r * (2 * P) + h * P, P), :], hn2[:, h, :]).then_inc(s.stored, 16)
                    sp.dma_start(io["out"][0, bass.ds(r * (2 * P) + h * P, P), :], xt[:, h, :]) \
                        .then_inc(s.stored, 16)
            sp.wait_ge(s.stored, 64 + 32 * NT)

        @block.gpsimd
        def _(pool):
            step = Steps(pool, s.pool_steps)
            pool.sem_inc(s.stored, 64)
            with pool.Fori(0, NT // 2) as r:
                step.enter(r, 4)
                for h in range(2):
                    hold(pool, s.o_summed, 2 * r + h + 1, s.passed)
                    inverse_root(pool, step, st[:, h, 4:8], st[:, h, 0:4], keep["minus_half"]).then_inc(s.o_rms, 1)
                for h in range(2):
                    hold(pool, s.x_squared, 2 * r + h + 1, s.passed)
                    inverse_root(pool, step, st[:, h, 9:10], st[:, h, 8:9], keep["minus_half"]).then_inc(s.x_rms, 1)
                step.leave(NT // 2)

        @block.scalar
        def _(act):
            with act.Fori(0, NT // 2) as r:
                for h in range(2):
                    t = 2 * r + h
                    hold(act, s.free, t + 1, s.passed)
                    act.activation(junk[:, h, 0:AH * DV], tile_of(o, t), ACT.Square, scale=DV ** -0.5) \
                        .then_inc(s.o_squared, 1)
                for h in range(2):
                    t = 2 * r + h
                    act.wait_ge(s.o_turned, t + 1)
                    act.copy(left[:, h, LC:NC, :], tp2[h][:, 0:AH, :]).then_inc(s.left_ready, 1)
                for h in range(2):
                    t = 2 * r + h
                    act.wait_ge(s.x_ready, t + 1)
                    act.activation(junk[:, h, :], xt[:, h, :], ACT.Square, scale=D ** -0.5,
                                   accum_out=st[:, h, 8:9]).then_inc(s.x_squared, 1)
                for h in range(2):
                    t = 2 * r + h
                    act.wait_ge(s.turned, t + 1)
                    act.copy(hT2[:, h, :, :], tp2[h][:]).then_inc(s.hT_ready, 1)

        @block.vector
        def _(dve):
            step = Steps(dve, s.vec)
            dve.sem_inc(s.free, 2)
            dve.wait_ge(s.gain_loaded, 16)
            step.did(dve.tensor_scalar(o_gain[:], o_gain[:], 1.0 - LAM_INIT, None, ALU.mult))
            step.wait()
            with dve.Fori(0, NT // 2) as r:
                step.enter(r, 2 * 3)
                for h in range(2):
                    t = 2 * r + h
                    dve.wait_ge(s.free, t + 1)
                    dve.tensor_scalar(left[:, h, 0:LC, :], yT[:, :, bass.ds(t * P, P)], 1.0, None, ALU.mult) \
                        .then_inc(s.y_taken, 1)
                    dve.wait_ge(s.o_squared, t + 1)
                    dve.tensor_reduce(st[:, h, 0:4], junk[:, h, 0:AH * DV].rearrange("p (g d) -> p g d", d=DV), AX,
                                      ALU.add).then_inc(s.o_summed, 1)
                for h in range(2):
                    t = 2 * r + h
                    dve.wait_ge(s.o_rms, t + 1)
                    step.did(dve.tensor_tensor(on[:, h, :].rearrange("p (g d) -> p g d", d=DV),
                                               tile_of(o, t).rearrange("p (g d) -> p g d", d=DV),
                                               spread(st[:, h, 4:8], DV), ALU.mult))
                    step.wait()
                    dve.tensor_tensor(on[:, h, :].rearrange("p (g d) -> p g d", d=DV),
                                      on[:, h, :].rearrange("p (g d) -> p g d", d=DV), tiled(o_gain[:], AH),
                                      ALU.mult).then_inc(s.o_normed, 1)
                for h in range(2):
                    t = 2 * r + h
                    dve.wait_ge(s.out_done, t + 1)
                    step.did(dve.tensor_tensor(junk[:, h, :], acc2[h][:].rearrange("p a n -> p (a n)"), mod[:, 0, :],
                                               ALU.mult))
                    step.wait()
                    dve.wait_ge(x_loaded[h], 16 * r + 16)
                    dve.tensor_tensor(xt[:, h, :], xt[:, h, :], junk[:, h, :], ALU.add).then_inc(s.x_ready, 1)
                for h in range(2):
                    t = 2 * r + h
                    dve.wait_ge(s.x_rms, t + 1)
                    step.did(dve.scalar_tensor_tensor(hn2[:, h, :], xt[:, h, :], st[:, h, 9:10], mod[:, 2, :],
                                                      ALU.mult, ALU.mult))
                    step.wait()
                    dve.tensor_tensor(hn2[:, h, :], hn2[:, h, :], mod[:, 1, :], ALU.add).then_inc(s.rows_ready, 1)
                for h in range(2):
                    t = 2 * r + h
                    dve.wait_ge(s.logits_done, t + 1)
                    dve.wait_ge(s.stored, 64 + 64 * r)
                    dve.tensor_scalar(tile_of(logits, t), acc2[h][:, 0, 0:E2], 1.0, None,
                                      ALU.mult).then_inc(s.free, 1)
                step.leave(NT // 2)

        @block.tensor
        def _(pe):
            pe.wait_ge(s.w_loaded, 16)
            pe.wait_ge(s.wr_loaded, 16)
            with pe.Fori(0, NT // 2) as r:
                for h in range(2):
                    pe.wait_ge(s.o_normed, 2 * r + h + 1)
                    for c in range(AH):
                        last = pe.transpose(tp2[h][:, c, :], on[:, h, c * DV:(c + 1) * DV], ident)
                    last.then_inc(s.o_turned, 1)
                for h in range(2):
                    pe.wait_ge(s.left_ready, 2 * r + h + 1)
                    pe.wait_ge(s.y_taken, 2 * r + h + 1)
                    for n in range(2):
                        last = product(pe, acc2[h][:, n, :], left[:, h, :, :], w[:, :, n * 512:(n + 1) * 512])
                    last.then_inc(s.out_done, 1)
                for h in range(2):
                    pe.wait_ge(s.rows_ready, 2 * r + h + 1)
                    transpose_tile(pe, tp2[h], hn2[:, h, :], ident).then_inc(s.turned, 1)
                for h in range(2):
                    pe.wait_ge(s.hT_ready, 2 * r + h + 1)
                    product(pe, acc2[h][:, 0, 0:E2], hT2[:, h, :, :], wr).then_inc(s.logits_done, 1)
                pe.wait_ge(s.free, 2 * r + 4)


class ChoiceRouting:

    def __init__(self, keep):
        self.keep = keep

    def buffers(self, ph, o):
        self.o = o
        self.aff = o.gate[:, :, 0:E2]
        self.t = {n: ph.sb(n, [P, NT]) for n in "top total".split()}
        self.w = {n: ph.sb(n, [E2, T]) for n in "affT work above tied count".split()}
        self.one = ph.sb("one_row", [E2, T])
        self.top8 = ph.sb("top8", [E2, 8])
        self.need = ph.sb("need", [E2, 1])
        self.s = ph.sems("shifted exps affinities turned taken chosen slots_turned", ns=True)

    def sync(self, sp):
        pass

    def scalar(self, act):
        act.wait_ge(self.s.shifted, 1)
        act.activation(self.keep["logits2"][:], self.keep["logits2"][:], ACT.Exp).then_inc(self.s.exps, 1)

    def tensor(self, pe):
        ident = self.keep["consts"][:, K_IDENT:K_IDENT + P]
        pe.wait_ge(self.s.affinities, 1)
        for t in range(NT):
            last = pe.transpose(self.o.pa[0:E2, t // 4, t % 4 * P:(t % 4 + 1) * P], self.o.gate[:, t, 0:E2], ident)
        last.then_inc(self.s.turned, 1)
        pe.wait_ge(self.s.chosen, 1)
        for t in range(NT):
            last = pe.transpose(self.o.pb[:, 0, t * E2:(t + 1) * E2], self.w["count"][:, t * P:(t + 1) * P],
                                ident[0:E2, 0:E2])
        last.then_inc(self.s.slots_turned, 1)

    def vector(self, dve, step):
        w, t, o, s = self.w, self.t, self.o, self.s
        logits = self.keep["logits2"][:]

        def do(instruction):
            step.did(instruction)
            step.wait()

        do(dve.memset(self.one[:], 1.0))
        do(dve.tensor_reduce(t["top"][:], logits, AX, ALU.max))
        do(dve.tensor_tensor(logits, logits, spread(t["top"][:], E2), ALU.subtract))
        dve.sem_inc(s.shifted, 1)
        dve.wait_ge(s.exps, 1)
        do(dve.tensor_reduce(t["total"][:], logits, AX, ALU.add))
        do(dve.reciprocal(t["total"][:], t["total"][:]))
        do(dve.tensor_tensor(self.aff, logits, spread(t["total"][:], E2), ALU.mult))
        dve.sem_inc(s.affinities, 1)
        dve.wait_ge(s.turned, 1)
        do(dve.tensor_copy(w["affT"][:], o.pa[0:E2, :, :].rearrange("p a n -> p (a n)")))
        do(dve.tensor_copy(w["work"][:], w["affT"][:]))
        for n in range(CAP // 8):
            do(dve.max(self.top8[:], w["work"][:]))
            if n < CAP // 8 - 1:
                do(dve.match_replace(w["work"][:], self.top8[:], w["work"][:], -1.0))
        least = self.top8[:, 7:8]
        do(dve.tensor_scalar(w["above"][:], w["affT"][:], least, None, ALU.is_gt))
        do(dve.tensor_scalar(w["tied"][:], w["affT"][:], least, None, ALU.is_equal))
        do(dve.tensor_reduce(self.need[:], w["above"][:], AX, ALU.add))
        do(dve.tensor_scalar(self.need[:], self.need[:], -1.0, float(CAP), ALU.mult, ALU.add))
        do(dve.tensor_tensor_scan(w["count"][:], self.one[:], w["tied"][:], 0.0, ALU.mult, ALU.add))
        do(dve.tensor_scalar(w["count"][:], w["count"][:], self.need[:], None, ALU.is_le))
        do(dve.tensor_tensor(w["tied"][:], w["tied"][:], w["count"][:], ALU.mult))
        do(dve.tensor_tensor(w["above"][:], w["above"][:], w["tied"][:], ALU.add))
        do(dve.tensor_tensor_scan(w["count"][:], self.one[:], w["above"][:], -1.0, ALU.mult, ALU.add))
        do(dve.tensor_scalar(w["above"][:], w["above"][:], -FAR, FAR, ALU.mult, ALU.add))
        do(dve.tensor_tensor(w["count"][:], w["count"][:], w["above"][:], ALU.add))
        dve.sem_inc(s.chosen, 1)
        dve.wait_ge(s.slots_turned, 1)
        do(dve.tensor_copy(o.slot_of[:, :, 0:E2], o.pb[:, 0, 0:NT * E2].rearrange("p (t e) -> p t e", e=E2)))


def build(nc, io):
    keep = {}
    with ExitStack() as ctx:
        sb = lambda name, shape, dt=F32: ctx.enter_context(nc.sbuf_tensor(name, shape, dt))
        keep["consts"] = sb("consts", [P, K_ALL])
        keep["minus_half"] = sb("minus_half", [P, 1])[:, :]
        keep["zero"] = sb("zero", [P, 1])[:, :]
        keep["rows"] = nc.dram_tensor("expert_rows", (T, D), F32).ap()
        keep["acc"] = nc.dram_tensor("moe_sums", (T + P, D), F32).ap()
        keep["mod_part"] = nc.dram_tensor("mod_part", (P, MOD), F32).ap()
        keep["logits"] = sb("logits", [P, NT, LOGITS])
        with ExitStack() as first:
            keep["x"] = first.enter_context(nc.sbuf_tensor("x_res", [P, NT, D], F32))
            keep["kmT"] = first.enter_context(nc.sbuf_tensor("kmT", [P, NC, MEM], F32))
            keep["vm"] = first.enter_context(nc.sbuf_tensor("vm", [P, MEM // P, D], F32))
            phase_memory(nc, io, keep)
            phase_mix(nc, io, keep)
            phase_cross(nc, io, keep)
        phase_experts(nc, io, keep, dict(name="moe1", experts=E1, width=F1, rows=keep["rows"], sums=keep["acc"],
                                         w1="w1", w3="w3", w2="w2", out_scale=None, overflow=True,
                                         pick=lambda w, e: w[bass.ds(e, 1), :, :].rearrange("a k n -> (a k) n")),
                      GroupRouting(keep))
        keep["mod"] = sb("mod", [P, 4, D])
        keep["logits2"] = sb("logits2", [P, NT, E2])
        keep["line"] = nc.dram_tensor("bias_line", (AH, P, 512), F32).ap()
        with ExitStack() as second:
            own = lambda name, shape: second.enter_context(nc.sbuf_tensor(name, shape, F32))
            keep["yT"] = own("yT", [P, LC, T])
            with ExitStack() as attended:
                keep["qT"] = attended.enter_context(nc.sbuf_tensor("qT", [P, AH, T], F32))
                keep["kT"] = attended.enter_context(nc.sbuf_tensor("kT", [P, AH, T], F32))
                keep["v"] = attended.enter_context(nc.sbuf_tensor("v", [P, NT, AH * DV], F32))
                with ExitStack() as inner:
                    keep["hT"] = inner.enter_context(nc.sbuf_tensor("hT", [P, NC, T], F32))
                    with ExitStack() as gate:
                        keep["zT"] = gate.enter_context(nc.sbuf_tensor("zT", [P, LC, T], F32))
                        phase_second_norm(nc, io, keep)
                        phase_lru(nc, io, keep)
                    phase_qkv(nc, io, keep)
                keep["o"] = attended.enter_context(nc.sbuf_tensor("o", [P, NT, AH * DV], F32))
                phase_attention(nc, io, keep)
                phase_second_out(nc, io, keep)
        phase_experts(nc, io, keep, dict(name="moe2", experts=E2, width=F2, rows=keep["rows"], sums=io["out"][0],
                                         w1="w1_2", w3="w3_2", w2="w2_2", out_scale=keep["mod"][:, 3, :],
                                         overflow=False,
                                         pick=lambda w, e: w[0][bass.ds(e, 1), :, :].rearrange("a k n -> (a k) n")),
                      ChoiceRouting(keep))


INPUTS = ["x", "mem", "norm_mix", "w_in", "q_norm", "k_norm", "attn_sinks", "sgu_norm", "sgu_w", "sgu_b",
          "out_norm_attn", "out_norm_sgu", "w_out", "norm_cross", "norm_mem", "w_cq", "w_ck", "w_cv", "cq_norm",
          "ck_norm", "w_co", "norm_ffn", "w_router_group", "w_router_expert", "w1", "w3", "w2", "c_2", "w_mod_2",
          "b_mod_2", "g_norm1_2", "w_in_2", "conv_w_2", "conv_b_2", "lru_w_a_2", "lru_b_a_2", "lru_w_x_2",
          "lru_b_x_2", "lru_lambda_2", "g_q_2", "g_k_2", "lambda_qk_2", "g_attn_out_2", "rel_bias_2", "w_out_2",
          "g_norm2_2", "w_router_2", "w1_2", "w3_2", "w2_2"]


def kernel(**inputs):
    from concourse import bacc
    from concourse.bass_utils import run_bass_kernel_spmd

    nc = bacc.Bacc("TRN2", target_bir_lowering=False, num_devices=1)
    arrays, io = {}, {}
    for name in INPUTS:
        a = np.ascontiguousarray(inputs[name])
        arrays[f"in_{name}"] = a
        io[name] = nc.dram_tensor(f"in_{name}", a.shape, mybir.dt.from_np(a.dtype), kind="ExternalInput").ap()
    arrays["in_consts"] = constants()
    io["consts"] = nc.dram_tensor("in_consts", (P, K_ALL), F32, kind="ExternalInput").ap()
    io["out"] = nc.dram_tensor("out", (1, T, D), F32, kind="ExternalOutput").ap()
    build(nc, io)
    r = run_bass_kernel_spmd(nc, [arrays], core_ids=[0])
    return r.results[0]["out"]
```
